# Optimizing a Trainium2 kernel written in Bass

```python
import jax, jax.numpy as jnp
from jax import lax
import numpy as np

D_MODEL = 1024
BATCH = 1
SEQ = 1024
DEPTH = 2

N_A_LAYERS = DEPTH // 2
N_B_LAYERS = DEPTH - N_A_LAYERS
PLE_DIM = 256
CONV_WIDTH = 31
CONV_EXPAND = 2
CONV_CH = CONV_EXPAND * D_MODEL
HEAD_DIM = 64
N_HEADS = D_MODEL // HEAD_DIM
ATTN_WIDTH = N_HEADS * HEAD_DIM
DILATION_GROUPS = ((128, 1), (512, 4), (2048, 16))
N_GROUPS = len(DILATION_GROUPS)
ROPE_THETA = 500000.0
ROPE_DIM = HEAD_DIM // 4
EPS = 1e-6
NEG_INF = -1e30

kernel_name = "yoco_conformer_dilated_hybrid"

def rmsnorm(x, g):
    xf = x.astype(jnp.float32)
    y = xf * lax.rsqrt(jnp.mean(xf * xf, axis=-1, keepdims=True) + EPS)
    return (y * g.astype(jnp.float32)).astype(x.dtype)

def layernorm(x, g, b):
    xf = x.astype(jnp.float32)
    mu = jnp.mean(xf, axis=-1, keepdims=True)
    var = jnp.mean(jnp.square(xf - mu), axis=-1, keepdims=True)
    y = (xf - mu) * lax.rsqrt(var + EPS) * g.astype(jnp.float32) + b.astype(jnp.float32)
    return y.astype(x.dtype)

def rope_partial(x, pos):
    half = ROPE_DIM // 2
    inv = ROPE_THETA ** (-jnp.arange(half, dtype=jnp.float32) * (2.0 / ROPE_DIM))
    ang = pos.astype(jnp.float32)[:, None] * inv[None, :]
    cos = jnp.cos(ang)[None, :, None, :]
    sin = jnp.sin(ang)[None, :, None, :]
    xf = x.astype(jnp.float32)
    x1 = xf[..., :half]
    x2 = xf[..., half:ROPE_DIM]
    out = jnp.concatenate([x1 * cos - x2 * sin, x1 * sin + x2 * cos, xf[..., ROPE_DIM:]], axis=-1)
    return out.astype(x.dtype)

def mixer_a(u, w_in, conv_w, conv_b, ln_g, ln_b, w_out):
    a, b, z = jnp.split(u @ w_in, 3, axis=-1)
    glu = a * jax.nn.sigmoid(b)
    y = lax.conv_general_dilated(
        glu, conv_w[:, None, :], window_strides=(1,),
        padding=[(CONV_WIDTH - 1, 0)],
        dimension_numbers=('NWC', 'WIO', 'NWC'),
        feature_group_count=CONV_CH)
    y = jax.nn.silu(layernorm(y + conv_b, ln_g, ln_b))
    return (y * jax.nn.silu(z)) @ w_out

def dilated_attention(q, k, v, span, dil):
    B, S, H, Dh = q.shape
    L = S // dil
    nb = -(-L // span)
    Lp = nb * span
    pad = Lp - L
    N = B * dil

    def to_res(t):
        return t.reshape(B, L, dil, H, Dh).transpose(0, 2, 1, 3, 4).reshape(N, L, H, Dh)

    qb = jnp.pad(to_res(q), ((0, 0), (0, pad), (0, 0), (0, 0))).reshape(N, nb, span, H, Dh)
    kp = jnp.pad(to_res(k), ((0, 0), (span, pad), (0, 0), (0, 0)))
    vp = jnp.pad(to_res(v), ((0, 0), (span, pad), (0, 0), (0, 0)))

    def band(t):
        return jnp.concatenate([t[:, :Lp].reshape(N, nb, span, H, Dh),
                                t[:, span:].reshape(N, nb, span, H, Dh)], axis=2)

    kb, vb = band(kp), band(vp)
    s = jnp.einsum('nbqhd,nbkhd->nbhqk', qb, kb).astype(jnp.float32) * (Dh ** -0.5)
    qi = jnp.arange(span)[:, None]
    kj = jnp.arange(2 * span)[None, :]
    dist = qi - kj + span
    key_idx = jnp.arange(nb)[:, None] * span + jnp.arange(2 * span)[None, :] - span
    mask = ((dist >= 0) & (dist <= span))[None] & (key_idx >= 0)[:, None, :]
    s = jnp.where(mask[None, :, None], s, NEG_INF)
    lse = jax.nn.logsumexp(s, axis=-1)
    prob = jnp.exp(s - lse[..., None])
    o = jnp.einsum('nbhqk,nbkhd->nbqhd', prob.astype(v.dtype), vb)
    o = o.reshape(B, dil, Lp, H, Dh)[:, :, :L].transpose(0, 2, 1, 3, 4).reshape(B, S, H, Dh)
    lse = lse.transpose(0, 1, 3, 2).reshape(B, dil, Lp, H)[:, :, :L]
    lse = lse.transpose(0, 2, 1, 3).reshape(B, S, H)
    return o, lse

def mixer_b(u, w_in, q_g, w_out, k_sh, v_sh, pos):
    B, S, _ = u.shape
    proj = u @ w_in
    q_all = proj[..., :N_GROUPS * ATTN_WIDTH].reshape(B, S, N_GROUPS, N_HEADS, HEAD_DIM)
    gate = proj[..., N_GROUPS * ATTN_WIDTH:]
    outs, lses = [], []
    for g, (window, dil) in enumerate(DILATION_GROUPS):
        q = rope_partial(rmsnorm(q_all[:, :, g], q_g[g]), pos)
        o, lse = dilated_attention(q, k_sh, v_sh, window // dil, dil)
        outs.append(o)
        lses.append(lse)
    wts = jax.nn.softmax(jnp.stack(lses, axis=0), axis=0)
    o = jnp.einsum('gbsh,gbshd->bshd', wts.astype(outs[0].dtype), jnp.stack(outs, axis=0))
    return (o.reshape(B, S, ATTN_WIDTH) * jax.nn.silu(gate)) @ w_out

def setup_inputs(seed: int = 0) -> dict:
    key = jax.random.key(seed)
    ks = jax.random.split(key, 20)
    f32 = jnp.float32

    def nrm(k, shape, fan_in):
        return jax.random.normal(k, shape, f32) * (fan_in ** -0.5)

    def gain(k, shape):
        return 1.0 + 0.02 * jax.random.normal(k, shape, f32)

    return {
        "x": jax.random.normal(ks[0], (BATCH, SEQ, D_MODEL), f32),
        "p": jax.random.normal(ks[1], (DEPTH, BATCH, SEQ, PLE_DIM), f32),
        "norm_g": gain(ks[2], (DEPTH, D_MODEL)),
        "w_in_a": nrm(ks[3], (N_A_LAYERS, D_MODEL, 3 * CONV_CH), D_MODEL),
        "conv_w": nrm(ks[4], (N_A_LAYERS, CONV_WIDTH, CONV_CH), CONV_WIDTH),
        "conv_b": 0.02 * jax.random.normal(ks[5], (N_A_LAYERS, CONV_CH), f32),
        "ln_g": gain(ks[6], (N_A_LAYERS, CONV_CH)),
        "ln_b": 0.02 * jax.random.normal(ks[7], (N_A_LAYERS, CONV_CH), f32),
        "w_out_a": nrm(ks[8], (N_A_LAYERS, CONV_CH, D_MODEL), CONV_CH),
        "kv_norm_g": gain(ks[9], (D_MODEL,)),
        "w_kv": nrm(ks[10], (D_MODEL, 2 * ATTN_WIDTH), D_MODEL),
        "k_norm_g": gain(ks[11], (HEAD_DIM,)),
        "w_in_b": nrm(ks[12], (N_B_LAYERS, D_MODEL, (N_GROUPS + 1) * ATTN_WIDTH), D_MODEL),
        "q_norm_g": gain(ks[13], (N_B_LAYERS, N_GROUPS, HEAD_DIM)),
        "w_out_b": nrm(ks[14], (N_B_LAYERS, ATTN_WIDTH, D_MODEL), ATTN_WIDTH),
        "ple_norm_g": gain(ks[15], (DEPTH, D_MODEL)),
        "w_ple_gate": nrm(ks[16], (DEPTH, D_MODEL, D_MODEL), D_MODEL),
        "w_ple_proj": nrm(ks[17], (DEPTH, PLE_DIM, D_MODEL), PLE_DIM),
    }

def reference(x, p, norm_g, w_in_a, conv_w, conv_b, ln_g, ln_b, w_out_a,
              kv_norm_g, w_kv, k_norm_g, w_in_b, q_norm_g, w_out_b,
              ple_norm_g, w_ple_gate, w_ple_proj):
    B, S, _ = x.shape
    pos = jnp.arange(S)
    k_sh = None
    v_sh = None
    for i in range(DEPTH):
        u = rmsnorm(x, norm_g[i])
        if i < N_A_LAYERS:
            j = i
            h = x + mixer_a(u, w_in_a[j], conv_w[j], conv_b[j], ln_g[j], ln_b[j], w_out_a[j])
        else:
            j = i - N_A_LAYERS
            h = x + mixer_b(u, w_in_b[j], q_norm_g[j], w_out_b[j], k_sh, v_sh, pos)
        ple_gate = jax.nn.sigmoid(rmsnorm(h, ple_norm_g[i]) @ w_ple_gate[i])
        h = h + ple_gate * (p[i] @ w_ple_proj[i])
        if i == N_A_LAYERS - 1:
            k_sh, v_sh = jnp.split(rmsnorm(h, kv_norm_g) @ w_kv, 2, axis=-1)
            k_sh = rope_partial(rmsnorm(k_sh.reshape(B, S, N_HEADS, HEAD_DIM), k_norm_g), pos)
            v_sh = v_sh.reshape(B, S, N_HEADS, HEAD_DIM)
        x = h
    return x


_drawn_inputs = setup_inputs


def setup_inputs(seed=0):
    import zlib

    import numpy as np

    out = dict(_drawn_inputs(seed))
    spreads = {}
    factors = {'norm_g': 6.3,
     'conv_b': 4.745,
     'ln_g': 8.0,
     'ln_b': 8.0,
     'kv_norm_g': 8.0,
     'k_norm_g': 8.0,
     'q_norm_g': 8.0,
     'ple_norm_g': 8.0}
    for name, (base, spread) in spreads.items():
        noise = np.random.default_rng([zlib.crc32(name.encode()), seed]).standard_normal(out[name].shape)
        drawn = base * np.exp(spread * noise) if base else spread * noise
        out[name] = __import__('jax').numpy.asarray(drawn.astype(out[name].dtype))
    for name, factor in factors.items():
        out[name] = (out[name] * factor).astype(out[name].dtype)
    return out
```

```python
from contextlib import ExitStack

import numpy as np

import concourse.bass as bass
from concourse import mybir

F32 = mybir.dt.float32
F32R = mybir.dt.float32r
BF16 = mybir.dt.bfloat16
ALU = mybir.AluOpType
ACT = mybir.ActivationFunctionType
AX = mybir.AxisListType

P = 128
D = 1024
S = 1024
CH = 2 * D
TAPS = 31
HEAD = 64
ROPE = HEAD // 4
PLE = 256
GROUPS = 3
EPS = 1e-6
HALF = 512
KT = D // P
CT = CH // P
PK = PLE // P
PAIRS = KT
PAD = TAPS - 1

B_ABZ = 0
B_OUTA = B_ABZ + 3 * CT
B_PROJ0 = B_OUTA + 2 * KT
B_GATE0 = B_PROJ0 + 2
B_V = B_GATE0 + KT
B_K = B_V + KT
B_QG = B_K + KT
B_OUTB = B_QG + 4 * PAIRS
B_PROJ1 = B_OUTB + KT
B_GATE1 = B_PROJ1 + 2
BLOCKS = B_GATE1 + KT

V_NORM = 0
V_PLE = V_NORM + 2 * KT
V_KV = V_PLE + 2 * KT
V_CB = V_KV + KT
V_LNG = V_CB + CT
V_LNB = V_LNG + CT
V_KG = V_LNB + CT
V_QG = V_KG + 1
V_CW = V_QG + GROUPS
VECS = V_CW + CT * TAPS

RES = 4
QB = S // HALF
SPAN = 128
STEPS = [(b, hh, r) for b in range(QB) for hh in range(2) for r in range(RES)]
NEAR = HALF + SPAN
FAR = 2 * SPAN
MASKS = RES * NEAR + 2 * FAR
C1 = NEAR
C2 = 2 * HALF


def build(nc, xT, pT, vecs_in, w_in, cs_in, ident_in, blk_in, hind_in, mask_in, out):
    z_dram = nc.dram_tensor("z_dram", (CT * P, S), F32, kind="Internal").ap()
    k_dram = nc.dram_tensor("k_dram", (KT * P, S), F32, kind="Internal").ap()
    v_dram = nc.dram_tensor("v_dram", (KT * P, S), F32, kind="Internal").ap()
    o_dram = nc.dram_tensor("o_dram", (KT * P, S), F32, kind="Internal").ap()
    h_dram = nc.dram_tensor("h_dram", (P, KT * S), F32, kind="Internal").ap()

    with ExitStack() as ctx:
        KB = 1024
        size = 207 * KB + 512
        arena = ctx.enter_context(nc.sbuf_tensor("arena", [P, size], mybir.dt.uint8))
        base = nc.lookup_mloc(arena).addr if False else ARENA_BASE(nc, size)

        def at(name, shape, dt, off):
            n = int(np.prod(shape[1:])) * (2 if dt == BF16 else 4)
            assert off % 32 == 0 and off + n <= size, name
            return nc.alloc_sbuf_tensor_at(name, shape, dt, offset=base + off)

        H_AT, U_AT, Y_AT, W_AT, T_AT = 0, 32 * KB, 96 * KB, 160 * KB, 184 * KB
        H = at("H", [P, KT, S], F32, H_AT)
        U = at("U", [P, 2 * KT, S], F32R, U_AT)
        Y = at("Y", [P, CT, S], F32, Y_AT)
        YR = at("YR", [P, CT, S], F32R, Y_AT)
        W_raw = at("W_raw", [P, 2, S], F32, W_AT)
        W_hi = at("W_hi", [P, 2, S], F32R, W_AT + 8 * KB)
        W_lo = at("W_lo", [P, 2, S], F32R, W_AT + 16 * KB)
        t = T_AT
        vecs = at("vecs", [P, VECS], F32, t); t += -(-VECS * 4 // 32) * 32
        ones_d = at("ones_d", [P, P], F32, t); t += 512
        ones_c = at("ones_c", [P, HEAD], F32, t); t += 256
        blk = at("blk", [P, P], F32, t); t += 512
        ident = at("ident", [P, P], F32, t); t += 512
        ident_b = at("ident_b", [P, P], BF16, t); t += 256
        hind = at("hind", [P, 2], F32, t); t += 32
        eps_d = at("eps_d", [P, 2], F32, t); t += 32
        stat = at("stat", [P, 96], F32, t); t += 384
        zero = at("zero", [P, 8], F32, t); t += 32
        T2 = t
        R = at("R", [P, S], F32, t); t += 4 * KB
        SIG = at("SIG", [P, S], F32, t); t += 4 * KB
        TMP = at("TMP", [P, S], F32, t); t += 4 * KB
        GLU = at("GLU", [P, S + 32], F32, t); t += 4 * KB + 128
        masks = at("masks", [P, MASKS], BF16, T2)
        sg = at("sg", [P, 2, S], F32, T2 + 6 * KB)
        otok = at("otok", [P, QB * RES, P], F32, T2 + 14 * KB)
        small = at("small", [P, 16], F32, T2 + 18 * KB)
        lsum = at("lsum", [P, 2], F32, T2 + 18 * KB + 64)
        cos = at("cos", [P, S], F32, H_AT)
        sin = at("sin", [P, S], F32, H_AT + 4 * KB)
        raw_g = at("raw_g", [P, S], F32, H_AT + 8 * KB)
        sqr = at("sqr", [P, S], F32, H_AT + 12 * KB)
        r_k = at("r_k", [P, S], F32, H_AT + 16 * KB)
        shuf = at("shuf", [P, S], F32, H_AT + 20 * KB)
        roped = at("roped", [P, S], F32, H_AT + 24 * KB)
        obuf = at("obuf", [P, S], F32, H_AT + 28 * KB)
        kpair = at("kpair", [P, 2, S], F32, U_AT)
        vpair = at("vpair", [P, 2, S], F32, U_AT + 8 * KB)
        vtok = at("vtok", [P, 2 * KT, P], F32, U_AT + 16 * KB)
        qbuf = at("qbuf", [P, 2, GROUPS, S], F32, U_AT + 24 * KB)
        prob = at("prob", [P, 2, NEAR + 2 * FAR], F32, U_AT + 48 * KB)
        probT = at("probT", [P, 2, NEAR + FAR], F32, U_AT + 57 * KB)
        assert 57 * KB + 2 * (NEAR + FAR) * 4 <= 64 * KB

        psum = ctx.enter_context(nc.psum_tensor("psum", [P, 8 * HALF], F32))
        G = [psum[:, 0:S], psum[:, S:2 * S]]
        CONV = psum[:, 2 * S:3 * S]
        STAT = psum[:, 3 * S:4 * S]
        SC = psum[:, 2 * HALF:5 * HALF]
        PT = psum[:, 5 * HALF:7 * HALF]
        MISC = psum[:, 7 * HALF:8 * HALF]

        def sem(name):
            return ctx.enter_context(nc.semaphore(name))

        w_raw_in = [sem(f"w_raw_in{s}") for s in range(2)]
        w_hi_done = sem("w_hi_done")
        w_split = sem("w_split")
        zero_set = sem("zero_set")
        gemm_done = sem("gemm_done")
        c_vecs, c_x, c_misc, c_ones = sem("c_vecs"), sem("c_x"), sem("c_misc"), sem("c_ones")
        n_sq, n_root, n_rec, n_tmp, n_hi, n_lo = (sem(s) for s in ("n_sq", "n_root", "n_rec", "n_tmp", "n_hi", "n_lo"))
        stat0 = sem("stat0")
        sig_ready, glu_ready, conv_step, y_ready = (sem(s) for s in ("sig_ready", "glu_ready", "conv_step", "y_ready"))
        z_ready, z_stored, sq_ready, stat_ready = (sem(s) for s in ("z_ready", "z_stored", "sq_ready", "stat_ready"))
        ln_step, ln_root, ln_rec = sem("ln_step"), sem("ln_root"), sem("ln_rec")
        z_back = [sem("z_back0"), sem("z_back1")]
        y_cent, y_norm, y_silu, yz_ready, yz_hi, yz_lo = (sem(s) for s in ("y_cent", "y_norm", "y_silu", "yz_ready", "yz_hi", "yz_lo"))
        h_mix, h_sq, h_stat = sem("h_mix"), sem("h_sq"), sem("h_stat")
        p_in, p_hi, p_lo, proj_done, pp_ready = (sem(s) for s in ("p_in", "p_hi", "p_lo", "proj_done", "pp_ready"))
        gate_sig, gate_mul, h_gate, g_sq, g_stat = (sem(s) for s in ("gate_sig", "gate_mul", "h_gate", "g_sq", "g_stat"))
        v_ready, h_stored, rope_in = (sem(s) for s in ("v_ready", "h_stored", "rope_in"))
        v_stored = [sem("v_stored0"), sem("v_stored1")]
        k_gain, k_sq, k_stat, k_root, k_rec, k_chain, k_ready, k_stored = (
            sem(s) for s in ("k_gain", "k_sq", "k_stat", "k_root", "k_rec", "k_chain", "k_ready", "k_stored"))
        q_gain, q_sq, q_stat, q_root, q_rec, q_chain, q_ready = (
            sem(s) for s in ("q_gain", "q_sq", "q_stat", "q_root", "q_rec", "q_chain", "q_ready"))
        gate_ready = sem("gate_ready")
        kv_in = [sem("kv_in0"), sem("kv_in1")]
        mask_in_s = sem("mask_in_s")
        v_turned, v_tok = sem("v_turned"), sem("v_tok")
        sc_ready, sc_max, m_chain, p_ready, p_sum = (sem(s) for s in ("sc_ready", "sc_max", "m_chain", "p_ready", "p_sum"))
        pt_ready, pt_copied, o_ready, l_chain, o_tok = (sem(s) for s in ("pt_ready", "pt_copied", "o_ready", "l_chain", "o_tok"))
        ot_ready, o_gated, o_stored = sem("ot_ready"), sem("o_gated"), sem("o_stored")
        o_back, h_back, o_hi, o_lo = sem("o_back"), sem("h_back"), sem("o_hi"), sem("o_lo")
        out_done = sem("out_done")

        block = ctx.enter_context(nc.Block())

        @block.sync
        def _(sp):
            def load(n, s):
                sp.dma_start(W_raw[:, s, :], w_in[bass.ds(n * P, P), :]).then_inc(w_raw_in[s], 16)

            for s in range(2):
                load(s, s)
            with sp.Fori(1, BLOCKS // 2) as j:
                for s in range(2):
                    sp.wait_ge(w_raw_in[s], j * 16)
                    sp.wait_ge(w_split, j * 2 + (s - 1))
                    load(j * 2 + s, s)

        @block.gpsimd
        def _(pool):
            def split(n, j, s, reuse):
                pool.wait_ge(w_raw_in[s], (j + 1) * 16)
                if reuse:
                    pool.wait_ge(gemm_done, n - 1)
                pool.tensor_tensor(W_hi[:, s, :], W_raw[:, s, :], zero[:, 0:1].to_broadcast([P, S]),
                                   ALU.subtract).then_inc(w_hi_done, 1)
                pool.wait_ge(w_hi_done, n + 1)
                pool.tensor_tensor(W_lo[:, s, :], W_raw[:, s, :], W_hi[:, s, :].bitcast(F32),
                                   ALU.subtract).then_inc(w_split, 1)

            pool.memset(zero[:, :], 0.0).then_inc(zero_set, 1)
            pool.wait_ge(zero_set, 1)
            for s in range(2):
                split(s, 0, s, False)
            with pool.Fori(1, BLOCKS // 2) as j:
                for s in range(2):
                    split(j * 2 + s, j, s, True)

        @block.tensor
        def _(pe):
            def block_gemm(n, slot, acc, hi, lo, tiles, start=True, stop=True, ready=None):
                pe.wait_ge(w_split, n + 1)
                last = None
                for i, (wk, xk) in enumerate(tiles):
                    if ready is not None:
                        pe.wait_ge(ready[0], ready[1] + i + 1)
                    cols = slice(wk * P, wk * P + P)
                    parts = ((W_hi, hi), (W_hi, lo), (W_lo, hi))
                    for j, (w, x) in enumerate(parts):
                        for h in range(2):
                            half = slice(h * HALF, h * HALF + HALF)
                            last = pe.matmul(acc[:, half], w[:, slot, cols], x[:, xk, half],
                                             start=start and i == 0 and j == 0,
                                             stop=stop and i == len(tiles) - 1 and j == 2)
                return last

            full = [(k, k) for k in range(KT)]
            U_hi, U_lo = U[:, 0:KT, :], U[:, KT:2 * KT, :]
            Y_hi, Y_lo = YR[:, 0:KT, :], YR[:, KT:2 * KT, :]

            def add_stat(lhsT, squares, acc, start, stop, signal):
                for h in range(2):
                    half = slice(h * HALF, h * HALF + HALF)
                    last = pe.matmul(acc[:, half], lhsT, squares[:, half], start=start, stop=stop,
                                     skip_group_check=True)
                if signal is not None:
                    last.then_inc(signal, 1)

            pe.wait_ge(c_ones, 4)
            for k in range(KT):
                pe.wait_ge(n_sq, k + 1)
                add_stat(ones_d[:, :], Y[:, k, :], STAT, k == 0, k == KT - 1, stat0)

            def add_channel_stat(c, start, stop):
                pe.wait_ge(y_ready, c + 1)
                pe.wait_ge(sq_ready, c + 1)
                y = Y[:, c, :]
                add_stat(ones_c[:, :], y, STAT[0:HEAD, :], start, stop, None)
                add_stat(ones_c[:, :], R[:, :], STAT[HEAD:P, :], start, stop, stat_ready)

            def abz(c, par, first, second):
                if not first:
                    pe.wait_ge(sig_ready, c)
                block_gemm(c * 3, par, G[par], U_hi, U_lo, full,
                           ready=(n_lo, 0) if first else None).then_inc(gemm_done, 1)
                if not first:
                    pe.wait_ge(z_ready, c)
                block_gemm(c * 3 + 1, 1 - par, G[1 - par], U_hi, U_lo, full).then_inc(gemm_done, 1)
                pe.wait_ge(glu_ready, c + 1)
                block_gemm(c * 3 + 2, par, G[par], U_hi, U_lo, full).then_inc(gemm_done, 1)
                if not first:
                    add_channel_stat(c - 1, second, False)

            abz(0, 0, True, False)
            abz(1, 1, False, True)
            with pe.Fori(1, CT // 2) as i:
                for u in range(2):
                    abz(i * 2 + u, u, False, False)
            add_channel_stat(CT - 1, False, True)

            def feature_stat(count, squares, signal, start, stop, ready):
                pe.wait_ge(ready, count)
                add_stat(ones_d[:, :], squares, STAT, start, stop, signal)

            def out_a(m, par, first):
                lead = isinstance(m, int) and m == 0
                if not first:
                    pe.wait_ge(h_mix, m - 1)
                block_gemm(m * 2 + B_OUTA, 0, G[par], U, YR, full, stop=False,
                           ready=(yz_lo, 0) if lead else None).then_inc(gemm_done, 1)
                block_gemm(m * 2 + (B_OUTA + 1), 1, G[par], U, YR, [(k, k + KT) for k in range(KT)],
                           start=False, ready=(yz_lo, KT) if lead else None).then_inc(gemm_done, 1)

            def stat_after(m, first_stat, ready, signal):
                feature_stat(m, GLU[:, 0:S], signal, first_stat, False, ready)

            pe.wait_ge(z_ready, CT)
            out_a(0, 0, True)
            out_a(1, 1, True)
            pe.wait_ge(ln_rec, 1)
            feature_stat(1, GLU[:, 0:S], h_stat, True, False, h_sq)
            with pe.Fori(1, KT // 2) as i:
                for u in range(2):
                    out_a(i * 2 + u, u, False)
                    feature_stat(i * 2 + u, GLU[:, 0:S], h_stat, False, False, h_sq)
            feature_stat(KT, GLU[:, 0:S], h_stat, False, True, h_sq)

            def ple(layer, b_proj, b_gate, with_stat):
                done, root = layer * KT, 8 * (1 if layer == 0 else 4)
                for m in range(KT):
                    if m < 2:
                        pe.wait_ge(h_mix, done + KT - 1 + m)
                    else:
                        pe.wait_ge(pp_ready, done + m - 1)
                    if m == 0:
                        pe.wait_ge(p_lo, (layer + 1) * PK)
                    last = block_gemm(b_proj + m // 4, m // 4, G[m % 2], YR[:, PK:2 * PK, :],
                                      YR[:, 2 * PK:3 * PK, :], [(m % 4 * PK + k, k) for k in range(PK)])
                    last.then_inc(proj_done, 1)
                    if m % 4 == 3:
                        pe.wait_ge(proj_done, done + m + 1)
                        pe.sem_inc(gemm_done, 1)
                def gate(m, par, lead):
                    if lead:
                        pe.wait_ge(pp_ready, done + KT - 1 + par)
                    else:
                        pe.wait_ge(gate_sig, m + (done - 1))
                    block_gemm(m + b_gate, par, G[par], U_hi, U_lo, full,
                               ready=(n_lo, root) if lead and par == 0 else None).then_inc(gemm_done, 1)

                def gate_stat(m, start, stop):
                    if with_stat:
                        feature_stat(m, GLU[:, 0:S], g_stat, start, stop, g_sq)

                gate(0, 0, True)
                gate(1, 1, True)
                gate_stat(1, True, False)
                with pe.Fori(1, KT // 2) as i:
                    for u in range(2):
                        gate(i * 2 + u, u, False)
                        gate_stat(i * 2 + u, False, False)
                gate_stat(KT, False, True)

            ple(0, B_PROJ0, B_GATE0, True)

            def value(m, par, lead):
                if lead:
                    pe.wait_ge(gate_sig, KT - 1 + par)
                else:
                    pe.wait_ge(v_ready, m - 1)
                block_gemm(m + B_V, par, G[par], U_hi, U_lo, full,
                           ready=(n_lo, 16) if lead and par == 0 else None).then_inc(gemm_done, 1)

            value(0, 0, True)
            value(1, 1, True)
            with pe.Fori(1, KT // 2) as i:
                for u in range(2):
                    value(i * 2 + u, u, False)

            def key_stat(m):
                pe.wait_ge(k_sq, m)
                add_stat(blk[:, :], sqr[:, :], STAT, True, True, k_stat)

            def key(m, par, lead):
                if lead:
                    pe.wait_ge(v_ready, KT - 1 + par)
                else:
                    pe.wait_ge(k_sq, m - 1)
                block_gemm(m + B_K, par, G[par], U_hi, U_lo, full).then_inc(gemm_done, 1)

            pe.wait_ge(c_misc, 48)
            pe.wait_ge(c_ones, 6)
            key(0, 0, True)
            key(1, 1, True)
            key_stat(1)
            with pe.Fori(1, KT // 2) as i:
                for u in range(2):
                    key(i * 2 + u, u, False)
                    pe.wait_ge(k_root, i * 2 + (u - 1))
                    key_stat(i * 2 + u)
            pe.wait_ge(k_root, KT - 1)
            key_stat(KT)

            def project(pair, g, steps):
                n = pair * 4 + (B_QG + g)
                for part in steps:
                    if part == 0:
                        pe.wait_ge(q_sq, q_evac_before(pair, g))
                        if g == 0:
                            pe.wait_ge(gate_ready, pair) if not isinstance(pair, int) or pair > 0 else None
                    tiles = [(k, k) for k in range(2 * part, 2 * part + 2)]
                    last = block_gemm(n, g % 2, G[0], Y_hi, Y_lo, tiles, start=part == 0, stop=part == 3)
                    if part == 3:
                        last.then_inc(gemm_done, 1)

            def q_evac_before(pair, g):
                return pair * GROUPS + g

            def query_stats(pair, g):
                pe.wait_ge(q_sq, pair * GROUPS + (g + 1))
                for b in range(QB):
                    for r in range(RES):
                        col = (b * RES + r) * 8 + g
                        last = pe.matmul(MISC[:, col:col + 5:4],
                                         sqr[:, b * HALF + r:b * HALF + HALF:RES], hind[:, :],
                                         start=True, stop=True, skip_group_check=True)
                last.then_inc(q_stat, 1)

            def turn_values(pair, par):
                vt = vpair[:, par, :]
                for rnd in range(4):
                    bank = PT[:, (rnd % 2) * HALF:(rnd % 2) * HALF + HALF]
                    if rnd >= 2:
                        pe.wait_ge(v_tok, pair * 4 + (rnd - 1))
                    for k in range(4):
                        if rnd < 2:
                            src = vt[:, (rnd * 4 + k) * P:(rnd * 4 + k + 1) * P]
                        else:
                            b = rnd - 2
                            src = vt[:, b * HALF + k:b * HALF + HALF:RES]
                        last = pe.transpose(bank[:, k * P:k * P + P], src, ident[:, :])
                    last.then_inc(v_turned, 1)

            def scores(pair, par, s):
                b, hh, r = STEPS[s]
                rows = slice(hh * HEAD, hh * HEAD + HEAD)
                kt = kpair[rows, par, :]
                q = [qbuf[rows, par, g, b * HALF + r:b * HALF + HALF:RES] for g in range(GROUPS)]
                near = NEAR if b else HALF
                pieces = [(0, 0, HALF)] + ([(0, HALF, NEAR)] if b else [])
                last = None
                for g, lo, hi in pieces:
                    k0 = b * HALF - (SPAN if b else 0)
                    m0 = r * NEAR + (0 if b else SPAN)
                    pe.matmul(SC[:, lo:hi], q[0], kt[:, k0 + lo:k0 + hi], start=True, stop=False,
                              skip_group_check=True)
                    pe.matmul(SC[:, lo:hi], ident_b[:, :], masks[:, m0 + lo:m0 + hi], start=False,
                              stop=True, skip_group_check=True)
                n = FAR if b else SPAN
                for g, col, m0 in ((1, C1, RES * NEAR), (2, C2, RES * NEAR + FAR)):
                    pe.matmul(SC[:, col:col + n], q[g], kt[:, r:r + RES * n - (RES - 1):RES],
                              start=True, stop=False, skip_group_check=True)
                    m1 = m0 + FAR - n
                    last = pe.matmul(SC[:, col:col + n], ident_b[:, :], masks[:, m1:m1 + n],
                                     start=False, stop=True, skip_group_check=True)
                last.then_inc(sc_ready, 1)

            def key_tiles(b):
                return (NEAR if b else HALF) // P, (2 if b else 1)

            def turn_probs(s):
                b, hh, r = STEPS[s]
                nn, nf = key_tiles(b)
                cols = [k * P for k in range(nn)] + [C1 + k * P for k in range(nf)]
                for j, col in enumerate(cols):
                    last = pe.transpose(PT[:, j * P:j * P + P], prob[:, s % 2, col:col + P], ident[:, :])
                last.then_inc(pt_ready, 1)

            def weigh_values(s):
                b, hh, r = STEPS[s]
                nn, nf = key_tiles(b)
                k0 = (3 if b else 0)
                tiles = [k0 + k for k in range(nn)] + [KT + k * RES + r for k in range(nf)]
                for j, tile in enumerate(tiles):
                    last = pe.matmul(MISC[:, 0:HEAD], probT[:, s % 2, j * P:j * P + P],
                                     vtok[:, tile, hh * HEAD:hh * HEAD + HEAD],
                                     start=j == 0, stop=j == len(tiles) - 1)
                last.then_inc(o_ready, 1)

            def turn_output(pair, b):
                pe.wait_ge(o_tok, pair * 16 + (b + 1) * 8)
                for r in range(RES):
                    last = pe.transpose(MISC[:, r:HALF:RES], otok[:, b * RES + r, :], ident[:, :])
                last.then_inc(ot_ready, 1)

            def attend(pair, par, first, project_next):
                pe.wait_ge(kv_in[par], (pair + (2 - par)) * 16)
                if not first:
                    pe.wait_ge(pt_copied, pair * 16)
                turn_values(pair, par)
                pe.wait_ge(v_tok, pair * 4 + 4)
                pe.wait_ge(q_ready, pair * GROUPS + GROUPS)
                for s in range(16):
                    b, hh, r = STEPS[s]
                    if s > 0 or not first:
                        pe.wait_ge(p_ready, pair * 16 + s)
                    scores(pair, par, s)
                    if s > 0:
                        pe.wait_ge(p_sum, pair * 16 + s)
                        if s > 1:
                            pe.wait_ge(pt_copied, pair * 16 + (s - 1))
                        turn_probs(s - 1)
                    if project_next:
                        project(pair + 1, s // 4, [s % 4])
                    if s > 0:
                        pe.wait_ge(pt_copied, pair * 16 + s)
                        misc_free(pair, s - 1, first)
                        weigh_values(s - 1)
                    if project_next and s % 4 == 0 and s > 0:
                        pe.wait_ge(o_tok, pair * 16 + s)
                        query_stats_in(pair + 1, s // 4 - 1)
                    if s == 8:
                        turn_output(pair, 0)
                pe.wait_ge(p_sum, pair * 16 + 16)
                pe.wait_ge(pt_copied, pair * 16 + 15)
                turn_probs(15)
                pe.wait_ge(pt_copied, pair * 16 + 16)
                misc_free(pair, 15, first)
                weigh_values(15)
                turn_output(pair, 1)

            def misc_free(pair, s, first):
                if s > 0:
                    pe.wait_ge(o_tok, pair * 16 + s)
                elif not first:
                    pe.wait_ge(o_gated, pair * 2)
                if s == 8:
                    pe.wait_ge(o_gated, pair * 2 + 1)

            def query_stats_in(pair, g):
                query_stats(pair, g)
                pe.wait_ge(q_root, pair * GROUPS + (g + 1))

            pe.wait_ge(k_sq, KT)
            pe.wait_ge(n_lo, 32)
            for g in range(4):
                if g:
                    pe.wait_ge(q_sq, g)
                block_gemm(B_QG + g, g % 2, G[0], Y_hi, Y_lo, full).then_inc(gemm_done, 1)
                if g < GROUPS:
                    query_stats_in(0, g)
            pe.wait_ge(mask_in_s, 16)

            attend(0, 0, True, True)
            attend(1, 1, False, True)
            with pe.Fori(1, PAIRS // 2 - 1) as i:
                for u in range(2):
                    attend(i * 2 + u, u, False, True)
            attend(PAIRS - 2, 0, False, True)
            attend(PAIRS - 1, 1, False, False)

            def out_b(m, par, lead):
                if not lead:
                    pe.wait_ge(h_mix, m + (KT - 1))
                block_gemm(m + B_OUTB, par, G[par], U_hi, U_lo, full,
                           ready=(o_lo, 0) if lead and par == 0 else None).then_inc(gemm_done, 1)

            pe.wait_ge(o_gated, 2 * PAIRS)
            out_b(0, 0, True)
            out_b(1, 1, True)
            feature_stat(KT + 1, GLU[:, 0:S], h_stat, True, False, h_sq)
            with pe.Fori(1, KT // 2) as i:
                for u in range(2):
                    out_b(i * 2 + u, u, False)
                    feature_stat(i * 2 + (KT + u), GLU[:, 0:S], h_stat, False, False, h_sq)
            feature_stat(2 * KT, GLU[:, 0:S], h_stat, False, True, h_sq)
            ple(1, B_PROJ1, B_GATE1, False)

        @block.scalar
        def _(act):
            act.dma_start(H[:, :, :], xT).then_inc(c_x, 16)
            act.dma_start(vecs[:, :], vecs_in).then_inc(c_vecs, 16)
            act.dma_start(blk[:, :], blk_in).then_inc(c_misc, 16)
            act.dma_start(hind[:, :], hind_in).then_inc(c_misc, 16)
            act.dma_start(ident[:, :], ident_in).then_inc(c_misc, 16)

            act.wait_ge(c_x, 16)
            with act.Fori(0, KT) as k:
                act.activation(Y[:, k, :], H[:, k, :], ACT.Square).then_inc(n_sq, 1)

            def root(signal, src=STAT, dst=R):
                act.activation(dst[:, :], src, ACT.Sqrt, bias=eps_d[:, 0:1]).then_inc(signal, 1)

            def norm_hi(instance, dst):
                with act.Fori(0, KT // 2) as i:
                    for u, scratch in enumerate((TMP, SIG)):
                        act.wait_ge(n_tmp, i * 2 + (8 * instance + u + 1))
                        act.activation(dst[:, i * 2 + u, :], scratch[:, :], ACT.Copy).then_inc(n_hi, 1)

            act.wait_ge(stat0, KT)
            act.wait_ge(c_ones, 5)
            root(n_root)
            norm_hi(0, U)

            def abz(c, par, first, second):
                act.wait_ge(gemm_done, c * 3 + 2)
                if not first:
                    act.wait_ge(glu_ready, c)
                act.activation(SIG[:, :], G[1 - par], ACT.Sigmoid).then_inc(sig_ready, 1)
                if not first:
                    channel_square(c - 1, second)
                act.wait_ge(gemm_done, c * 3 + 3)
                if not first:
                    act.wait_ge(z_stored, c * 16)
                act.activation(TMP[:, :], G[par], ACT.Silu).then_inc(z_ready, 1)
                act.wait_ge(z_ready, c + 1)
                act.dma_start(z_dram[bass.ds(c * P, P), :], TMP[:, :]).then_inc(z_stored, 16)

            def channel_square(c, first):
                act.wait_ge(y_ready, c + 1)
                if not first:
                    act.wait_ge(stat_ready, c)
                act.activation(R[:, :], Y[:, c, :], ACT.Square).then_inc(sq_ready, 1)

            abz(0, 0, True, False)
            abz(1, 1, False, True)
            with act.Fori(1, CT // 2) as i:
                for u in range(2):
                    abz(i * 2 + u, u, False, False)
            channel_square(CT - 1, False)

            act.wait_ge(ln_step, 6)
            act.activation(R[:, :], R[:, :], ACT.Sqrt).then_inc(ln_root, 1)

            z_buf = (TMP, GLU)

            def z_load(c, par):
                act.dma_start(z_buf[par][:, 0:S], z_dram[bass.ds(c * P, P), :]).then_inc(z_back[par], 16)

            act.wait_ge(z_stored, CT * 16)
            act.wait_ge(ln_root, 1)
            act.wait_ge(ln_rec, 1)
            z_load(0, 0)
            z_load(1, 1)

            def ln_silu(c):
                act.wait_ge(y_norm, c + 1)
                act.activation(Y[:, c, :], Y[:, c, :], ACT.Silu, scale=vecs[:, V_LNG + c:V_LNG + c + 1] if isinstance(c, int) else vecs[:, bass.ds(c + V_LNG, 1)],
                               bias=vecs[:, V_LNB + c:V_LNB + c + 1] if isinstance(c, int) else vecs[:, bass.ds(c + V_LNB, 1)]).then_inc(y_silu, 1)

            def ln_hi(c, par, more):
                act.wait_ge(yz_ready, c + 1)
                act.activation(U[:, c, :], Y[:, c, :], ACT.Copy).then_inc(yz_hi, 1)
                if more:
                    z_load(c + 2, par)

            ln_silu(0)
            with act.Fori(0, CT // 2 - 1) as i:
                for u in range(2):
                    ln_silu(i * 2 + (u + 1))
                    ln_hi(i * 2 + u, u, True)
            ln_silu(CT - 1)
            ln_hi(CT - 2, 0, False)
            ln_hi(CT - 1, 1, False)

            def stream_square(m, first, layer, made, squared, counted):
                act.wait_ge(made, m + (layer * KT + 1))
                if not first:
                    act.wait_ge(counted, m + layer * KT)
                act.activation(GLU[:, 0:S], H[:, m, :], ACT.Square).then_inc(squared, 1)

            def stream_squares(layer):
                stream_square(0, True, layer, h_mix, h_sq, h_stat)
                with act.Fori(1, KT) as m:
                    stream_square(m, False, layer, h_mix, h_sq, h_stat)

            def ple(layer, instance, with_stat):
                done = layer * KT
                act.wait_ge(gemm_done, (B_PROJ0, B_PROJ1)[layer])
                act.dma_start(Y[:, 0:PK, :], pT[:, layer, :, :]).then_inc(p_in, 16)
                act.wait_ge(p_in, (layer + 1) * 16)
                for k in range(PK):
                    act.activation(YR[:, PK + k, :], Y[:, k, :], ACT.Copy).then_inc(p_hi, 1)
                act.wait_ge(h_stat, done + KT)
                root(n_root)
                norm_hi(instance, U)
                for m in range(KT):
                    act.wait_ge(proj_done, done + m + 1)
                    act.activation(Y[:, KT + m, :], G[m % 2], ACT.Copy).then_inc(pp_ready, 1)

                def gate(m, par, first):
                    act.wait_ge(gemm_done, m + ((B_GATE0, B_GATE1)[layer] + 1))
                    if not first:
                        act.wait_ge(gate_mul, m + done)
                    act.activation(SIG[:, :], G[par], ACT.Sigmoid).then_inc(gate_sig, 1)

                def square(m, first):
                    if with_stat:
                        stream_square(m, first, layer, h_gate, g_sq, g_stat)
                    else:
                        act.wait_ge(h_gate, m + (done + 1))
                        act.dma_start(out[:, m, :] if isinstance(m, int) else out[:, bass.ds(m, 1), :],
                                      H[:, m, :] if isinstance(m, int) else H[:, bass.ds(m, 1), :]).then_inc(out_done, 16)

                gate(0, 0, True)
                gate(1, 1, False)
                square(0, True)
                with act.Fori(1, KT // 2) as i:
                    for u in range(2):
                        gate(i * 2 + u, u, False)
                        square(i * 2 + (u - 1), False)
                square(KT - 1, False)

            stream_squares(0)
            ple(0, 1, True)

            act.wait_ge(g_stat, KT)
            root(n_root)
            norm_hi(2, U)
            norm_hi(3, YR)
            act.wait_ge(n_lo, 32)
            act.dma_start(h_dram, H[:, :, :].rearrange("p k s -> p (k s)")).then_inc(h_stored, 16)

            v_buf = (TMP, SIG)

            def value(m, j, par, first):
                act.wait_ge(gemm_done, m + (B_V + 1))
                if not first:
                    act.wait_ge(v_stored[par], j * 16)
                act.activation(v_buf[par][:, :], G[par], ACT.Copy).then_inc(v_ready, 1)
                act.wait_ge(v_ready, m + 1)
                act.dma_start(v_dram[bass.ds(m * P, P), :], v_buf[par][:, :]).then_inc(v_stored[par], 16)

            value(0, 0, 0, True)
            value(1, 0, 1, True)
            with act.Fori(1, KT // 2) as i:
                for u in range(2):
                    value(i * 2 + u, i, u, False)

            act.wait_ge(h_stored, 16)
            act.dma_start(cos[:, :], cs_in[0]).then_inc(rope_in, 16)
            act.dma_start(sin[:, :], cs_in[1]).then_inc(rope_in, 16)

            def key(m, par, first):
                act.wait_ge(gemm_done, m + (B_K + 1))
                if not first:
                    act.wait_ge(k_chain, m * 4 - 3)
                act.activation(raw_g[:, :], G[par], ACT.Copy, scale=vecs[:, V_KG:V_KG + 1]).then_inc(k_gain, 1)
                if not first:
                    act.wait_ge(k_stat, m)
                act.activation(sqr[:, :], G[par], ACT.Square).then_inc(k_sq, 1)
                act.wait_ge(k_stat, m + 1)
                if not first:
                    act.wait_ge(k_chain, m * 4 - 3)
                root(k_root, STAT, r_k)

            def key_store(m):
                act.wait_ge(k_ready, m + 1)
                act.dma_start(k_dram[bass.ds(m * P, P), :], roped[:, :]).then_inc(k_stored, 16)

            key(0, 0, True)
            key(1, 1, False)
            key_store(0)
            with act.Fori(1, KT // 2) as i:
                for u in range(2):
                    key(i * 2 + u, u, False)
                    key_store(i * 2 + (u - 1))
            key_store(KT - 1)

            for u in range(2):
                act.wait_ge(v_stored[u], KT // 2 * 16)
            act.wait_ge(k_stored, KT * 16)
            act.wait_ge(gemm_done, B_QG)
            act.dma_start(masks[:, :], mask_in).then_inc(mask_in_s, 16)

            def load_pair(pair, par):
                act.dma_start(kpair[:, par, :], k_dram[bass.ds(pair * P, P), :]).then_inc(kv_in[par], 16)
                act.dma_start(vpair[:, par, :], v_dram[bass.ds(pair * P, P), :]).then_inc(kv_in[par], 16)

            load_pair(0, 0)
            load_pair(1, 1)

            def query(pair, g, first):
                act.wait_ge(gemm_done, pair * 4 + (B_QG + g + 1))
                if not first:
                    act.wait_ge(q_chain, pair * 9 + (3 * g - 1))
                    act.wait_ge(q_stat, pair * GROUPS + g)
                act.activation(raw_g[:, :], G[0], ACT.Copy, scale=vecs[:, V_QG + g:V_QG + g + 1]).then_inc(q_gain, 1)
                act.activation(sqr[:, :], G[0], ACT.Square).then_inc(q_sq, 1)

            def query_root(pair, par, g):
                act.wait_ge(q_stat, pair * GROUPS + (g + 1))
                cols = stat[:, par * 48:par * 48 + 48].rearrange("p (t h g) -> p t h g", h=2, g=GROUPS)
                src = MISC[:, 0:64].rearrange("p (t h g) -> p t h g", h=2, g=4)
                act.activation(cols[:, :, :, g], src[:, :, :, g], ACT.Sqrt,
                               bias=eps_d[:, 1:2]).then_inc(q_root, 1)

            def gate_silu(pair, par):
                act.wait_ge(gemm_done, pair * 4 + (B_QG + 4))
                act.activation(sg[:, par, :], G[0], ACT.Silu).then_inc(gate_ready, 1)

            def exps(pair, par, s):
                b, hh, r = STEPS[s]
                act.wait_ge(sc_max, pair * 16 + (s + 1))
                nn, nf = (NEAR, FAR) if b else (HALF, SPAN)
                tile = b * RES + r
                for g, col, n in ((0, 0, nn), (1, C1, nf), (2, C2, nf)):
                    at_ = par * 48 + tile * 6 + hh * 3 + g
                    dst = col if g < 2 else C1 + FAR
                    ins = act.activation(prob[:, s % 2, dst:dst + n], SC[:, col:col + n], ACT.Exp,
                                         bias=small[:, 4:5], scale=stat[:, at_:at_ + 1],
                                         accum_out=small[:, 8 + g:9 + g])
                ins.then_inc(p_ready, 1)

            def copy_turned(pair, s):
                b, hh, r = STEPS[s]
                n = (NEAR + FAR) if b else (HALF + SPAN)
                act.wait_ge(pt_ready, pair * 16 + (s + 1))
                act.activation(probT[:, s % 2, 0:n], PT[:, 0:n], ACT.Copy).then_inc(pt_copied, 1)

            for g in range(GROUPS):
                query(0, g, g == 0)
                query_root(0, 0, g)
            gate_silu(0, 0)
            act.wait_ge(mask_in_s, 16)

            def attend(pair, par, project_next, load_next):
                for s in range(16):
                    exps(pair, par, s)
                    if s > 0:
                        copy_turned(pair, s - 1)
                    if project_next:
                        if s % 4 == 3 and s < 15:
                            query(pair + 1, s // 4, False)
                        if s % 4 == 0 and s > 0:
                            query_root(pair + 1, 1 - par, s // 4 - 1)
                copy_turned(pair, 15)
                if project_next:
                    gate_silu(pair + 1, 1 - par)
                for b in range(QB):
                    act.wait_ge(o_gated, pair * 2 + (b + 1))
                act.dma_start(o_dram[bass.ds(pair * P, P), :], obuf[:, :]).then_inc(o_stored, 16)
                if load_next:
                    load_pair(pair + 2, par)

            attend(0, 0, True, True)
            attend(1, 1, True, True)
            with act.Fori(1, PAIRS // 2 - 1) as i:
                for u in range(2):
                    attend(i * 2 + u, u, True, True)
            attend(PAIRS - 2, 0, True, False)
            attend(PAIRS - 1, 1, False, False)

            act.wait_ge(o_stored, PAIRS * 16)
            act.wait_ge(gemm_done, B_OUTB)
            for k in range(KT):
                act.dma_start(Y[:, k, :], o_dram[k * P:k * P + P, :]).then_inc(o_back, 16)
            act.dma_start(H[:, :, :].rearrange("p k s -> p (k s)"), h_dram).then_inc(h_back, 16)
            act.wait_ge(o_back, KT * 16)
            with act.Fori(0, KT) as k:
                act.activation(U[:, k, :], Y[:, k, :], ACT.Copy).then_inc(o_hi, 1)
            stream_squares(1)
            ple(1, 4, False)
            act.wait_ge(out_done, KT * 16)

        @block.vector
        def _(dve):
            dve.memset(ones_d[:, :], 1.0 / D).then_inc(c_ones, 1)
            dve.memset(ones_c[:, :], 1.0 / CH).then_inc(c_ones, 1)
            dve.memset(GLU[:, 0:PAD], 0.0).then_inc(c_ones, 1)
            dve.memset(eps_d[:, 0:1], EPS).then_inc(c_ones, 1)
            dve.memset(eps_d[:, 1:2], EPS * HEAD).then_inc(c_ones, 1)
            dve.wait_ge(c_vecs, 16)
            dve.wait_ge(c_ones, 5)

            def vec(col):
                return vecs[:, col:col + 1] if isinstance(col, int) else vecs[:, bass.ds(col, 1)]

            def norm(instance, roots, gain, hi, lo, recip=True):
                if recip:
                    dve.wait_ge(n_root, roots)
                    dve.reciprocal(R[:, :], R[:, :]).then_inc(n_rec, 1)
                    dve.wait_ge(n_rec, roots)
                base_n = 8 * instance
                if instance:
                    dve.wait_ge(n_lo, base_n)

                def scaled(k, scratch):
                    dve.scalar_tensor_tensor(out=scratch[:, :], in0=H[:, k, :], scalar=vec(k + gain), in1=R[:, :],
                                             op0=ALU.mult, op1=ALU.mult).then_inc(n_tmp, 1)

                def low(k, scratch):
                    dve.wait_ge(n_hi, k + (base_n + 1))
                    dve.tensor_tensor(lo[:, k, :], scratch[:, :], hi[:, k, :].bitcast(F32),
                                      ALU.subtract).then_inc(n_lo, 1)

                scaled(0, TMP)
                scaled(1, SIG)
                with dve.Fori(0, KT // 2 - 1) as i:
                    for u, scratch in enumerate((TMP, SIG)):
                        low(i * 2 + u, scratch)
                        dve.wait_ge(n_lo, i * 2 + (u + base_n + 1))
                        scaled(i * 2 + (u + 2), scratch)
                low(KT - 2, TMP)
                low(KT - 1, SIG)

            dve.wait_ge(c_x, 16)
            norm(0, 1, V_NORM, U[:, 0:KT, :], U[:, KT:2 * KT, :])

            def convolve(c, par, first):
                if not first:
                    dve.wait_ge(y_ready, c)
                dve.wait_ge(gemm_done, c * 3 + 1)
                dve.wait_ge(sig_ready, c + 1)
                dve.tensor_tensor(GLU[:, PAD:PAD + S], G[par], SIG[:, :], ALU.mult).then_inc(glu_ready, 1)
                dve.wait_ge(glu_ready, c + 1)
                dve.tensor_scalar(CONV, GLU[:, 0:S], vec(c * TAPS + V_CW), vec(c + V_CB),
                                  ALU.mult, ALU.add).then_inc(conv_step, 1)
                for j in range(1, TAPS):
                    dve.wait_ge(conv_step, c * (TAPS - 1) + j)
                    last = j == TAPS - 1
                    dve.scalar_tensor_tensor(out=Y[:, c, :] if last else CONV, in0=GLU[:, j:j + S],
                                             scalar=vec(c * TAPS + (V_CW + j)), in1=CONV, op0=ALU.mult,
                                             op1=ALU.add).then_inc(y_ready if last else conv_step, 1)

            dve.wait_ge(stat0, KT)
            convolve(0, 0, True)
            convolve(1, 1, False)
            with dve.Fori(1, CT // 2) as i:
                for u in range(2):
                    convolve(i * 2 + u, u, False)

            dve.wait_ge(stat_ready, CT)
            dve.wait_ge(z_stored, CT * 16)
            lo_p, hi_p = slice(0, HEAD), slice(HEAD, P)
            for dst in (lo_p, hi_p):
                dve.tensor_copy(SIG[dst, :], STAT[lo_p, :]).then_inc(ln_step, 1)
                dve.tensor_copy(R[dst, :], STAT[hi_p, :]).then_inc(ln_step, 1)
            dve.wait_ge(ln_step, 4)
            dve.tensor_tensor(TMP[:, :], SIG[:, :], SIG[:, :], ALU.mult).then_inc(y_cent, 1)
            dve.wait_ge(y_cent, 1)
            dve.tensor_tensor(R[:, :], R[:, :], TMP[:, :], ALU.subtract).then_inc(ln_step, 1)
            dve.wait_ge(ln_step, 5)
            dve.tensor_scalar(R[:, :], R[:, :], 0.0, EPS, ALU.max, ALU.add).then_inc(ln_step, 1)
            dve.wait_ge(ln_root, 1)
            dve.reciprocal(R[:, :], R[:, :]).then_inc(ln_rec, 1)
            dve.wait_ge(ln_rec, 1)

            z_buf = (TMP, GLU)

            def ln_norm(c):
                dve.tensor_tensor(Y[:, c, :], Y[:, c, :], SIG[:, :], ALU.subtract).then_inc(y_cent, 1)
                dve.wait_ge(y_cent, c + 2)
                dve.tensor_tensor(Y[:, c, :], Y[:, c, :], R[:, :], ALU.mult).then_inc(y_norm, 1)

            def ln_gate(c, j, par):
                dve.wait_ge(y_silu, c + 1)
                dve.wait_ge(z_back[par], j * 16 + 16)
                dve.tensor_tensor(Y[:, c, :], Y[:, c, :], z_buf[par][:, 0:S], ALU.mult).then_inc(yz_ready, 1)

            def ln_low(c):
                dve.wait_ge(yz_hi, c + 1)
                dve.tensor_tensor(YR[:, c, :], Y[:, c, :], U[:, c, :].bitcast(F32), ALU.subtract).then_inc(yz_lo, 1)

            ln_norm(0)
            ln_norm(1)
            ln_gate(0, 0, 0)
            ln_norm(2)
            ln_gate(1, 0, 1)
            ln_low(0)
            with dve.Fori(1, CT // 2 - 1) as i:
                for u in range(2):
                    ln_norm(i * 2 + (u + 1))
                    ln_gate(i * 2 + u, i, u)
                    ln_low(i * 2 + (u - 1))
            ln_norm(CT - 1)
            ln_gate(CT - 2, CT // 2 - 1, 0)
            ln_low(CT - 3)
            ln_gate(CT - 1, CT // 2 - 1, 1)
            ln_low(CT - 2)
            ln_low(CT - 1)

            def residual(layer, n0, per):
                with dve.Fori(0, KT // 2) as i:
                    for u in range(2):
                        dve.wait_ge(gemm_done, i * (2 * per) + (n0 + (u + 1) * per))
                        dve.tensor_tensor(H[:, i * 2 + u, :], H[:, i * 2 + u, :], G[u], ALU.add).then_inc(h_mix, 1)

            def ple(layer, instance):
                done = layer * KT
                for k in range(PK):
                    dve.wait_ge(p_hi, layer * PK + k + 1)
                    dve.tensor_tensor(YR[:, 2 * PK + k, :], Y[:, k, :], YR[:, PK + k, :].bitcast(F32),
                                      ALU.subtract).then_inc(p_lo, 1)
                norm(instance, (2, 4)[layer], V_PLE + layer * KT, U[:, 0:KT, :], U[:, KT:2 * KT, :])
                def gate(m, first):
                    dve.wait_ge(gate_sig, m + (done + 1))
                    if not first:
                        dve.wait_ge(h_gate, m + done)
                    dve.tensor_tensor(TMP[:, :], SIG[:, :], Y[:, m + KT, :], ALU.mult).then_inc(gate_mul, 1)
                    dve.wait_ge(gate_mul, m + (done + 1))
                    dve.tensor_tensor(H[:, m, :], H[:, m, :], TMP[:, :], ALU.add).then_inc(h_gate, 1)

                gate(0, True)
                with dve.Fori(1, KT) as m:
                    gate(m, False)

            residual(0, B_OUTA, 2)
            ple(0, 1)
            norm(2, 3, V_KV, U[:, 0:KT, :], U[:, KT:2 * KT, :])
            norm(3, 3, V_NORM + KT, YR[:, 0:KT, :], YR[:, KT:2 * KT, :], recip=False)

            turn = list(range(ROPE // 2, ROPE)) + list(range(ROPE // 2)) + list(range(ROPE, 32))

            def key(m, first):
                dve.wait_ge(k_root, m + 1)
                dve.wait_ge(k_gain, m + 1)
                dve.reciprocal(r_k[:, :], r_k[:, :]).then_inc(k_rec, 1)
                dve.wait_ge(k_rec, m + 1)
                if not first:
                    dve.wait_ge(k_ready, m)
                dve.tensor_tensor(raw_g2[:, :], raw_g[:, :], r_k[:, :], ALU.mult).then_inc(k_chain, 1)
                if not first:
                    dve.wait_ge(k_stored, m * 16)
                dve.wait_ge(k_chain, m * 4 + 1)
                dve.tensor_tensor(roped[:, :], raw_g2[:, :], cos[:, :], ALU.mult).then_inc(k_chain, 1)
                dve.stream_shuffle(shuf[:, :], raw_g2[:, :], turn).then_inc(k_chain, 1)
                dve.wait_ge(k_chain, m * 4 + 3)
                dve.tensor_tensor(shuf[:, :], shuf[:, :], sin[:, :], ALU.mult).then_inc(k_chain, 1)
                dve.wait_ge(k_chain, m * 4 + 4)
                dve.tensor_tensor(roped[:, :], roped[:, :], shuf[:, :], ALU.add).then_inc(k_ready, 1)

            raw_g2 = obuf
            dve.wait_ge(c_misc, 48)
            dve.tensor_copy(ident_b[:, :], ident[:, :]).then_inc(c_ones, 1)
            dve.wait_ge(rope_in, 32)
            key(0, True)
            with dve.Fori(1, KT) as m:
                key(m, False)

            def query(pair, par, g, first):
                dve.wait_ge(q_gain, pair * GROUPS + (g + 1))
                q = qbuf[:, par, g, :]
                if not first:
                    dve.wait_ge(q_ready, pair * GROUPS + g)
                dve.tensor_tensor(q, raw_g[:, :], cos[:, :], ALU.mult).then_inc(q_chain, 1)
                dve.stream_shuffle(shuf[:, :], raw_g[:, :], turn).then_inc(q_chain, 1)
                dve.wait_ge(q_chain, pair * 9 + (3 * g + 2))
                dve.tensor_tensor(shuf[:, :], shuf[:, :], sin[:, :], ALU.mult).then_inc(q_chain, 1)
                dve.wait_ge(q_chain, pair * 9 + (3 * g + 3))
                dve.tensor_tensor(q, q, shuf[:, :], ALU.add).then_inc(q_ready, 1)

            def query_scale(pair, par):
                dve.wait_ge(q_root, pair * GROUPS + GROUPS)
                cols = stat[:, par * 48:par * 48 + 48]
                dve.reciprocal(cols, cols).then_inc(q_rec, 1)

            def values(pair):
                for rnd in range(4):
                    dve.wait_ge(v_turned, pair * 4 + (rnd + 1))
                    bank = PT[:, (rnd % 2) * HALF:(rnd % 2) * HALF + HALF]
                    dve.tensor_copy(vtok[:, 4 * rnd:4 * rnd + 4, :].rearrange("p t n -> p (t n)"), bank).then_inc(v_tok, 1)

            def maxima(pair, par, s, first):
                b, hh, r = STEPS[s]
                dve.wait_ge(sc_ready, pair * 16 + (s + 1))
                if s > 0 or not first:
                    dve.wait_ge(p_ready, pair * 16 + s)
                nn, nf = (NEAR, FAR) if b else (HALF, SPAN)
                dve.tensor_reduce(small[:, 0:1], SC[:, 0:nn], AX.X, ALU.max).then_inc(m_chain, 1)
                far = SC[:, C1:C1 + 2 * (C2 - C1)].rearrange("p (g n) -> p g n", g=2)[:, :, 0:nf]
                dve.tensor_reduce(small[:, 1:3], far, AX.X, ALU.max).then_inc(m_chain, 1)
                dve.wait_ge(m_chain, pair * 48 + (3 * s + 2))
                at_ = par * 48 + (b * RES + r) * 6 + hh * 3
                dve.tensor_tensor(small[:, 0:3], small[:, 0:3], stat[:, at_:at_ + 3], ALU.mult).then_inc(m_chain, 1)
                dve.wait_ge(m_chain, pair * 48 + (3 * s + 3))
                dve.tensor_reduce(small[:, 4:5], small[:, 0:3], AX.X, ALU.max, negate=True).then_inc(sc_max, 1)

            def add_far(pair, s):
                b, hh, r = STEPS[s]
                nf = FAR if b else SPAN
                dve.wait_ge(p_ready, pair * 16 + (s + 1))
                dve.tensor_reduce(lsum[:, s % 2:s % 2 + 1], small[:, 8:11], AX.X, ALU.add).then_inc(l_chain, 1)
                dve.tensor_tensor(prob[:, s % 2, C1:C1 + nf], prob[:, s % 2, C1:C1 + nf],
                                  prob[:, s % 2, C1 + FAR:C1 + FAR + nf], ALU.add).then_inc(p_sum, 1)
                dve.wait_ge(l_chain, pair * 32 + (2 * s + 1))
                dve.reciprocal(lsum[:, s % 2:s % 2 + 1], lsum[:, s % 2:s % 2 + 1]).then_inc(l_chain, 1)

            def output(pair, s):
                b, hh, r = STEPS[s]
                dve.wait_ge(o_ready, pair * 16 + (s + 1))
                dve.wait_ge(l_chain, pair * 32 + (2 * s + 2))
                dve.tensor_scalar(otok[:, b * RES + r, hh * HEAD:hh * HEAD + HEAD], MISC[:, 0:HEAD],
                                  lsum[:, s % 2:s % 2 + 1], None, ALU.mult).then_inc(o_tok, 1)

            def gated(pair, par, b, first):
                dve.wait_ge(ot_ready, pair * 2 + (b + 1))
                if b == 0 and not first:
                    dve.wait_ge(o_stored, pair * 16)
                half = slice(b * HALF, b * HALF + HALF)
                dve.tensor_tensor(obuf[:, half], MISC, sg[:, par, half], ALU.mult).then_inc(o_gated, 1)

            dve.wait_ge(k_stored, KT * 16)
            for g in range(GROUPS):
                query(0, 0, g, g == 0)
            query_scale(0, 0)
            dve.wait_ge(q_rec, 1)
            dve.wait_ge(gate_ready, 1)

            def attend(pair, par, first, project_next):
                values(pair)
                if not first:
                    dve.wait_ge(gate_ready, pair + 1)
                for s in range(16):
                    maxima(pair, par, s, first)
                    if s > 0:
                        output(pair, s - 1)
                    add_far(pair, s)
                    if s == 8:
                        gated(pair, par, 0, first)
                    if project_next and s % 4 == 0 and s > 0:
                        query(pair + 1, 1 - par, s // 4 - 1, False)
                output(pair, 15)
                gated(pair, par, 1, first)
                if project_next:
                    query_scale(pair + 1, 1 - par)
                    dve.wait_ge(q_rec, pair + 2)

            attend(0, 0, True, True)
            attend(1, 1, False, True)
            with dve.Fori(1, PAIRS // 2 - 1) as i:
                for u in range(2):
                    attend(i * 2 + u, u, False, True)
            attend(PAIRS - 2, 0, False, True)
            attend(PAIRS - 1, 1, False, False)

            with dve.Fori(0, KT) as k:
                dve.wait_ge(o_hi, k + 1)
                dve.tensor_tensor(U[:, k + KT, :], Y[:, k, :], U[:, k, :].bitcast(F32), ALU.subtract).then_inc(o_lo, 1)
            dve.wait_ge(h_back, 16)
            residual(1, B_OUTB, 1)
            ple(1, 4)


def ARENA_BASE(nc, size):
    return nc.sbuf_base - size


def kernel(x, p, norm_g, w_in_a, conv_w, conv_b, ln_g, ln_b, w_out_a, kv_norm_g, w_kv, k_norm_g,
           w_in_b, q_norm_g, w_out_b, ple_norm_g, w_ple_gate, w_ple_proj):
    import ml_dtypes
    import concourse.bacc as bacc
    from concourse.bass_utils import run_bass_kernel_spmd

    f = np.float32

    def cols(w, n0):
        return w[:, n0:n0 + P].reshape(-1, P, P).transpose(1, 0, 2).reshape(P, -1)

    def proj_blocks(w):
        return [np.concatenate([cols(w, (4 * j + m) * P) for m in range(4)], axis=1) for j in range(2)]

    x, p, norm_g, w_in_a, conv_w, conv_b, ln_g, ln_b, w_out_a, kv_norm_g, w_kv, k_norm_g, w_in_b, \
        q_norm_g, w_out_b, ple_norm_g, w_ple_gate, w_ple_proj = (
            np.asarray(a) for a in (x, p, norm_g, w_in_a, conv_w, conv_b, ln_g, ln_b, w_out_a, kv_norm_g, w_kv,
                                    k_norm_g, w_in_b, q_norm_g, w_out_b, ple_norm_g, w_ple_gate, w_ple_proj))
    wa, woa, wb, wob = w_in_a[0], w_out_a[0], w_in_b[0], w_out_b[0]
    blocks = []
    for c in range(CT):
        blocks += [cols(wa, part * CH + c * P) for part in range(3)]
    for m in range(KT):
        blocks += [cols(woa[0:D], m * P), cols(woa[D:CH], m * P)]
    blocks += proj_blocks(w_ple_proj[0])
    blocks += [cols(w_ple_gate[0], m * P) for m in range(KT)]
    blocks += [cols(w_kv, D + m * P) for m in range(KT)]
    blocks += [cols(w_kv, m * P) for m in range(KT)]
    for i in range(PAIRS):
        blocks += [cols(wb, g * D + i * P) for g in range(4)]
    blocks += [cols(wob, m * P) for m in range(KT)]
    blocks += proj_blocks(w_ple_proj[1])
    blocks += [cols(w_ple_gate[1], m * P) for m in range(KT)]
    w_all = np.concatenate(blocks, axis=0)

    def tiles(v):
        return v.reshape(-1, P).T

    vecs = np.concatenate([
        tiles(norm_g), tiles(ple_norm_g), tiles(kv_norm_g), tiles(conv_b), tiles(ln_g), tiles(ln_b),
        np.tile(k_norm_g, 2)[:, None], np.tile(q_norm_g[0], (1, 2)).T,
        conv_w[0].T.reshape(CT, P, TAPS).transpose(1, 0, 2).reshape(P, CT * TAPS)], axis=1)

    half = ROPE // 2
    inv = f(500000.0) ** (-np.arange(half, dtype=f) * f(2.0 / ROPE))
    ang = np.arange(S, dtype=f)[:, None] * inv[None, :]
    cs = np.zeros((2, P, S), f)
    cs[0] = 1.0
    for head in range(2):
        for part in range(2):
            rows = slice(head * HEAD + part * half, head * HEAD + (part + 1) * half)
            cs[0, rows] = np.cos(ang).T
            cs[1, rows] = (np.sin(ang) if part else -np.sin(ang)).T
    ident = np.eye(P, dtype=f)
    blk = np.kron(np.eye(2), np.ones((HEAD, HEAD))).astype(f) / f(HEAD)
    hind = np.kron(np.eye(2), np.ones((HEAD, 1))).astype(f)
    masks = np.full((P, MASKS), -1e30, f)
    q = np.arange(P)[:, None]
    for r in range(RES):
        dist = RES * q + r + SPAN - np.arange(NEAR)[None, :]
        masks[:, r * NEAR:(r + 1) * NEAR][(dist >= 0) & (dist <= SPAN)] = 0
    dist = q + SPAN - np.arange(FAR)[None, :]
    masks[:, RES * NEAR:RES * NEAR + FAR][(dist >= 0) & (dist <= SPAN)] = 0
    masks[:, RES * NEAR + FAR:][(dist >= 0) & (dist % 4 == 0)] = 0

    arrays = {
        "in_xT": x[0].T.reshape(KT, P, S).transpose(1, 0, 2),
        "in_pT": p[:, 0].transpose(0, 2, 1).reshape(2, PK, P, S).transpose(2, 0, 1, 3),
        "in_vecs": vecs, "in_w": w_all, "in_cs": cs, "in_ident": ident, "in_blk": blk, "in_hind": hind,
        "in_masks": masks.astype(ml_dtypes.bfloat16),
    }
    arrays = {k: np.ascontiguousarray(v) for k, v in arrays.items()}
    nc = bacc.Bacc("TRN2", target_bir_lowering=False, num_devices=1)
    args = [nc.dram_tensor(k, v.shape, mybir.dt.from_np(v.dtype), kind="ExternalInput").ap()
            for k, v in arrays.items()]
    out = nc.dram_tensor("out_hT", (P, KT, S), F32, kind="ExternalOutput").ap()
    build(nc, *args, out)
    r = run_bass_kernel_spmd(nc, [arrays], core_ids=[0])
    hT = r.results[0]["out_hT"]
    return np.ascontiguousarray(hT.transpose(2, 1, 0).reshape(1, S, D))
```

```python
from contextlib import ExitStack

import numpy as np

import concourse.bass as bass
from concourse import mybir

F32 = mybir.dt.float32
F32R = mybir.dt.float32r
BF16 = mybir.dt.bfloat16
ALU = mybir.AluOpType
ACT = mybir.ActivationFunctionType
AX = mybir.AxisListType

P = 128
D = 1024
S = 1024
CH = 2 * D
TAPS = 31
HEAD = 64
ROPE = HEAD // 4
PLE = 256
GROUPS = 3
EPS = 1e-6
HALF = 512
KT = D // P
CT = CH // P
PK = PLE // P
PAIRS = KT
PAD = TAPS - 1
SIDE = 5
MAIN = TAPS - SIDE

B_ABZ = 0
B_OUTA = B_ABZ + 3 * CT
B_PROJ0 = B_OUTA + 2 * KT
B_GATE0 = B_PROJ0 + 2
B_V = B_GATE0 + KT
B_K = B_V + KT
B_QG = B_K + KT
B_OUTB = B_QG + 4 * PAIRS
B_PROJ1 = B_OUTB + KT
B_GATE1 = B_PROJ1 + 2
BLOCKS = B_GATE1 + KT

V_NORM = 0
V_PLE = V_NORM + 2 * KT
V_KV = V_PLE + 2 * KT
V_CB = V_KV + KT
V_LNG = V_CB + CT
V_LNB = V_LNG + CT
V_KG = V_LNB + CT
V_QG = V_KG + 1
V_CW = V_QG + GROUPS
VECS = V_CW + CT * TAPS

RES = 4
QB = S // HALF
SPAN = 128
STEPS = [(b, hh, r) for b in range(QB) for hh in range(2) for r in range(RES)]
NEAR = HALF + SPAN
FAR = 2 * SPAN
MASKS = RES * NEAR + 2 * FAR
C1 = NEAR
C2 = 2 * HALF


def build(nc, xT, pT, vecs_in, w_in, cs_in, ident_in, blk_in, hind_in, mask_in, out):
    z_dram = nc.dram_tensor("z_dram", (CT * P, S), F32, kind="Internal").ap()
    k_dram = nc.dram_tensor("k_dram", (KT * P, S), F32, kind="Internal").ap()
    v_dram = nc.dram_tensor("v_dram", (KT * P, S), F32, kind="Internal").ap()
    o_dram = nc.dram_tensor("o_dram", (KT * P, S), F32, kind="Internal").ap()
    h_dram = nc.dram_tensor("h_dram", (P, KT * S), F32, kind="Internal").ap()

    with ExitStack() as ctx:
        KB = 1024
        size = 207 * KB + 512
        arena = ctx.enter_context(nc.sbuf_tensor("arena", [P, size], mybir.dt.uint8))
        base = nc.lookup_mloc(arena).addr if False else ARENA_BASE(nc, size)

        def at(name, shape, dt, off):
            n = int(np.prod(shape[1:])) * (2 if dt == BF16 else 4)
            assert off % 32 == 0 and off + n <= size, name
            return nc.alloc_sbuf_tensor_at(name, shape, dt, offset=base + off)

        H_AT, U_AT, Y_AT, W_AT, T_AT = 0, 32 * KB, 96 * KB, 160 * KB, 184 * KB
        H = at("H", [P, KT, S], F32, H_AT)
        U = at("U", [P, 2 * KT, S], F32R, U_AT)
        Y = at("Y", [P, CT, S], F32, Y_AT)
        YR = at("YR", [P, CT, S], F32R, Y_AT)
        W_raw = at("W_raw", [P, 2, S], F32, W_AT)
        W_hi = at("W_hi", [P, 2, S], F32R, W_AT + 8 * KB)
        W_lo = at("W_lo", [P, 2, S], F32R, W_AT + 16 * KB)
        t = T_AT
        vecs = at("vecs", [P, VECS], F32, t); t += -(-VECS * 4 // 32) * 32
        ones_d = at("ones_d", [P, P], F32, t); t += 512
        ones_c = at("ones_c", [P, P], F32, t); t += 512
        blk = at("blk", [P, P], F32, t); t += 512
        ident = at("ident", [P, P], F32, t); t += 512
        ident_b = at("ident_b", [P, P], BF16, t); t += 256
        hind = at("hind", [P, 2], F32, t); t += 32
        eps_d = at("eps_d", [P, 2], F32, t); t += 32
        stat = at("stat", [P, 96], F32, t); t += 384
        zero = at("zero", [P, 8], F32, t); t += 32
        T2 = t
        R = at("R", [P, S], F32, t); t += 4 * KB
        SIG = at("SIG", [P, S], F32, t); t += 4 * KB
        TMP = at("TMP", [P, S], F32, t); t += 4 * KB
        GLU = at("GLU", [P, S], F32, t); t += 4 * KB
        glu = at("glu", [P, 2, S + 32], F32, H_AT)
        prod = at("prod", [P, 2, S], F32, H_AT + 8 * KB + 256)
        part = at("part", [P, 2, S], F32, H_AT + 16 * KB + 256)
        sum_sq = at("sum_sq", [P, S], F32, H_AT + 24 * KB + 256)
        sum_y = GLU
        masks = at("masks", [P, MASKS], BF16, T2)
        sg = at("sg", [P, 2, S], F32, T2 + 6 * KB)
        otok = at("otok", [P, QB * RES, P], F32, T2 + 14 * KB)
        small = at("small", [P, 16], F32, T2 + 18 * KB)
        lsum = at("lsum", [P, 2], F32, T2 + 18 * KB + 64)
        cos = at("cos", [P, S], F32, H_AT)
        sin = at("sin", [P, S], F32, H_AT + 4 * KB)
        raw_g = at("raw_g", [P, S], F32, H_AT + 8 * KB)
        sqr = at("sqr", [P, S], F32, H_AT + 12 * KB)
        r_k = at("r_k", [P, S], F32, H_AT + 16 * KB)
        shuf = at("shuf", [P, S], F32, H_AT + 20 * KB)
        roped = at("roped", [P, S], F32, H_AT + 24 * KB)
        gbuf = at("gbuf", [P, S], F32, H_AT + 24 * KB)
        obuf = at("obuf", [P, S], F32, H_AT + 28 * KB)
        kpair = at("kpair", [P, 2, S], F32, U_AT)
        vpair = at("vpair", [P, 2, S], F32, U_AT + 8 * KB)
        vtok = at("vtok", [P, 2 * KT, P], F32, U_AT + 16 * KB)
        qbuf = at("qbuf", [P, 2, GROUPS, S], F32, U_AT + 24 * KB)
        prob = at("prob", [P, 2, NEAR + 2 * FAR], F32, U_AT + 48 * KB)
        probT = at("probT", [P, 2, NEAR + FAR], F32, U_AT + 57 * KB)
        assert 57 * KB + 2 * (NEAR + FAR) * 4 <= 64 * KB

        psum = ctx.enter_context(nc.psum_tensor("psum", [P, 8 * HALF], F32))
        G = [psum[:, 0:S], psum[:, S:2 * S]]
        CONV = [psum[:, 2 * S:3 * S], psum[:, 3 * S:4 * S]]
        E2 = psum[:, 2 * S:3 * S]
        STAT = psum[:, 3 * S:4 * S]
        SC = psum[:, 2 * HALF:5 * HALF]
        PT = psum[:, 5 * HALF:7 * HALF]
        MISC = psum[:, 7 * HALF:8 * HALF]

        def sem(name):
            return ctx.enter_context(nc.semaphore(name))

        w_raw_in = [sem(f"w_raw_in{s}") for s in range(2)]
        w_hi_done = sem("w_hi_done")
        w_split = sem("w_split")
        zero_set = sem("zero_set")
        gemm_done = sem("gemm_done")
        c_vecs, c_x, c_misc, c_ones = sem("c_vecs"), sem("c_x"), sem("c_misc"), sem("c_ones")
        n_sq, n_log, n_root, n_tmp, n_hi, n_lo = (sem(s) for s in ("n_sq", "n_log", "n_root", "n_tmp", "n_hi", "n_lo"))
        stat0 = sem("stat0")
        sig_ready, glu_ready, conv_step, y_ready = (sem(s) for s in ("sig_ready", "glu_ready", "conv_step", "y_ready"))
        z_ready, z_stored, sq_ready, stat_ready = (sem(s) for s in ("z_ready", "z_stored", "sq_ready", "stat_ready"))
        sums_zero, part_first, prod_ready, part_add, sum_add, sq_add, x_back = (
            sem(s) for s in ("sums_zero", "part_first", "prod_ready", "part_add", "sum_add", "sq_add", "x_back"))
        glu_pad, mean_copied, conv_odd = sem("glu_pad"), sem("mean_copied"), sem("conv_odd")
        ln_step, ln_log, ln_root = sem("ln_step"), sem("ln_log"), sem("ln_root")
        z_back = [sem("z_back0"), sem("z_back1")]
        y_cent, y_norm, y_silu, yz_ready, yz_hi, yz_lo = (sem(s) for s in ("y_cent", "y_norm", "y_silu", "yz_ready", "yz_hi", "yz_lo"))
        h_mix, h_sq, h_stat = sem("h_mix"), sem("h_sq"), sem("h_stat")
        p_in, p_hi, p_lo, proj_done, pp_ready = (sem(s) for s in ("p_in", "p_hi", "p_lo", "proj_done", "pp_ready"))
        gate_sig, gate_mul, h_gate, g_sq, g_stat = (sem(s) for s in ("gate_sig", "gate_mul", "h_gate", "g_sq", "g_stat"))
        v_ready, h_stored, rope_in = (sem(s) for s in ("v_ready", "h_stored", "rope_in"))
        v_stored = [sem("v_stored0"), sem("v_stored1")]
        k_gain, k_sq, k_stat, k_log, k_root, k_chain, k_ready, k_stored = (
            sem(s) for s in ("k_gain", "k_sq", "k_stat", "k_log", "k_root", "k_chain", "k_ready", "k_stored"))
        q_gain, q_sq, q_stat, q_kept, q_log, q_root, q_chain, q_ready = (
            sem(s) for s in ("q_gain", "q_sq", "q_stat", "q_kept", "q_log", "q_root", "q_chain", "q_ready"))
        gate_exp, gate_raw, gate_chain, gate_ready = (
            sem(s) for s in ("gate_exp", "gate_raw", "gate_chain", "gate_ready"))
        kv_in = [sem("kv_in0"), sem("kv_in1")]
        mask_in_s = sem("mask_in_s")
        v_turned, v_tok = sem("v_turned"), sem("v_tok")
        sc_near, sc_ready, sc_max, m_chain, p_part, p_sum = (
            sem(s) for s in ("sc_near", "sc_ready", "sc_max", "m_chain", "p_part", "p_sum"))
        pt_ready, pt_copied, o_ready, l_chain, o_tok = (sem(s) for s in ("pt_ready", "pt_copied", "o_ready", "l_chain", "o_tok"))
        ot_ready, o_gated, o_stored = sem("ot_ready"), sem("o_gated"), sem("o_stored")
        o_back, h_back, o_hi, o_lo = sem("o_back"), sem("h_back"), sem("o_hi"), sem("o_lo")
        out_done = sem("out_done")

        block = ctx.enter_context(nc.Block())

        @block.sync
        def _(sp):
            def load(n, s):
                sp.dma_start(W_raw[:, s, :], w_in[bass.ds(n * P, P), :]).then_inc(w_raw_in[s], 16)

            for s in range(2):
                load(s, s)
            with sp.Fori(1, BLOCKS // 2) as j:
                for s in range(2):
                    sp.wait_ge(w_raw_in[s], j * 16)
                    sp.wait_ge(w_split, j * 2 + (s - 1))
                    load(j * 2 + s, s)

        @block.gpsimd
        def _(pool):
            def split(n, j, s, reuse):
                pool.wait_ge(w_raw_in[s], (j + 1) * 16)
                if reuse:
                    pool.wait_ge(gemm_done, n - 1)
                pool.tensor_tensor(zero[:, 1:2], zero[:, 0:1], zero[:, 0:1], ALU.add)
                pool.tensor_copy(W_hi[:, s, :], W_raw[:, s, :]).then_inc(w_hi_done, 1)
                pool.wait_ge(w_hi_done, n + 1)
                pool.tensor_tensor(W_lo[:, s, :], W_raw[:, s, :], W_hi[:, s, :].bitcast(F32),
                                   ALU.subtract).then_inc(w_split, 1)

            pool.memset(zero[:, :], 0.0).then_inc(zero_set, 1)
            pool.wait_ge(zero_set, 1)
            for s in range(2):
                split(s, 0, s, False)
            pool.memset(sum_y[:, :], 0.0).then_inc(sums_zero, 1)
            pool.wait_ge(n_lo, KT)
            pool.memset(sum_sq[:, :], 0.0).then_inc(sums_zero, 1)
            pool.wait_ge(sums_zero, 2)

            def add_products(c, par, lo, hi):
                for k in range(lo, hi):
                    pool.wait_ge(prod_ready, c * (SIDE - 1) + k)
                    if k == 1:
                        pool.wait_ge(part_first, c + 1)
                    else:
                        pool.wait_ge(part_add, c * (SIDE - 1) + (k - 1))
                    pool.tensor_tensor(part[:, par, :], part[:, par, :], prod[:, k % 2, :],
                                       ALU.add).then_inc(part_add, 1)

            def add_channel(c, first):
                pool.wait_ge(y_ready, c + 1)
                if not first:
                    pool.wait_ge(sum_add, c)
                pool.tensor_tensor(sum_y[:, :], sum_y[:, :], Y[:, c, :], ALU.add).then_inc(sum_add, 1)
                pool.wait_ge(sq_ready, c + 1)
                if not first:
                    pool.wait_ge(sq_add, c)
                pool.tensor_tensor(sum_sq[:, :], sum_sq[:, :], R[:, :], ALU.add).then_inc(sq_add, 1)

            def channel(c, i, u, stats, first_stat):
                n = c * 3 + 2
                s = u
                split(n, i * 3 + (1 + u), s, True)
                if stats:
                    add_channel(c - 2, first_stat)
                add_products(c, u, 1, 3)
                split(n + 1, i * 3 + (1 + u) + (1 if s else 0), 1 - s, True)
                add_products(c, u, 3, 5)
                split(n + 2, i * 3 + (2 + u), s, True)
                add_products(c, u, 5, SIDE)

            channel(0, 0, 0, False, False)
            channel(1, 0, 1, False, False)
            channel(2, 1, 0, True, True)
            channel(3, 1, 1, True, False)
            with pool.Fori(2, CT // 2) as i:
                for u in range(2):
                    channel(i * 2 + u, i, u, True, False)
            add_channel(CT - 2, False)
            add_channel(CT - 1, False)

            def center(c):
                pool.tensor_tensor(Y[:, c, :], Y[:, c, :], SIG[:, :], ALU.subtract).then_inc(y_cent, 1)

            pool.wait_ge(mean_copied, 1)
            with pool.Fori(0, CT) as c:
                center(c)

            with pool.Fori((3 * CT + 2) // 2, BLOCKS // 2) as j:
                for s in range(2):
                    split(j * 2 + s, j, s, True)

        @block.tensor
        def _(pe):
            def block_gemm(n, slot, acc, hi, lo, tiles, start=True, stop=True, ready=None):
                pe.wait_ge(w_split, n + 1)
                last = None
                for i, (wk, xk) in enumerate(tiles):
                    if ready is not None:
                        pe.wait_ge(ready[0], ready[1] + i + 1)
                    cols = slice(wk * P, wk * P + P)
                    parts = ((W_hi, hi), (W_hi, lo), (W_lo, hi))
                    for j, (w, x) in enumerate(parts):
                        for h in range(2):
                            half = slice(h * HALF, h * HALF + HALF)
                            last = pe.matmul(acc[:, half], w[:, slot, cols], x[:, xk, half],
                                             start=start and i == 0 and j == 0,
                                             stop=stop and i == len(tiles) - 1 and j == 2)
                return last

            full = [(k, k) for k in range(KT)]
            U_hi, U_lo = U[:, 0:KT, :], U[:, KT:2 * KT, :]
            Y_hi, Y_lo = YR[:, 0:KT, :], YR[:, KT:2 * KT, :]

            def add_stat(lhsT, squares, acc, start, stop, signal):
                for h in range(2):
                    half = slice(h * HALF, h * HALF + HALF)
                    last = pe.matmul(acc[:, half], lhsT, squares[:, half], start=start, stop=stop,
                                     skip_group_check=True)
                if signal is not None:
                    last.then_inc(signal, 1)

            pe.wait_ge(c_ones, 3)
            for k in range(KT):
                pe.wait_ge(n_sq, k + 1)
                add_stat(ones_d[:, :], Y[:, k, :], STAT, k == 0, k == KT - 1, stat0)

            def abz(c, par, first):
                if not first:
                    pe.wait_ge(sig_ready, c)
                block_gemm(c * 3, par, G[par], U_hi, U_lo, full,
                           ready=(n_lo, 0) if first else None).then_inc(gemm_done, 1)
                if not first:
                    pe.wait_ge(z_ready, c)
                block_gemm(c * 3 + 1, 1 - par, G[1 - par], U_hi, U_lo, full).then_inc(gemm_done, 1)
                pe.wait_ge(glu_ready, c + 1)
                block_gemm(c * 3 + 2, par, G[par], U_hi, U_lo, full).then_inc(gemm_done, 1)

            abz(0, 0, True)
            abz(1, 1, False)
            with pe.Fori(1, CT // 2) as i:
                for u in range(2):
                    abz(i * 2 + u, u, False)
            pe.wait_ge(y_ready, CT)
            pe.wait_ge(sum_add, CT)
            add_stat(ones_c[:, :], sum_y, STAT, True, True, stat_ready)
            pe.wait_ge(sq_add, CT)
            add_stat(ones_c[:, :], sum_sq, E2, True, True, stat_ready)

            def feature_stat(count, squares, signal, start, stop, ready):
                pe.wait_ge(ready, count)
                add_stat(ones_d[:, :], squares, STAT, start, stop, signal)

            def out_a(m, par, first):
                lead = isinstance(m, int) and m == 0
                if not first:
                    pe.wait_ge(h_mix, m - 1)
                block_gemm(m * 2 + B_OUTA, 0, G[par], U, YR, full, stop=False,
                           ready=(yz_lo, 0) if lead else None).then_inc(gemm_done, 1)
                block_gemm(m * 2 + (B_OUTA + 1), 1, G[par], U, YR, [(k, k + KT) for k in range(KT)],
                           start=False, ready=(yz_lo, KT) if lead else None).then_inc(gemm_done, 1)

            def stat_after(m, first_stat, ready, signal):
                feature_stat(m, GLU[:, :], signal, first_stat, False, ready)

            pe.wait_ge(z_ready, CT)
            out_a(0, 0, True)
            out_a(1, 1, True)
            pe.wait_ge(y_norm, CT)
            feature_stat(1, GLU[:, :], h_stat, True, False, h_sq)
            with pe.Fori(1, KT // 2) as i:
                for u in range(2):
                    out_a(i * 2 + u, u, False)
                    feature_stat(i * 2 + u, GLU[:, :], h_stat, False, False, h_sq)
            feature_stat(KT, GLU[:, :], h_stat, False, True, h_sq)

            def ple(layer, b_proj, b_gate, with_stat):
                done, root = layer * KT, 8 * (1 if layer == 0 else 4)
                for m in range(KT):
                    if m < 2:
                        pe.wait_ge(h_mix, done + KT - 1 + m)
                    else:
                        pe.wait_ge(pp_ready, done + m - 1)
                    if m == 0:
                        pe.wait_ge(p_lo, (layer + 1) * PK)
                    last = block_gemm(b_proj + m // 4, m // 4, G[m % 2], YR[:, PK:2 * PK, :],
                                      YR[:, 2 * PK:3 * PK, :], [(m % 4 * PK + k, k) for k in range(PK)])
                    last.then_inc(proj_done, 1)
                    if m % 4 == 3:
                        pe.wait_ge(proj_done, done + m + 1)
                        pe.sem_inc(gemm_done, 1)
                def gate(m, par, lead):
                    if lead:
                        pe.wait_ge(pp_ready, done + KT - 1 + par)
                    else:
                        pe.wait_ge(gate_sig, m + (done - 1))
                    block_gemm(m + b_gate, par, G[par], U_hi, U_lo, full,
                               ready=(n_lo, root) if lead and par == 0 else None).then_inc(gemm_done, 1)

                def gate_stat(m, start, stop):
                    if with_stat:
                        feature_stat(m, GLU[:, :], g_stat, start, stop, g_sq)

                gate(0, 0, True)
                gate(1, 1, True)
                gate_stat(1, True, False)
                with pe.Fori(1, KT // 2) as i:
                    for u in range(2):
                        gate(i * 2 + u, u, False)
                        gate_stat(i * 2 + u, False, False)
                gate_stat(KT, False, True)

            ple(0, B_PROJ0, B_GATE0, True)

            def value(m, par, lead):
                if lead:
                    pe.wait_ge(gate_sig, KT - 1 + par)
                else:
                    pe.wait_ge(v_ready, m - 1)
                block_gemm(m + B_V, par, G[par], U_hi, U_lo, full,
                           ready=(n_lo, 16) if lead and par == 0 else None).then_inc(gemm_done, 1)

            value(0, 0, True)
            value(1, 1, True)
            with pe.Fori(1, KT // 2) as i:
                for u in range(2):
                    value(i * 2 + u, u, False)

            def key_stat(m):
                pe.wait_ge(k_sq, m)
                add_stat(blk[:, :], sqr[:, :], STAT, True, True, k_stat)

            def key(m, par, lead):
                if lead:
                    pe.wait_ge(v_ready, KT - 1 + par)
                else:
                    pe.wait_ge(k_sq, m - 1)
                block_gemm(m + B_K, par, G[par], U_hi, U_lo, full).then_inc(gemm_done, 1)

            pe.wait_ge(c_misc, 48)
            pe.wait_ge(c_ones, 5)
            key(0, 0, True)
            key(1, 1, True)
            key_stat(1)
            with pe.Fori(1, KT // 2) as i:
                for u in range(2):
                    key(i * 2 + u, u, False)
                    pe.wait_ge(k_root, i * 2 + (u - 1))
                    key_stat(i * 2 + u)
            pe.wait_ge(k_root, KT - 1)
            key_stat(KT)

            def project(pair, g, part):
                if part == 0:
                    if g:
                        pe.wait_ge(q_sq, pair * GROUPS + g)
                    elif not (isinstance(pair, int) and pair == 0):
                        pe.wait_ge(gate_raw, pair)
                tiles = [(k, k) for k in range(3 * part, min(3 * part + 3, KT))]
                last = block_gemm(pair * 4 + (B_QG + g), g % 2, G[0], Y_hi, Y_lo, tiles,
                                  start=part == 0, stop=part == 2)
                if part == 2:
                    last.then_inc(gemm_done, 1)

            def query_stats(pair, g):
                pe.wait_ge(q_sq, pair * GROUPS + (g + 1))
                for b in range(QB):
                    for r in range(RES):
                        col = (b * RES + r) * 8 + g
                        last = pe.matmul(MISC[:, col:col + 5:4],
                                         sqr[:, b * HALF + r:b * HALF + HALF:RES], hind[:, :],
                                         start=True, stop=True, skip_group_check=True)
                last.then_inc(q_stat, 1)

            def turn_values(pair, par, rnd):
                vt = vpair[:, par, :]
                bank = (PT[:, 0:HALF], PT[:, HALF:2 * HALF], MISC, PT[:, 0:HALF])[rnd]
                for k in range(4):
                    if rnd < 2:
                        src = vt[:, (rnd * 4 + k) * P:(rnd * 4 + k + 1) * P]
                    else:
                        src = vt[:, (rnd - 2) * HALF + k:(rnd - 2) * HALF + HALF:RES]
                    last = pe.transpose(bank[:, k * P:k * P + P], src, ident[:, :])
                last.then_inc(v_turned, 1)

            def scores(pair, par, s, seen):
                b, hh, r = STEPS[s]
                rows = slice(hh * HEAD, hh * HEAD + HEAD)
                kt = kpair[rows, par, :]
                q = [qbuf[rows, par, g, b * HALF + r:b * HALF + HALF:RES] for g in range(GROUPS)]
                n = FAR if b else SPAN
                k0 = b * HALF - (SPAN if b else 0)
                m0 = r * NEAR + (0 if b else SPAN)

                def piece(g, keys, col, mask, n):
                    pe.matmul(SC[:, col:col + n], q[g], keys, start=True, stop=False, skip_group_check=True)
                    return pe.matmul(SC[:, col:col + n], ident_b[:, :], masks[:, mask:mask + n],
                                     start=False, stop=True, skip_group_check=True)

                far_keys = kt[:, r:r + RES * n - (RES - 1):RES]
                if seen is not None:
                    pe.wait_ge(p_part, seen + 1)
                piece(0, kt[:, k0:k0 + HALF], 0, m0, HALF)
                if seen is not None:
                    pe.wait_ge(p_part, seen + 2)
                if b:
                    piece(0, kt[:, k0 + HALF:k0 + NEAR], HALF, m0 + HALF, SPAN)
                piece(1, far_keys, C1, RES * NEAR + FAR - n, n).then_inc(sc_near, 1)
                if seen is not None:
                    pe.wait_ge(p_part, seen + 3)
                last = piece(2, far_keys, C2, RES * NEAR + 2 * FAR - n, n)
                last.then_inc(sc_ready, 1)

            def key_tiles(b):
                return (NEAR if b else HALF) // P, (2 if b else 1)

            def turn_probs(s):
                b, hh, r = STEPS[s]
                nn, nf = key_tiles(b)
                cols = [k * P for k in range(nn)] + [C1 + k * P for k in range(nf)]
                for j, col in enumerate(cols):
                    last = pe.transpose(PT[:, j * P:j * P + P], prob[:, s % 2, col:col + P], ident[:, :])
                last.then_inc(pt_ready, 1)

            def weigh_values(s):
                b, hh, r = STEPS[s]
                nn, nf = key_tiles(b)
                k0 = (3 if b else 0)
                tiles = [k0 + k for k in range(nn)] + [KT + k * RES + r for k in range(nf)]
                for j, tile in enumerate(tiles):
                    last = pe.matmul(MISC[:, 0:HEAD], probT[:, s % 2, j * P:j * P + P],
                                     vtok[:, tile, hh * HEAD:hh * HEAD + HEAD],
                                     start=j == 0, stop=j == len(tiles) - 1)
                last.then_inc(o_ready, 1)

            def turn_output(pair, b):
                for r in range(RES):
                    last = pe.transpose(MISC[:, r:HALF:RES], otok[:, b * RES + r, :], ident[:, :])
                last.then_inc(ot_ready, 1)

            def attend(pair, par, first, project_next):
                done = pair * 16
                for s in range(16):
                    if s == 0:
                        pe.wait_ge(kv_in[par], (pair + (2 - par)) * 16)
                        pe.wait_ge(q_ready, pair * GROUPS + GROUPS)
                    scores(pair, par, s, None if first and s == 0 else 3 * (done + s - 1))

                    if s == 2:
                        if not first:
                            pe.wait_ge(v_tok, pair * 4 + 3)
                            turn_output(pair - 1, 1)
                            pe.wait_ge(o_gated, pair * 2)
                        pe.wait_ge(v_tok, pair * 4 + 4)
                    if s >= 2 or not first:
                        pe.wait_ge(pt_copied, done + (s - 1))
                        if s - 2 > 0 or not first:
                            pe.wait_ge(o_tok, done + (s - 2))
                        if s == 11:
                            pe.wait_ge(o_gated, pair * 2 + 1)
                        if project_next and s in (6, 10, 14):
                            pe.wait_ge(q_kept, pair * GROUPS + (GROUPS + (s - 2) // 4))
                        weigh_values((s - 2) % 16)

                    if s == 1:
                        if not first:
                            pe.wait_ge(pt_copied, done)
                        turn_values(pair, par, 0)
                        turn_values(pair, par, 1)
                        if not first:
                            pe.wait_ge(o_tok, done)
                        turn_values(pair, par, 2)
                        if project_next:
                            project(pair + 1, 0, 0)
                        pe.wait_ge(v_tok, pair * 4 + 1)
                        turn_values(pair, par, 3)
                        pe.wait_ge(v_tok, pair * 4 + 4)
                    if s >= 1 or not first:
                        pe.wait_ge(p_sum, done + s)
                        if s > 1 or not first:
                            pe.wait_ge(pt_copied, done + (s - 1))
                        turn_probs((s - 1) % 16)

                    if s == 10:
                        pe.wait_ge(o_tok, done + 8)
                        pe.wait_ge(o_tok, done + 9)
                        turn_output(pair, 0)
                    if project_next and s % 4 and s != 1:
                        project(pair + 1, s // 4, s % 4 - 1)
                    if project_next and s in (5, 9, 13):
                        pe.wait_ge(o_tok, done + (s - 1))
                        query_stats(pair + 1, (s - 5) // 4)

            def finish_attention(pair):
                done = pair * 16
                pe.wait_ge(pt_copied, done + 15)
                pe.wait_ge(o_tok, done + 14)
                weigh_values(14)
                pe.wait_ge(p_sum, done + 16)
                turn_probs(15)
                pe.wait_ge(pt_copied, done + 16)
                pe.wait_ge(o_tok, done + 15)
                weigh_values(15)
                pe.wait_ge(o_tok, done + 16)
                turn_output(pair, 1)

            pe.wait_ge(k_sq, KT)
            pe.wait_ge(n_lo, 32)
            for g in range(4):
                if g:
                    pe.wait_ge(q_sq, g)
                block_gemm(B_QG + g, g % 2, G[0], Y_hi, Y_lo, full).then_inc(gemm_done, 1)
                if g < GROUPS:
                    if g:
                        pe.wait_ge(q_kept, g)
                    query_stats(0, g)
            pe.wait_ge(mask_in_s, 16)

            attend(0, 0, True, True)
            attend(1, 1, False, True)
            with pe.Fori(1, PAIRS // 2 - 1) as i:
                for u in range(2):
                    attend(i * 2 + u, u, False, True)
            attend(PAIRS - 2, 0, False, True)
            attend(PAIRS - 1, 1, False, False)
            finish_attention(PAIRS - 1)

            def out_b(m, par, lead):
                if not lead:
                    pe.wait_ge(h_mix, m + (KT - 1))
                block_gemm(m + B_OUTB, par, G[par], U_hi, U_lo, full,
                           ready=(o_lo, 0) if lead and par == 0 else None).then_inc(gemm_done, 1)

            pe.wait_ge(o_gated, 2 * PAIRS)
            out_b(0, 0, True)
            out_b(1, 1, True)
            feature_stat(KT + 1, GLU[:, :], h_stat, True, False, h_sq)
            with pe.Fori(1, KT // 2) as i:
                for u in range(2):
                    out_b(i * 2 + u, u, False)
                    feature_stat(i * 2 + (KT + u), GLU[:, :], h_stat, False, False, h_sq)
            feature_stat(2 * KT, GLU[:, :], h_stat, False, True, h_sq)
            ple(1, B_PROJ1, B_GATE1, False)

        @block.scalar
        def _(act):
            act.dma_start(H[:, :, :], xT).then_inc(c_x, 16)
            act.dma_start(vecs[:, :], vecs_in).then_inc(c_vecs, 16)
            act.dma_start(blk[:, :], blk_in).then_inc(c_misc, 16)
            act.dma_start(hind[:, :], hind_in).then_inc(c_misc, 16)
            act.dma_start(ident[:, :], ident_in).then_inc(c_misc, 16)

            act.wait_ge(c_x, 16)
            with act.Fori(0, KT) as k:
                act.activation(Y[:, k, :], H[:, k, :], ACT.Square).then_inc(n_sq, 1)

            def inverse_root(logged, signal, n, src, dst, bias=0.0):
                act.activation(dst, src, ACT.Ln, bias=bias).then_inc(logged, 1)
                act.wait_ge(logged, n)
                act.activation(dst, dst, ACT.Exp, scale=-0.5).then_inc(signal, 1)

            def norm_root(n):
                inverse_root(n_log, n_root, n, STAT, R[:, :], eps_d[:, 0:1])

            def norm_hi(instance, dst):
                with act.Fori(0, KT // 2) as i:
                    for u, scratch in enumerate((TMP, SIG)):
                        act.wait_ge(n_tmp, i * 2 + (8 * instance + u + 1))
                        act.activation(dst[:, i * 2 + u, :], scratch[:, :], ACT.Copy).then_inc(n_hi, 1)

            act.wait_ge(stat0, KT)
            act.wait_ge(c_ones, 4)
            norm_root(1)
            norm_hi(0, U)

            def side_products(c, par, warm):
                act.wait_ge(glu_ready, c + 1)
                if warm:
                    act.wait_ge(y_ready, c - 1)
                act.activation(part[:, par, :], glu[:, par, 0:S], ACT.Identity, scale=vec(c * TAPS + V_CW),
                               bias=vec(c + V_CB)).then_inc(part_first, 1)
                for k in range(1, SIDE):
                    if k > 2:
                        act.wait_ge(part_add, c * (SIDE - 1) + (k - 2))
                    elif not (isinstance(c, int) and c == 0):
                        act.wait_ge(part_add, c * (SIDE - 1) + (k - 2))
                    act.activation(prod[:, k % 2, :], glu[:, par, k:k + S], ACT.Copy,
                                   scale=vec(c * TAPS + (V_CW + k))).then_inc(prod_ready, 1)

            def vec(col):
                return vecs[:, col:col + 1] if isinstance(col, int) else vecs[:, bass.ds(col, 1)]

            def abz(c, par, first, warm):
                act.wait_ge(gemm_done, c * 3 + 2)
                if not first:
                    act.wait_ge(glu_ready, c)
                act.activation(SIG[:, :], G[1 - par], ACT.Sigmoid).then_inc(sig_ready, 1)
                if warm:
                    channel_square(c - 2, isinstance(c, int) and c == 2)
                side_products(c, par, warm)
                act.wait_ge(gemm_done, c * 3 + 3)
                if not first:
                    act.wait_ge(z_stored, c * 16)
                act.activation(TMP[:, :], G[par], ACT.Silu).then_inc(z_ready, 1)
                act.wait_ge(z_ready, c + 1)
                act.dma_start(z_dram[bass.ds(c * P, P), :], TMP[:, :]).then_inc(z_stored, 16)

            def channel_square(c, first):
                act.wait_ge(y_ready, c + 1)
                if not first:
                    act.wait_ge(sq_add, c)
                act.activation(R[:, :], Y[:, c, :], ACT.Square).then_inc(sq_ready, 1)

            act.wait_ge(glu_pad, 1)
            abz(0, 0, True, False)
            abz(1, 1, False, False)
            abz(2, 0, False, True)
            abz(3, 1, False, True)
            with act.Fori(2, CT // 2) as i:
                for u in range(2):
                    abz(i * 2 + u, u, False, True)
            channel_square(CT - 2, False)
            channel_square(CT - 1, False)

            act.wait_ge(z_stored, CT * 16)
            act.wait_ge(stat_ready, 1)
            act.activation(SIG[:, :], STAT, ACT.Copy).then_inc(mean_copied, 1)
            act.activation(TMP[:, :], STAT, ACT.Square).then_inc(mean_copied, 1)
            act.wait_ge(stat_ready, 2)
            act.dma_start(H[:, :, :], xT).then_inc(x_back, 16)
            act.wait_ge(ln_step, 2)
            inverse_root(ln_log, ln_root, 1, R[:, :], STAT)

            z_buf = (TMP, GLU)

            def z_load(c, par):
                act.dma_start(z_buf[par][:, :], z_dram[bass.ds(c * P, P), :]).then_inc(z_back[par], 16)

            z_load(0, 0)
            z_load(1, 1)

            def ln_silu(c):
                act.wait_ge(y_norm, c + 1)
                act.activation(Y[:, c, :], Y[:, c, :], ACT.Silu, scale=vecs[:, V_LNG + c:V_LNG + c + 1] if isinstance(c, int) else vecs[:, bass.ds(c + V_LNG, 1)],
                               bias=vecs[:, V_LNB + c:V_LNB + c + 1] if isinstance(c, int) else vecs[:, bass.ds(c + V_LNB, 1)]).then_inc(y_silu, 1)

            def ln_hi(c, par, more):
                act.wait_ge(yz_ready, c + 1)
                act.activation(U[:, c, :], Y[:, c, :], ACT.Copy).then_inc(yz_hi, 1)
                if more:
                    z_load(c + 2, par)

            ln_silu(0)
            with act.Fori(0, CT // 2 - 1) as i:
                for u in range(2):
                    ln_silu(i * 2 + (u + 1))
                    ln_hi(i * 2 + u, u, True)
            ln_silu(CT - 1)
            ln_hi(CT - 2, 0, False)
            ln_hi(CT - 1, 1, False)

            def stream_square(m, first, layer, made, squared, counted):
                act.wait_ge(made, m + (layer * KT + 1))
                if not first:
                    act.wait_ge(counted, m + layer * KT)
                act.activation(GLU[:, :], H[:, m, :], ACT.Square).then_inc(squared, 1)

            def stream_squares(layer):
                stream_square(0, True, layer, h_mix, h_sq, h_stat)
                with act.Fori(1, KT) as m:
                    stream_square(m, False, layer, h_mix, h_sq, h_stat)

            def ple(layer, instance, with_stat):
                done = layer * KT
                act.wait_ge(gemm_done, (B_PROJ0, B_PROJ1)[layer])
                act.dma_start(Y[:, 0:PK, :], pT[:, layer, :, :]).then_inc(p_in, 16)
                act.wait_ge(p_in, (layer + 1) * 16)
                for k in range(PK):
                    act.activation(YR[:, PK + k, :], Y[:, k, :], ACT.Copy).then_inc(p_hi, 1)
                act.wait_ge(h_stat, done + KT)
                norm_root((2, 4)[layer])
                norm_hi(instance, U)
                for m in range(KT):
                    act.wait_ge(proj_done, done + m + 1)
                    act.activation(Y[:, KT + m, :], G[m % 2], ACT.Copy).then_inc(pp_ready, 1)

                def gate(m, par, first):
                    act.wait_ge(gemm_done, m + ((B_GATE0, B_GATE1)[layer] + 1))
                    if not first:
                        act.wait_ge(gate_mul, m + done)
                    act.activation(SIG[:, :], G[par], ACT.Sigmoid).then_inc(gate_sig, 1)

                def square(m, first):
                    if with_stat:
                        stream_square(m, first, layer, h_gate, g_sq, g_stat)
                    else:
                        act.wait_ge(h_gate, m + (done + 1))
                        act.dma_start(out[:, m, :] if isinstance(m, int) else out[:, bass.ds(m, 1), :],
                                      H[:, m, :] if isinstance(m, int) else H[:, bass.ds(m, 1), :]).then_inc(out_done, 16)

                gate(0, 0, True)
                gate(1, 1, False)
                square(0, True)
                with act.Fori(1, KT // 2) as i:
                    for u in range(2):
                        gate(i * 2 + u, u, False)
                        square(i * 2 + (u - 1), False)
                square(KT - 1, False)

            stream_squares(0)
            ple(0, 1, True)

            act.wait_ge(g_stat, KT)
            norm_root(3)
            norm_hi(2, U)
            norm_hi(3, YR)
            act.wait_ge(n_lo, 32)
            act.dma_start(h_dram, H[:, :, :].rearrange("p k s -> p (k s)")).then_inc(h_stored, 16)

            v_buf = (TMP, SIG)

            def value(m, j, par, first):
                act.wait_ge(gemm_done, m + (B_V + 1))
                if not first:
                    act.wait_ge(v_stored[par], j * 16)
                act.activation(v_buf[par][:, :], G[par], ACT.Copy).then_inc(v_ready, 1)
                act.wait_ge(v_ready, m + 1)
                act.dma_start(v_dram[bass.ds(m * P, P), :], v_buf[par][:, :]).then_inc(v_stored[par], 16)

            value(0, 0, 0, True)
            value(1, 0, 1, True)
            with act.Fori(1, KT // 2) as i:
                for u in range(2):
                    value(i * 2 + u, i, u, False)

            act.wait_ge(h_stored, 16)
            act.dma_start(cos[:, :], cs_in[0]).then_inc(rope_in, 16)
            act.dma_start(sin[:, :], cs_in[1]).then_inc(rope_in, 16)

            def key(m, par, first):
                act.wait_ge(gemm_done, m + (B_K + 1))
                if not first:
                    act.wait_ge(k_chain, m * 4 - 3)
                act.activation(raw_g[:, :], G[par], ACT.Copy, scale=vecs[:, V_KG:V_KG + 1]).then_inc(k_gain, 1)
                if not first:
                    act.wait_ge(k_stat, m)
                act.activation(sqr[:, :], G[par], ACT.Square).then_inc(k_sq, 1)
                act.wait_ge(k_stat, m + 1)
                if not first:
                    act.wait_ge(k_chain, m * 4 - 3)
                inverse_root(k_log, k_root, m + 1, STAT, r_k[:, :], eps_d[:, 0:1])

            def key_store(m):
                act.wait_ge(k_ready, m + 1)
                act.dma_start(k_dram[bass.ds(m * P, P), :], roped[:, :]).then_inc(k_stored, 16)

            key(0, 0, True)
            key(1, 1, False)
            key_store(0)
            with act.Fori(1, KT // 2) as i:
                for u in range(2):
                    key(i * 2 + u, u, False)
                    key_store(i * 2 + (u - 1))
            key_store(KT - 1)

            for u in range(2):
                act.wait_ge(v_stored[u], KT // 2 * 16)
            act.wait_ge(k_stored, KT * 16)
            act.wait_ge(gemm_done, B_QG)
            act.dma_start(masks[:, :], mask_in).then_inc(mask_in_s, 16)

            def load_pair(pair, par):
                act.dma_start(kpair[:, par, :], k_dram[bass.ds(pair * P, P), :]).then_inc(kv_in[par], 16)
                act.dma_start(vpair[:, par, :], v_dram[bass.ds(pair * P, P), :]).then_inc(kv_in[par], 16)

            load_pair(0, 0)
            load_pair(1, 1)

            def query(pair, g, first):
                act.wait_ge(gemm_done, pair * 4 + (B_QG + g + 1))
                if not first:
                    act.wait_ge(q_chain, pair * 9 + (3 * g - 1))
                    act.wait_ge(q_stat, pair * GROUPS + g)
                act.activation(raw_g[:, :], G[0], ACT.Copy, scale=vecs[:, V_QG + g:V_QG + g + 1]).then_inc(q_gain, 1)
                act.activation(sqr[:, :], G[0], ACT.Square).then_inc(q_sq, 1)

            def query_root(pair, par):
                act.wait_ge(q_kept, pair * GROUPS + GROUPS)
                cols = stat[:, par * 48:par * 48 + 48]
                inverse_root(q_log, q_root, pair + 1, cols, cols, eps_d[:, 1:2])

            def gate_part(pair, par):
                act.wait_ge(gemm_done, pair * 4 + (B_QG + 4))
                act.activation(sg[:, par, :], G[0], ACT.Exp, scale=-1.0).then_inc(gate_exp, 1)
                act.activation(gbuf[:, :], G[0], ACT.Copy).then_inc(gate_raw, 1)

            def exps(pair, par, s):
                b, hh, r = STEPS[s]
                act.wait_ge(sc_max, pair * 16 + (s + 1))
                nn, nf = (NEAR, FAR) if b else (HALF, SPAN)
                tile = b * RES + r
                for g, col, n in ((0, 0, nn), (1, C1, nf), (2, C2, nf)):
                    at_ = par * 48 + tile * 6 + hh * 3 + g
                    dst = col if g < 2 else C1 + FAR
                    act.activation(prob[:, s % 2, dst:dst + n], SC[:, col:col + n], ACT.Exp,
                                   bias=small[:, 4:5], scale=stat[:, at_:at_ + 1],
                                   accum_out=small[:, 8 + g:9 + g]).then_inc(p_part, 1)

            def copy_turned(pair, s):
                b, hh, r = STEPS[s]
                n = (NEAR + FAR) if b else (HALF + SPAN)
                act.wait_ge(pt_ready, pair * 16 + (s + 1))
                act.activation(probT[:, s % 2, 0:n], PT[:, 0:n], ACT.Copy).then_inc(pt_copied, 1)

            for g in range(GROUPS):
                query(0, g, g == 0)
            query_root(0, 0)
            act.wait_ge(mask_in_s, 16)

            def attend(pair, par, first, project_next, load_next):
                for s in range(16):
                    exps(pair, par, s)
                    if s > 0:
                        copy_turned(pair, s - 1)
                    elif not first:
                        copy_turned(pair - 1, 15)
                    if s == 0:
                        gate_part(pair, par)
                    if project_next and s in (4, 8, 12):
                        query(pair + 1, s // 4 - 1, False)
                    if project_next and s == 14:
                        query_root(pair + 1, 1 - par)
                    if s == 5 and not first:
                        act.wait_ge(o_gated, pair * 2)
                        act.dma_start(o_dram[bass.ds((pair - 1) * P, P), :], obuf[:, :]).then_inc(o_stored, 16)
                        if load_next:
                            load_pair(pair + 1, 1 - par)

            def finish_attention(pair):
                copy_turned(pair, 15)
                act.wait_ge(o_gated, pair * 2 + 2)
                act.dma_start(o_dram[bass.ds(pair * P, P), :], obuf[:, :]).then_inc(o_stored, 16)

            attend(0, 0, True, True, True)
            attend(1, 1, False, True, True)
            with act.Fori(1, PAIRS // 2 - 1) as i:
                for u in range(2):
                    attend(i * 2 + u, u, False, True, True)
            attend(PAIRS - 2, 0, False, True, True)
            attend(PAIRS - 1, 1, False, False, False)
            finish_attention(PAIRS - 1)

            act.wait_ge(o_stored, PAIRS * 16)
            act.wait_ge(gemm_done, B_OUTB)
            for k in range(KT):
                act.dma_start(Y[:, k, :], o_dram[k * P:k * P + P, :]).then_inc(o_back, 16)
            act.dma_start(H[:, :, :].rearrange("p k s -> p (k s)"), h_dram).then_inc(h_back, 16)
            act.wait_ge(o_back, KT * 16)
            with act.Fori(0, KT) as k:
                act.activation(U[:, k, :], Y[:, k, :], ACT.Copy).then_inc(o_hi, 1)
            stream_squares(1)
            ple(1, 4, False)
            act.wait_ge(out_done, KT * 16)

        @block.vector
        def _(dve):
            dve.memset(ones_d[:, :], 1.0 / D).then_inc(c_ones, 1)
            dve.memset(ones_c[:, :], 1.0 / CH).then_inc(c_ones, 1)
            dve.memset(eps_d[:, 0:1], EPS).then_inc(c_ones, 1)
            dve.memset(eps_d[:, 1:2], EPS * HEAD).then_inc(c_ones, 1)
            dve.wait_ge(c_vecs, 16)
            dve.wait_ge(c_ones, 4)

            def vec(col):
                return vecs[:, col:col + 1] if isinstance(col, int) else vecs[:, bass.ds(col, 1)]

            def norm(instance, roots, gain, hi, lo):
                dve.wait_ge(n_root, roots)
                base_n = 8 * instance
                if instance:
                    dve.wait_ge(n_lo, base_n)

                def scaled(k, scratch):
                    dve.scalar_tensor_tensor(out=scratch[:, :], in0=H[:, k, :], scalar=vec(k + gain), in1=R[:, :],
                                             op0=ALU.mult, op1=ALU.mult).then_inc(n_tmp, 1)

                def low(k, scratch):
                    dve.wait_ge(n_hi, k + (base_n + 1))
                    dve.tensor_tensor(lo[:, k, :], scratch[:, :], hi[:, k, :].bitcast(F32),
                                      ALU.subtract).then_inc(n_lo, 1)

                scaled(0, TMP)
                scaled(1, SIG)
                with dve.Fori(0, KT // 2 - 1) as i:
                    for u, scratch in enumerate((TMP, SIG)):
                        low(i * 2 + u, scratch)
                        dve.wait_ge(n_lo, i * 2 + (u + base_n + 1))
                        scaled(i * 2 + (u + 2), scratch)
                low(KT - 2, TMP)
                low(KT - 1, SIG)

            dve.wait_ge(c_x, 16)
            norm(0, 1, V_NORM, U[:, 0:KT, :], U[:, KT:2 * KT, :])

            dve.wait_ge(n_lo, KT)
            dve.memset(glu[:, :, 0:PAD], 0.0).then_inc(glu_pad, 1)
            dve.wait_ge(glu_pad, 1)

            def gate_linear(c, par, warm):
                dve.wait_ge(gemm_done, c * 3 + 1)
                dve.wait_ge(sig_ready, c + 1)
                if warm:
                    dve.wait_ge(y_ready, c - 1)
                    dve.wait_ge(prod_ready, c * (SIDE - 1) - (SIDE - 1))
                dve.tensor_tensor(glu[:, par, PAD:PAD + S], G[par], SIG[:, :], ALU.mult).then_inc(glu_ready, 1)

            def convolve(c, par, first):
                dve.wait_ge(glu_ready, c + 1)
                dve.wait_ge(part_add, c * (SIDE - 1) + (SIDE - 1))
                if not first:
                    dve.wait_ge(y_ready, c)
                for t in range(MAIN):
                    j = SIDE + t
                    x, w, acc = glu[:, par, j:j + S], vec(c * TAPS + (V_CW + j)), CONV[t % 2]
                    if t >= 2:
                        dve.wait_ge(conv_step, c * (MAIN - 1) + (t - 1))
                    if t == 1:
                        dve.tensor_scalar(acc, x, w, None, ALU.mult).then_inc(conv_step, 1)
                    elif t == MAIN - 1:
                        dve.scalar_tensor_tensor(out=Y[:, c, :], in0=x, scalar=w, in1=acc, op0=ALU.mult,
                                                 op1=ALU.add).then_inc(conv_odd, 1)
                    else:
                        dve.scalar_tensor_tensor(out=acc, in0=x, scalar=w, in1=acc if t else part[:, par, :],
                                                 op0=ALU.mult, op1=ALU.add).then_inc(conv_step, 1)
                dve.wait_ge(conv_odd, c + 1)
                dve.wait_ge(conv_step, c * (MAIN - 1) + (MAIN - 1))
                dve.tensor_tensor(Y[:, c, :], Y[:, c, :], CONV[0], ALU.add).then_inc(y_ready, 1)

            gate_linear(0, 0, False)
            gate_linear(1, 1, False)
            convolve(0, 0, True)
            gate_linear(2, 0, True)
            convolve(1, 1, False)
            with dve.Fori(1, CT // 2 - 1) as i:
                for u in range(2):
                    gate_linear(i * 2 + (u + 1), 1 - u, True)
                    convolve(i * 2 + u, u, False)
            gate_linear(CT - 1, 1, True)
            convolve(CT - 2, 0, False)
            convolve(CT - 1, 1, False)

            dve.wait_ge(stat_ready, 2)
            dve.wait_ge(mean_copied, 2)
            dve.tensor_tensor(R[:, :], E2, TMP[:, :], ALU.subtract).then_inc(ln_step, 1)
            dve.wait_ge(ln_step, 1)
            dve.tensor_scalar(R[:, :], R[:, :], 0.0, EPS, ALU.max, ALU.add).then_inc(ln_step, 1)
            dve.wait_ge(ln_root, 1)

            z_buf = (TMP, GLU)

            def ln_norm(c):
                dve.wait_ge(y_cent, c + 1)
                dve.tensor_tensor(Y[:, c, :], Y[:, c, :], STAT, ALU.mult).then_inc(y_norm, 1)

            def ln_gate(c, j, par):
                dve.wait_ge(y_silu, c + 1)
                dve.wait_ge(z_back[par], j * 16 + 16)
                dve.tensor_tensor(Y[:, c, :], Y[:, c, :], z_buf[par][:, :], ALU.mult).then_inc(yz_ready, 1)

            def ln_low(c):
                dve.wait_ge(yz_hi, c + 1)
                dve.tensor_tensor(YR[:, c, :], Y[:, c, :], U[:, c, :].bitcast(F32), ALU.subtract).then_inc(yz_lo, 1)

            ln_norm(0)
            ln_norm(1)
            ln_gate(0, 0, 0)
            ln_norm(2)
            ln_gate(1, 0, 1)
            ln_low(0)
            with dve.Fori(1, CT // 2 - 1) as i:
                for u in range(2):
                    ln_norm(i * 2 + (u + 1))
                    ln_gate(i * 2 + u, i, u)
                    ln_low(i * 2 + (u - 1))
            ln_norm(CT - 1)
            ln_gate(CT - 2, CT // 2 - 1, 0)
            ln_low(CT - 3)
            ln_gate(CT - 1, CT // 2 - 1, 1)
            ln_low(CT - 2)
            ln_low(CT - 1)

            def residual(layer, n0, per):
                if layer == 0:
                    dve.wait_ge(x_back, 16)
                with dve.Fori(0, KT // 2) as i:
                    for u in range(2):
                        dve.wait_ge(gemm_done, i * (2 * per) + (n0 + (u + 1) * per))
                        dve.tensor_tensor(H[:, i * 2 + u, :], H[:, i * 2 + u, :], G[u], ALU.add).then_inc(h_mix, 1)

            def ple(layer, instance):
                done = layer * KT
                for k in range(PK):
                    dve.wait_ge(p_hi, layer * PK + k + 1)
                    dve.tensor_tensor(YR[:, 2 * PK + k, :], Y[:, k, :], YR[:, PK + k, :].bitcast(F32),
                                      ALU.subtract).then_inc(p_lo, 1)
                norm(instance, (2, 4)[layer], V_PLE + layer * KT, U[:, 0:KT, :], U[:, KT:2 * KT, :])
                def gate(m, first):
                    dve.wait_ge(gate_sig, m + (done + 1))
                    if not first:
                        dve.wait_ge(h_gate, m + done)
                    dve.tensor_tensor(TMP[:, :], SIG[:, :], Y[:, m + KT, :], ALU.mult).then_inc(gate_mul, 1)
                    dve.wait_ge(gate_mul, m + (done + 1))
                    dve.tensor_tensor(H[:, m, :], H[:, m, :], TMP[:, :], ALU.add).then_inc(h_gate, 1)

                gate(0, True)
                with dve.Fori(1, KT) as m:
                    gate(m, False)

            residual(0, B_OUTA, 2)
            ple(0, 1)
            norm(2, 3, V_KV, U[:, 0:KT, :], U[:, KT:2 * KT, :])
            norm(3, 3, V_NORM + KT, YR[:, 0:KT, :], YR[:, KT:2 * KT, :])

            turn = list(range(ROPE // 2, ROPE)) + list(range(ROPE // 2)) + list(range(ROPE, 32))

            def key(m, first):
                dve.wait_ge(k_root, m + 1)
                dve.wait_ge(k_gain, m + 1)
                if not first:
                    dve.wait_ge(k_ready, m)
                dve.tensor_tensor(raw_g2[:, :], raw_g[:, :], r_k[:, :], ALU.mult).then_inc(k_chain, 1)
                if not first:
                    dve.wait_ge(k_stored, m * 16)
                dve.wait_ge(k_chain, m * 4 + 1)
                dve.tensor_tensor(roped[:, :], raw_g2[:, :], cos[:, :], ALU.mult).then_inc(k_chain, 1)
                dve.stream_shuffle(shuf[:, :], raw_g2[:, :], turn).then_inc(k_chain, 1)
                dve.wait_ge(k_chain, m * 4 + 3)
                dve.tensor_tensor(shuf[:, :], shuf[:, :], sin[:, :], ALU.mult).then_inc(k_chain, 1)
                dve.wait_ge(k_chain, m * 4 + 4)
                dve.tensor_tensor(roped[:, :], roped[:, :], shuf[:, :], ALU.add).then_inc(k_ready, 1)

            raw_g2 = obuf
            dve.wait_ge(c_misc, 48)
            dve.tensor_copy(ident_b[:, :], ident[:, :]).then_inc(c_ones, 1)
            dve.wait_ge(rope_in, 32)
            key(0, True)
            with dve.Fori(1, KT) as m:
                key(m, False)

            def query(pair, par, g, part, first):
                q = qbuf[:, par, g, :]
                if part == 0:
                    dve.wait_ge(q_gain, pair * GROUPS + (g + 1))
                    if not first:
                        dve.wait_ge(q_ready, pair * GROUPS + g)
                    dve.tensor_tensor(q, raw_g[:, :], cos[:, :], ALU.mult).then_inc(q_chain, 1)
                elif part == 1:
                    dve.stream_shuffle(shuf[:, :], raw_g[:, :], turn).then_inc(q_chain, 1)
                elif part == 2:
                    dve.wait_ge(q_chain, pair * 9 + (3 * g + 2))
                    dve.tensor_tensor(shuf[:, :], shuf[:, :], sin[:, :], ALU.mult).then_inc(q_chain, 1)
                else:
                    dve.wait_ge(q_chain, pair * 9 + (3 * g + 3))
                    dve.tensor_tensor(q, q, shuf[:, :], ALU.add).then_inc(q_ready, 1)

            def keep_stats(pair, par, g):
                dve.wait_ge(q_stat, pair * GROUPS + (g + 1))
                cols = stat[:, par * 48:par * 48 + 48].rearrange("p (t h g) -> p t h g", h=2, g=GROUPS)
                src = MISC[:, 0:64].rearrange("p (t h g) -> p t h g", h=2, g=4)
                dve.tensor_copy(cols[:, :, :, g], src[:, :, :, g]).then_inc(q_kept, 1)

            def gate_rest(pair, par, part):
                if part == 0:
                    dve.wait_ge(gate_exp, pair + 1)
                    dve.tensor_scalar(sg[:, par, :], sg[:, par, :], 1.0, None, ALU.add).then_inc(gate_chain, 1)
                elif part < 5:
                    quarter = slice((part - 1) * FAR, part * FAR)
                    dve.wait_ge(gate_chain, pair * 5 + 1)
                    dve.reciprocal(sg[:, par, quarter], sg[:, par, quarter]).then_inc(gate_chain, 1)
                else:
                    dve.wait_ge(gate_chain, pair * 5 + 5)
                    dve.wait_ge(gate_raw, pair + 1)
                    dve.tensor_tensor(sg[:, par, :], gbuf[:, :], sg[:, par, :], ALU.mult).then_inc(gate_ready, 1)

            def values(pair, rnd):
                dve.wait_ge(v_turned, pair * 4 + (rnd + 1))
                bank = (PT[:, 0:HALF], PT[:, HALF:2 * HALF], MISC, PT[:, 0:HALF])[rnd]
                dve.tensor_copy(vtok[:, 4 * rnd:4 * rnd + 4, :].rearrange("p t n -> p (t n)"), bank).then_inc(v_tok, 1)

            def maxima(pair, par, s, first):
                b, hh, r = STEPS[s]
                dve.wait_ge(sc_near, pair * 16 + (s + 1))
                if s > 0 or not first:
                    dve.wait_ge(p_part, (pair * 16 + s) * 3)
                nn, nf = (NEAR, FAR) if b else (HALF, SPAN)
                dve.tensor_reduce(small[:, 0:1], SC[:, 0:nn], AX.X, ALU.max).then_inc(m_chain, 1)
                dve.wait_ge(sc_ready, pair * 16 + (s + 1))
                far = SC[:, C1:C1 + 2 * (C2 - C1)].rearrange("p (g n) -> p g n", g=2)[:, :, 0:nf]
                dve.tensor_reduce(small[:, 1:3], far, AX.X, ALU.max).then_inc(m_chain, 1)
                dve.wait_ge(m_chain, pair * 48 + (3 * s + 2))
                at_ = par * 48 + (b * RES + r) * 6 + hh * 3
                dve.tensor_tensor(small[:, 0:3], small[:, 0:3], stat[:, at_:at_ + 3], ALU.mult).then_inc(m_chain, 1)
                dve.wait_ge(m_chain, pair * 48 + (3 * s + 3))
                dve.tensor_reduce(small[:, 4:5], small[:, 0:3], AX.X, ALU.max, negate=True).then_inc(sc_max, 1)

            def add_far(pair, s, first):
                b, hh, r = STEPS[s]
                nf = FAR if b else SPAN
                dve.wait_ge(p_part, (pair * 16 + (s + 1)) * 3)
                if s > 1 or not first:
                    dve.wait_ge(o_tok, pair * 16 + (s - 1))
                dve.tensor_reduce(lsum[:, s % 2:s % 2 + 1], small[:, 8:11], AX.X, ALU.add).then_inc(l_chain, 1)
                dve.tensor_tensor(prob[:, s % 2, C1:C1 + nf], prob[:, s % 2, C1:C1 + nf],
                                  prob[:, s % 2, C1 + FAR:C1 + FAR + nf], ALU.add).then_inc(p_sum, 1)
                dve.wait_ge(l_chain, pair * 32 + (2 * s + 1))
                dve.reciprocal(lsum[:, s % 2:s % 2 + 1], lsum[:, s % 2:s % 2 + 1]).then_inc(l_chain, 1)

            def output(pair, s):
                b, hh, r = STEPS[s]
                dve.wait_ge(o_ready, pair * 16 + (s + 1))
                dve.wait_ge(l_chain, pair * 32 + (2 * s + 2))
                dve.tensor_scalar(otok[:, b * RES + r, hh * HEAD:hh * HEAD + HEAD], MISC[:, 0:HEAD],
                                  lsum[:, s % 2:s % 2 + 1], None, ALU.mult).then_inc(o_tok, 1)

            def gated(pair, par, b, first):
                dve.wait_ge(ot_ready, pair * 2 + (b + 1))
                if b == 0 and not first:
                    dve.wait_ge(o_stored, pair * 16)
                dve.wait_ge(gate_ready, pair + 1)
                half = slice(b * HALF, b * HALF + HALF)
                dve.tensor_tensor(obuf[:, half], MISC, sg[:, par, half], ALU.mult).then_inc(o_gated, 1)

            dve.wait_ge(k_stored, KT * 16)
            for g in range(GROUPS):
                for q_part in range(4):
                    query(0, 0, g, q_part, g == 0)
                keep_stats(0, 0, g)

            def attend(pair, par, first, project_next):
                dve.wait_ge(q_root, pair + 1)
                for s in range(16):
                    maxima(pair, par, s, first)
                    if s == 2 and not first:
                        gated(pair - 1, 1 - par, 1, False)
                    if s >= 2:
                        output(pair, s - 2)
                    elif not first:
                        output(pair - 1, 14 + s)
                    if s == 1:
                        for rnd in range(3):
                            values(pair, rnd)
                    add_far(pair, s, first)
                    if s == 0:
                        gate_rest(pair, par, 0)
                    if s == 1:
                        values(pair, 3)
                    if 2 <= s < 7:
                        gate_rest(pair, par, s - 1)
                    if s == 10:
                        gated(pair, par, 0, first)
                    if project_next and s >= 4:
                        query(pair + 1, 1 - par, s // 4 - 1, s % 4, False)
                    if project_next and s in (5, 9, 13):
                        keep_stats(pair + 1, 1 - par, (s - 5) // 4)

            def finish_attention(pair, par):
                output(pair, 14)
                output(pair, 15)
                gated(pair, par, 1, False)

            attend(0, 0, True, True)
            attend(1, 1, False, True)
            with dve.Fori(1, PAIRS // 2 - 1) as i:
                for u in range(2):
                    attend(i * 2 + u, u, False, True)
            attend(PAIRS - 2, 0, False, True)
            attend(PAIRS - 1, 1, False, False)
            finish_attention(PAIRS - 1, 1)

            with dve.Fori(0, KT) as k:
                dve.wait_ge(o_hi, k + 1)
                dve.tensor_tensor(U[:, k + KT, :], Y[:, k, :], U[:, k, :].bitcast(F32), ALU.subtract).then_inc(o_lo, 1)
            dve.wait_ge(h_back, 16)
            residual(1, B_OUTB, 1)
            ple(1, 4)


def ARENA_BASE(nc, size):
    return nc.sbuf_base - size


def kernel(x, p, norm_g, w_in_a, conv_w, conv_b, ln_g, ln_b, w_out_a, kv_norm_g, w_kv, k_norm_g,
           w_in_b, q_norm_g, w_out_b, ple_norm_g, w_ple_gate, w_ple_proj):
    import ml_dtypes
    import concourse.bacc as bacc
    from concourse.bass_utils import run_bass_kernel_spmd

    f = np.float32

    def cols(w, n0):
        return w[:, n0:n0 + P].reshape(-1, P, P).transpose(1, 0, 2).reshape(P, -1)

    def proj_blocks(w):
        return [np.concatenate([cols(w, (4 * j + m) * P) for m in range(4)], axis=1) for j in range(2)]

    x, p, norm_g, w_in_a, conv_w, conv_b, ln_g, ln_b, w_out_a, kv_norm_g, w_kv, k_norm_g, w_in_b, \
        q_norm_g, w_out_b, ple_norm_g, w_ple_gate, w_ple_proj = (
            np.asarray(a) for a in (x, p, norm_g, w_in_a, conv_w, conv_b, ln_g, ln_b, w_out_a, kv_norm_g, w_kv,
                                    k_norm_g, w_in_b, q_norm_g, w_out_b, ple_norm_g, w_ple_gate, w_ple_proj))
    wa, woa, wb, wob = w_in_a[0], w_out_a[0], w_in_b[0], w_out_b[0]
    blocks = []
    for c in range(CT):
        blocks += [cols(wa, part * CH + c * P) for part in range(3)]
    for m in range(KT):
        blocks += [cols(woa[0:D], m * P), cols(woa[D:CH], m * P)]
    blocks += proj_blocks(w_ple_proj[0])
    blocks += [cols(w_ple_gate[0], m * P) for m in range(KT)]
    blocks += [cols(w_kv, D + m * P) for m in range(KT)]
    blocks += [cols(w_kv, m * P) for m in range(KT)]
    for i in range(PAIRS):
        blocks += [cols(wb, g * D + i * P) for g in range(4)]
    blocks += [cols(wob, m * P) for m in range(KT)]
    blocks += proj_blocks(w_ple_proj[1])
    blocks += [cols(w_ple_gate[1], m * P) for m in range(KT)]
    w_all = np.concatenate(blocks, axis=0)

    def tiles(v):
        return v.reshape(-1, P).T

    vecs = np.concatenate([
        tiles(norm_g), tiles(ple_norm_g), tiles(kv_norm_g), tiles(conv_b), tiles(ln_g), tiles(ln_b),
        np.tile(k_norm_g, 2)[:, None], np.tile(q_norm_g[0], (1, 2)).T,
        conv_w[0].T.reshape(CT, P, TAPS).transpose(1, 0, 2).reshape(P, CT * TAPS)], axis=1)

    half = ROPE // 2
    inv = f(500000.0) ** (-np.arange(half, dtype=f) * f(2.0 / ROPE))
    ang = np.arange(S, dtype=f)[:, None] * inv[None, :]
    cs = np.zeros((2, P, S), f)
    cs[0] = 1.0
    for head in range(2):
        for part in range(2):
            rows = slice(head * HEAD + part * half, head * HEAD + (part + 1) * half)
            cs[0, rows] = np.cos(ang).T
            cs[1, rows] = (np.sin(ang) if part else -np.sin(ang)).T
    ident = np.eye(P, dtype=f)
    blk = np.kron(np.eye(2), np.ones((HEAD, HEAD))).astype(f) / f(HEAD)
    hind = np.kron(np.eye(2), np.ones((HEAD, 1))).astype(f)
    masks = np.full((P, MASKS), -1e30, f)
    q = np.arange(P)[:, None]
    for r in range(RES):
        dist = RES * q + r + SPAN - np.arange(NEAR)[None, :]
        masks[:, r * NEAR:(r + 1) * NEAR][(dist >= 0) & (dist <= SPAN)] = 0
    dist = q + SPAN - np.arange(FAR)[None, :]
    masks[:, RES * NEAR:RES * NEAR + FAR][(dist >= 0) & (dist <= SPAN)] = 0
    masks[:, RES * NEAR + FAR:][(dist >= 0) & (dist % 4 == 0)] = 0

    arrays = {
        "in_xT": x[0].T.reshape(KT, P, S).transpose(1, 0, 2),
        "in_pT": p[:, 0].transpose(0, 2, 1).reshape(2, PK, P, S).transpose(2, 0, 1, 3),
        "in_vecs": vecs, "in_w": w_all, "in_cs": cs, "in_ident": ident, "in_blk": blk, "in_hind": hind,
        "in_masks": masks.astype(ml_dtypes.bfloat16),
    }
    arrays = {k: np.ascontiguousarray(v) for k, v in arrays.items()}
    nc = bacc.Bacc("TRN2", target_bir_lowering=False, num_devices=1)
    args = [nc.dram_tensor(k, v.shape, mybir.dt.from_np(v.dtype), kind="ExternalInput").ap()
            for k, v in arrays.items()]
    out = nc.dram_tensor("out_hT", (P, KT, S), F32, kind="ExternalOutput").ap()
    build(nc, *args, out)
    r = run_bass_kernel_spmd(nc, [arrays], core_ids=[0])
    hT = r.results[0]["out_hT"]
    return np.ascontiguousarray(hT.transpose(2, 1, 0).reshape(1, S, D))
```

```python
from contextlib import ExitStack

import numpy as np

import concourse.bass as bass
from concourse import mybir

F32 = mybir.dt.float32
F32R = mybir.dt.float32r
BF16 = mybir.dt.bfloat16
ALU = mybir.AluOpType
ACT = mybir.ActivationFunctionType
AX = mybir.AxisListType

P = 128
D = 1024
S = 1024
CH = 2 * D
TAPS = 31
HEAD = 64
ROPE = HEAD // 4
PLE = 256
GROUPS = 3
EPS = 1e-6
HALF = 512
KT = D // P
CT = CH // P
PK = PLE // P
PAIRS = KT
PAD = TAPS - 1
SIDE = 7
STAGES = ((1, 3), (3, 5), (5, 7))
LEAD = 3
HI_SIDE = 3 * CT
MAIN = TAPS - SIDE
LAST = 16

B_ABZ = 0
B_OUTA = B_ABZ + 3 * CT
B_PROJ0 = B_OUTA + 2 * KT
B_GATE0 = B_PROJ0 + 2
B_V = B_GATE0 + KT
B_K = B_V + KT
B_QG = B_K + KT
B_OUTB = B_QG + 4 * PAIRS
B_PROJ1 = B_OUTB + KT
B_GATE1 = B_PROJ1 + 2
BLOCKS = B_GATE1 + KT

V_NORM = 0
V_PLE = V_NORM + 2 * KT
V_KV = V_PLE + 2 * KT
V_CB = V_KV + KT
V_LNG = V_CB + CT
V_LNB = V_LNG + CT
V_KG = V_LNB + CT
V_QG = V_KG + 1
V_CW = V_QG + GROUPS
VECS = V_CW + CT * TAPS

RES = 4
QB = S // HALF
SPAN = 128
STEPS = [(b, hh, r) for b in range(QB) for hh in range(2) for r in range(RES)]
NEAR = HALF + SPAN
FAR = 2 * SPAN
MASKS = RES * NEAR + 2 * FAR
C1 = NEAR
C2 = 2 * HALF

SPLIT = 10
EARLY = 11
GONE = 6


def early_tiles(s):
    return [k for k in range(KT - 1) if max(k - 1, 0) == s - SPLIT]


def build(nc, xT, pT, vecs_in, w_in, cs_in, ident_in, blk_in, hind_in, mask_in, out):
    z_dram = nc.dram_tensor("z_dram", (CT * P, S), F32, kind="Internal").ap()
    k_dram = nc.dram_tensor("k_dram", (KT * P, S), F32, kind="Internal").ap()
    v_dram = nc.dram_tensor("v_dram", (KT * P, S), F32, kind="Internal").ap()
    o_dram = nc.dram_tensor("o_dram", (KT * P, S), F32, kind="Internal").ap()
    h_dram = nc.dram_tensor("h_dram", (P, KT * S), F32, kind="Internal").ap()

    with ExitStack() as ctx:
        KB = 1024
        size = 207 * KB + 512
        ctx.enter_context(nc.sbuf_tensor("arena", [P, size], mybir.dt.uint8))
        base = nc.sbuf_base - size

        def at(name, shape, dt, off):
            n = int(np.prod(shape[1:])) * (2 if dt == BF16 else 4)
            assert off % 32 == 0 and off + n <= size, name
            return nc.alloc_sbuf_tensor_at(name, shape, dt, offset=base + off)

        H_AT, U_AT, Y_AT, W_AT, T_AT = 0, 32 * KB, 96 * KB, 160 * KB, 184 * KB
        H = at("H", [P, KT, S], F32, H_AT)
        U = at("U", [P, 2 * KT, S], F32R, U_AT)
        Y = at("Y", [P, CT, S], F32, Y_AT)
        YR = at("YR", [P, CT, S], F32R, Y_AT)
        W_raw = at("W_raw", [P, 2, S], F32, W_AT)
        W_hi = at("W_hi", [P, 2, S], F32R, W_AT + 8 * KB)
        W_lo = at("W_lo", [P, 2, S], F32R, W_AT + 16 * KB)
        t = T_AT
        vecs = at("vecs", [P, VECS], F32, t); t += -(-VECS * 4 // 32) * 32
        ones_d = at("ones_d", [P, P], F32, t); t += 512
        ones_c = at("ones_c", [P, P], F32, t); t += 512
        blk = at("blk", [P, P], F32, t); t += 512
        ident = at("ident", [P, P], F32, t); t += 512
        ident_b = at("ident_b", [P, P], BF16, t); t += 256
        hind = at("hind", [P, 2], F32, t); t += 32
        eps_d = at("eps_d", [P, 2], F32, t); t += 32
        stat = at("stat", [P, 96], F32, t); t += 384
        zero = at("zero", [P, 8], F32, t); t += 32
        T2 = t
        R = at("R", [P, S], F32, t); t += 4 * KB
        SIG = at("SIG", [P, S], F32, t); t += 4 * KB
        TMP = at("TMP", [P, S], F32, t); t += 4 * KB
        GLU = at("GLU", [P, S], F32, t); t += 4 * KB
        glu = at("glu", [P, 2, S + 32], F32, H_AT)
        prod = at("prod", [P, 2, S], F32, H_AT + 8 * KB + 256)
        part = at("part", [P, 2, S], F32, H_AT + 16 * KB + 256)
        sum_sq = at("sum_sq", [P, S], F32, H_AT + 24 * KB + 256)
        sum_y = GLU
        masks = at("masks", [P, MASKS], BF16, T2)
        sg = at("sg", [P, 2, S], F32, T2 + 6 * KB)
        otok = at("otok", [P, QB * RES, P], F32, T2 + 14 * KB)
        small = at("small", [P, 16], F32, T2 + 18 * KB)
        lsum = at("lsum", [P, 2], F32, T2 + 18 * KB + 64)
        cos = at("cos", [P, S], F32, H_AT)
        sin = at("sin", [P, S], F32, H_AT + 4 * KB)
        raw_g = at("raw_g", [P, S], F32, H_AT + 8 * KB)
        sqr = at("sqr", [P, S], F32, H_AT + 12 * KB)
        r_k = at("r_k", [P, S], F32, H_AT + 16 * KB)
        shuf = at("shuf", [P, S], F32, H_AT + 20 * KB)
        roped = at("roped", [P, S], F32, H_AT + 24 * KB)
        gbuf = at("gbuf", [P, S], F32, H_AT + 24 * KB)
        obuf = at("obuf", [P, S], F32, H_AT + 28 * KB)
        diag = at("diag", [P, LAST, P], F32, U_AT)
        kpair = at("kpair", [P, 2, S], F32, U_AT)
        vpair = at("vpair", [P, 2, S], F32, U_AT + 8 * KB)
        vtok = at("vtok", [P, 2 * KT, P], F32, U_AT + 16 * KB)
        qbuf = at("qbuf", [P, 2, GROUPS, S], F32, U_AT + 24 * KB)
        prob = at("prob", [P, 2, NEAR + 2 * FAR], F32, U_AT + 48 * KB)
        probT = at("probT", [P, 2, NEAR + FAR], F32, U_AT + 57 * KB)
        assert 57 * KB + 2 * (NEAR + FAR) * 4 <= 64 * KB

        psum = ctx.enter_context(nc.psum_tensor("psum", [P, 8 * HALF], F32))
        G = [psum[:, 0:S], psum[:, S:2 * S]]
        CONV = [psum[:, 2 * S:3 * S], psum[:, 3 * S:4 * S]]
        E2 = psum[:, 2 * S:3 * S]
        STAT = psum[:, 3 * S:4 * S]
        SC = psum[:, 2 * HALF:5 * HALF]
        PT = psum[:, 5 * HALF:7 * HALF]
        MISC = psum[:, 7 * HALF:8 * HALF]

        def sem(name):
            return ctx.enter_context(nc.semaphore(name))

        w_raw_in = [sem(f"w_raw_in{s}") for s in range(2)]
        w_hi_done = sem("w_hi_done")
        w_hi_side = sem("w_hi_side")
        w_split = sem("w_split")
        zero_set = sem("zero_set")
        gemm_done = sem("gemm_done")
        c_vecs, c_x, c_misc, c_ones = sem("c_vecs"), sem("c_x"), sem("c_misc"), sem("c_ones")
        n_sq, n_log, n_root, n_tmp, n_hi, n_lo = (sem(s) for s in ("n_sq", "n_log", "n_root", "n_tmp", "n_hi", "n_lo"))
        stat0 = sem("stat0")
        sig_ready, glu_ready, conv_step, y_ready = (sem(s) for s in ("sig_ready", "glu_ready", "conv_step", "y_ready"))
        z_ready, z_stored, sq_ready, stat_ready = (sem(s) for s in ("z_ready", "z_stored", "sq_ready", "stat_ready"))
        sums_zero, part_first, prod_ready, part_add, sum_add, sq_add, x_back = (
            sem(s) for s in ("sums_zero", "part_first", "prod_ready", "part_add", "sum_add", "sq_add", "x_back"))
        diag_ready, taps_done, conv_even = sem("diag_ready"), sem("taps_done"), sem("conv_even")
        glu_pad, mean_copied, conv_odd = sem("glu_pad"), sem("mean_copied"), sem("conv_odd")
        ln_step, ln_log, ln_root = sem("ln_step"), sem("ln_log"), sem("ln_root")
        z_back = [sem("z_back0"), sem("z_back1")]
        y_cent, y_norm, y_silu, yz_ready, yz_hi, yz_lo = (sem(s) for s in ("y_cent", "y_norm", "y_silu", "yz_ready", "yz_hi", "yz_lo"))
        h_mix, h_sq, h_stat = sem("h_mix"), sem("h_sq"), sem("h_stat")
        p_in, p_hi, p_lo, proj_done, pp_ready = (sem(s) for s in ("p_in", "p_hi", "p_lo", "proj_done", "pp_ready"))
        gate_sig, gate_mul, h_gate, g_sq, g_stat = (sem(s) for s in ("gate_sig", "gate_mul", "h_gate", "g_sq", "g_stat"))
        v_ready, h_stored, rope_in = (sem(s) for s in ("v_ready", "h_stored", "rope_in"))
        v_stored = sem("v_stored")
        k_gain, k_sq, k_stat, k_log, k_root, k_chain, k_ready, k_stored = (
            sem(s) for s in ("k_gain", "k_sq", "k_stat", "k_log", "k_root", "k_chain", "k_ready", "k_stored"))
        q_gain, q_sq, q_stat, q_kept, q_log, q_root, q_chain, q_ready = (
            sem(s) for s in ("q_gain", "q_sq", "q_stat", "q_kept", "q_log", "q_root", "q_chain", "q_ready"))
        gate_exp, gate_raw, gate_chain, gate_ready = (
            sem(s) for s in ("gate_exp", "gate_raw", "gate_chain", "gate_ready"))
        kv_in = [sem("kv_in0"), sem("kv_in1")]
        mask_in_s = sem("mask_in_s")
        v_turned, v_tok = sem("v_turned"), sem("v_tok")
        sc_near, sc_ready, sc_max, m_chain, p_part, p_sum = (
            sem(s) for s in ("sc_near", "sc_ready", "sc_max", "m_chain", "p_part", "p_sum"))
        pt_ready, pt_copied, o_ready, l_chain, o_tok = (sem(s) for s in ("pt_ready", "pt_copied", "o_ready", "l_chain", "o_tok"))
        ot_ready, o_gated, o_stored = sem("ot_ready"), sem("o_gated"), sem("o_stored")
        o_back, h_back, h_rest, o_hi, o_lo = (sem(s) for s in ("o_back", "h_back", "h_rest", "o_hi", "o_lo"))
        out_done = sem("out_done")

        first_acc = (G[0], G[1], E2, G[0])
        sq_buf = (GLU, SIG)

        block = ctx.enter_context(nc.Block())

        @block.sync
        def _(sp):
            def load(n, s):
                sp.dma_start(W_raw[:, s, :], w_in[bass.ds(n * P, P), :]).then_inc(w_raw_in[s], 16)

            for s in range(2):
                load(s, s)
            with sp.Fori(1, BLOCKS // 2) as j:
                for s in range(2):
                    sp.wait_ge(w_raw_in[s], j * 16)
                    sp.wait_ge(w_split, j * 2 + (s - 1))
                    load(j * 2 + s, s)

        @block.gpsimd
        def _(pool):
            def split(n, j, s, reuse, before=0):
                pool.wait_ge(w_raw_in[s], (j + 1) * 16)
                if reuse:
                    pool.wait_ge(gemm_done, n - 1)
                pool.tensor_tensor(zero[:, 1:2], zero[:, 0:1], zero[:, 0:1], ALU.add)
                pool.tensor_copy(W_hi[:, s, :], W_raw[:, s, :]).then_inc(w_hi_done, 1)
                pool.wait_ge(w_hi_done, n + (1 - before))
                pool.tensor_tensor(W_lo[:, s, :], W_raw[:, s, :], W_hi[:, s, :].bitcast(F32),
                                   ALU.subtract).then_inc(w_split, 1)

            pool.memset(zero[:, :], 0.0).then_inc(zero_set, 1)
            pool.wait_ge(zero_set, 1)
            for s in range(2):
                split(s, 0, s, False)
            pool.memset(sum_y[:, :], 0.0).then_inc(sums_zero, 1)
            pool.wait_ge(n_lo, KT)
            pool.memset(sum_sq[:, :], 0.0).then_inc(sums_zero, 1)
            pool.wait_ge(sums_zero, 2)

            def add_products(c, par, lo, hi):
                for k in range(lo, hi):
                    pool.wait_ge(prod_ready, c * (SIDE - 1) + k)
                    if k == 1:
                        pool.wait_ge(part_first, c + 1)
                    else:
                        pool.wait_ge(part_add, c * (SIDE - 1) + (k - 1))
                    pool.tensor_tensor(part[:, par, :], part[:, par, :], prod[:, (k + par * (SIDE - 1)) % 2, :],
                                       ALU.add).then_inc(part_add, 1)

            def add_channel(c, first):
                pool.wait_ge(y_ready, c + 1)
                if not first:
                    pool.wait_ge(sum_add, c)
                pool.tensor_tensor(sum_y[:, :], sum_y[:, :], Y[:, c, :], ALU.add).then_inc(sum_add, 1)
                pool.wait_ge(sq_ready, c + 1)
                if not first:
                    pool.wait_ge(sq_add, c)
                pool.tensor_tensor(sum_sq[:, :], sum_sq[:, :], R[:, :], ALU.add).then_inc(sq_add, 1)

            def low(c, u, d):
                s = (3 * u + 2 + d) % 2
                pool.wait_ge(w_hi_side, c * 3 + (d + 1))
                pool.tensor_tensor(W_lo[:, s, :], W_raw[:, s, :], W_hi[:, s, :].bitcast(F32),
                                   ALU.subtract).then_inc(w_split, 1)

            def channel(c, u, stats, first_stat):
                low(c, u, 0)
                if not (isinstance(c, int) and c == 0):
                    add_products(c - 1, 1 - u, *STAGES[2])
                low(c, u, 1)
                add_products(c, u, *STAGES[0])
                low(c, u, 2)
                if stats:
                    add_channel(c - 2, first_stat)
                add_products(c, u, *STAGES[1])

            channel(0, 0, False, False)
            channel(1, 1, False, False)
            channel(2, 0, True, True)
            channel(3, 1, True, False)
            with pool.Fori(2, CT // 2) as i:
                for u in range(2):
                    channel(i * 2 + u, u, True, False)
            add_products(CT - 1, 1, *STAGES[2])
            add_channel(CT - 2, False)
            add_channel(CT - 1, False)

            def center(c):
                pool.tensor_tensor(Y[:, c, :], Y[:, c, :], SIG[:, :], ALU.subtract).then_inc(y_cent, 1)

            pool.wait_ge(mean_copied, 1)
            with pool.Fori(0, CT) as c:
                center(c)

            with pool.Fori((3 * CT + 2) // 2, BLOCKS // 2) as j:
                for s in range(2):
                    split(j * 2 + s, j, s, True, HI_SIDE)

        @block.tensor
        def _(pe):
            def block_gemm(n, slot, acc, hi, lo, tiles, start=True, stop=True, ready=None):
                pe.wait_ge(w_split, n + 1)
                last = None
                for i, (wk, xk) in enumerate(tiles):
                    if ready is not None:
                        pe.wait_ge(ready[0], ready[1] + i + 1)
                    cols = slice(wk * P, wk * P + P)
                    parts = ((W_hi, hi), (W_hi, lo), (W_lo, hi))
                    for j, (w, x) in enumerate(parts):
                        for h in range(2):
                            half = slice(h * HALF, h * HALF + HALF)
                            last = pe.matmul(acc[:, half], w[:, slot, cols], x[:, xk, half],
                                             start=start and i == 0 and j == 0,
                                             stop=stop and i == len(tiles) - 1 and j == 2)
                return last

            def block_pair(n, ready):
                pe.wait_ge(w_split, n + 2)
                for k in range(KT):
                    pe.wait_ge(n_lo, ready + k + 1)
                    for s in range(2):
                        last = block_gemm(n + s, s, G[s], U_hi, U_lo, [(k, k)], start=k == 0, stop=k == KT - 1)
                        if k == KT - 1:
                            last.then_inc(gemm_done, 1)

            full = [(k, k) for k in range(KT)]
            U_hi, U_lo = U[:, 0:KT, :], U[:, KT:2 * KT, :]
            Y_hi, Y_lo = YR[:, 0:KT, :], YR[:, KT:2 * KT, :]
            O_hi, O_lo = Y_lo, Y_hi

            def add_stat(lhsT, squares, acc, start, stop, signal):
                for h in range(2):
                    half = slice(h * HALF, h * HALF + HALF)
                    last = pe.matmul(acc[:, half], lhsT, squares[:, half], start=start, stop=stop,
                                     skip_group_check=True)
                if signal is not None:
                    last.then_inc(signal, 1)

            pe.wait_ge(c_ones, 3)
            for k in range(KT):
                pe.wait_ge(n_sq, k + 1)
                add_stat(ones_d[:, :], Y[:, k, :], STAT, k == 0, k == KT - 1, stat0)

            def abz(c, par, first):
                if not first:
                    pe.wait_ge(glu_ready, c)
                    block_gemm(c * 3, par, G[par], U_hi, U_lo, full).then_inc(gemm_done, 1)
                    pe.wait_ge(z_ready, c)
                    block_gemm(c * 3 + 1, 1 - par, G[1 - par], U_hi, U_lo, full).then_inc(gemm_done, 1)
                else:
                    block_pair(0, 0)
                pe.wait_ge(sig_ready, c + 1)
                block_gemm(c * 3 + 2, par, G[par], U_hi, U_lo, full).then_inc(gemm_done, 1)

            abz(0, 0, True)
            abz(1, 1, False)
            with pe.Fori(1, CT // 2) as i:
                for u in range(2):
                    abz(i * 2 + u, u, False)
            pe.wait_ge(glu_ready, CT)
            for t in range(LAST):
                pe.wait_ge(diag_ready, t + 1)
                for h in range(2):
                    j = TAPS - LAST + t + h * HALF
                    last = pe.matmul(G[0][:, h * HALF:h * HALF + HALF], diag[:, t, :], glu[:, 1, j:j + HALF],
                                     start=t == 0, stop=t == LAST - 1)
            last.then_inc(taps_done, 1)

            pe.wait_ge(y_ready, CT)
            pe.wait_ge(sum_add, CT)
            add_stat(ones_c[:, :], sum_y, STAT, True, True, stat_ready)
            pe.wait_ge(sq_add, CT)
            add_stat(ones_c[:, :], sum_sq, E2, True, True, stat_ready)

            def feature_stat(count, squares, signal, start, stop, ready):
                pe.wait_ge(ready, count)
                add_stat(ones_d[:, :], squares, STAT, start, stop, signal)

            lead_acc = (G[0], G[1], E2)

            def out_a_lead():
                for k in range(CT):
                    pe.wait_ge(yz_lo, k + 1)
                    for m in range(LEAD):
                        at_ = k * LEAD + m
                        n, cols = B_OUTA + at_ // KT, slice(at_ % KT * P, at_ % KT * P + P)
                        if at_ % KT == 0:
                            pe.wait_ge(w_split, n + 1)
                        for j, (w, x) in enumerate(((W_hi, U), (W_hi, YR), (W_lo, U))):
                            for h in range(2):
                                half = slice(h * HALF, h * HALF + HALF)
                                last = pe.matmul(lead_acc[m][:, half], w[:, n % 2, cols], x[:, k, half],
                                                 start=k == 0 and j == 0, stop=k == CT - 1 and j == 2)
                        if at_ % KT == KT - 1:
                            last.then_inc(gemm_done, 1)

            def out_a(m, par):
                pe.wait_ge(h_mix, m - (LEAD - 1) if m < LEAD + 2 else m - 1)
                block_gemm(m * 2 + B_OUTA, 0, G[par], U, YR, full, stop=False).then_inc(gemm_done, 1)
                block_gemm(m * 2 + (B_OUTA + 1), 1, G[par], U, YR, [(k, k + KT) for k in range(KT)],
                           start=False).then_inc(gemm_done, 1)

            def stream_stat(m, layer, start=False, stop=False):
                feature_stat(m + (layer * KT + 1), sq_buf[m % 2][:, :], h_stat, start, stop, h_sq)

            pe.wait_ge(z_ready, CT)
            out_a_lead()
            pe.wait_ge(y_norm, CT)
            counted = 0
            for m in range(LEAD, KT):
                out_a(m, (m - LEAD) % 2)
                for k in range(counted, min(counted + 2, m)):
                    stream_stat(k, 0, k == 0)
                counted = min(counted + 2, m)
            stream_stat(KT - 1, 0, stop=True)

            def ple(layer, b_proj, b_gate, with_stat):
                done, root = layer * KT, 8 * (1 if layer == 0 else 4)
                for m in range(KT):
                    if m < 2:
                        pe.wait_ge(h_mix, done + KT)
                    else:
                        pe.wait_ge(pp_ready, done + m - 1)
                    if m == 0:
                        pe.wait_ge(p_lo, (layer + 1) * PK)
                    last = block_gemm(b_proj + m // 4, m // 4, G[m % 2], YR[:, PK:2 * PK, :],
                                      YR[:, 2 * PK:3 * PK, :], [(m % 4 * PK + k, k) for k in range(PK)])
                    last.then_inc(proj_done, 1)
                    if m % 4 == 3:
                        pe.wait_ge(proj_done, done + m + 1)
                        pe.sem_inc(gemm_done, 1)
                def gate(m, par, lead):
                    if lead:
                        pe.wait_ge(pp_ready, done + KT - 1 + par)
                    else:
                        pe.wait_ge(gate_sig, m + (done - 1))
                    block_gemm(m + b_gate, par, G[par], U_hi, U_lo, full,
                               ready=(n_lo, root) if lead and par == 0 else None).then_inc(gemm_done, 1)

                def gate_stat(m, start, stop):
                    if with_stat:
                        feature_stat(m, GLU[:, :], g_stat, start, stop, g_sq)

                gate(0, 0, True)
                gate(1, 1, True)
                gate_stat(1, True, False)
                with pe.Fori(1, KT // 2) as i:
                    for u in range(2):
                        gate(i * 2 + u, u, False)
                        gate_stat(i * 2 + u, False, False)
                gate_stat(KT, False, True)

            ple(0, B_PROJ0, B_GATE0, True)

            def value(m, par):
                pe.wait_ge(v_ready, m - 1)
                block_gemm(m + B_V, par, G[par], U_hi, U_lo, full).then_inc(gemm_done, 1)

            pe.wait_ge(gate_sig, KT)
            block_pair(B_V, 16)
            with pe.Fori(1, KT // 2) as i:
                for u in range(2):
                    value(i * 2 + u, u)

            def key_stat(m):
                pe.wait_ge(k_sq, m)
                add_stat(blk[:, :], sqr[:, :], STAT, True, True, k_stat)

            def key(m, par, lead):
                if lead:
                    pe.wait_ge(v_ready, KT - 1 + par)
                else:
                    pe.wait_ge(k_sq, m - 1)
                block_gemm(m + B_K, par, G[par], U_hi, U_lo, full).then_inc(gemm_done, 1)

            pe.wait_ge(c_misc, 48)
            pe.wait_ge(c_ones, 5)
            key(0, 0, True)
            key(1, 1, True)
            key_stat(1)
            with pe.Fori(1, KT // 2) as i:
                for u in range(2):
                    key(i * 2 + u, u, False)
                    pe.wait_ge(k_root, i * 2 + (u - 1))
                    key_stat(i * 2 + u)
            pe.wait_ge(n_lo, 32)
            pe.wait_ge(k_sq, KT - 1)
            block_gemm(B_QG, 0, first_acc[0], Y_hi, Y_lo, full).then_inc(gemm_done, 1)
            pe.wait_ge(k_root, KT - 1)
            key_stat(KT)

            def project(pair, g, part):
                if part == 0:
                    if g:
                        pe.wait_ge(q_sq, pair * GROUPS + g)
                    elif not (isinstance(pair, int) and pair == 0):
                        pe.wait_ge(gate_raw, pair)
                tiles = [(k, k) for k in range(3 * part, min(3 * part + 3, KT))]
                last = block_gemm(pair * 4 + (B_QG + g), g % 2, G[0], Y_hi, Y_lo, tiles,
                                  start=part == 0, stop=part == 2)
                if part == 2:
                    last.then_inc(gemm_done, 1)

            def query_stats(pair, g):
                pe.wait_ge(q_sq, pair * GROUPS + (g + 1))
                for b in range(QB):
                    for r in range(RES):
                        col = (b * RES + r) * 8 + g
                        last = pe.matmul(MISC[:, col:col + 5:4],
                                         sqr[:, b * HALF + r:b * HALF + HALF:RES], hind[:, :],
                                         start=True, stop=True, skip_group_check=True)
                last.then_inc(q_stat, 1)

            def turn_values(pair, par, rnd):
                vt = vpair[:, par, :]
                bank = (PT[:, 0:HALF], PT[:, HALF:2 * HALF], MISC, PT[:, 0:HALF])[rnd]
                for k in range(4):
                    if rnd < 2:
                        src = vt[:, (rnd * 4 + k) * P:(rnd * 4 + k + 1) * P]
                    else:
                        src = vt[:, (rnd - 2) * HALF + k:(rnd - 2) * HALF + HALF:RES]
                    last = pe.transpose(bank[:, k * P:k * P + P], src, ident[:, :])
                last.then_inc(v_turned, 1)

            def scores(pair, par, s, seen):
                b, hh, r = STEPS[s]
                rows = slice(hh * HEAD, hh * HEAD + HEAD)
                kt = kpair[rows, par, :]
                q = [qbuf[rows, par, g, b * HALF + r:b * HALF + HALF:RES] for g in range(GROUPS)]
                n = FAR if b else SPAN
                k0 = b * HALF - (SPAN if b else 0)
                m0 = r * NEAR + (0 if b else SPAN)

                def piece(g, keys, col, mask, n):
                    pe.matmul(SC[:, col:col + n], q[g], keys, start=True, stop=False, skip_group_check=True)
                    return pe.matmul(SC[:, col:col + n], ident_b[:, :], masks[:, mask:mask + n],
                                     start=False, stop=True, skip_group_check=True)

                far_keys = kt[:, r:r + RES * n - (RES - 1):RES]
                if seen is not None:
                    pe.wait_ge(p_part, seen + 1)
                piece(0, kt[:, k0:k0 + HALF], 0, m0, HALF)
                if seen is not None:
                    pe.wait_ge(p_part, seen + 2)
                if b:
                    piece(0, kt[:, k0 + HALF:k0 + NEAR], HALF, m0 + HALF, SPAN)
                piece(1, far_keys, C1, RES * NEAR + FAR - n, n).then_inc(sc_near, 1)
                if seen is not None:
                    pe.wait_ge(p_part, seen + 3)
                last = piece(2, far_keys, C2, RES * NEAR + 2 * FAR - n, n)
                last.then_inc(sc_ready, 1)

            def key_tiles(b):
                return (NEAR if b else HALF) // P, (2 if b else 1)

            def turn_probs(s):
                b, hh, r = STEPS[s]
                nn, nf = key_tiles(b)
                cols = [k * P for k in range(nn)] + [C1 + k * P for k in range(nf)]
                for j, col in enumerate(cols):
                    last = pe.transpose(PT[:, j * P:j * P + P], prob[:, s % 2, col:col + P], ident[:, :])
                last.then_inc(pt_ready, 1)

            def weigh_values(s):
                b, hh, r = STEPS[s]
                nn, nf = key_tiles(b)
                k0 = (3 if b else 0)
                tiles = [k0 + k for k in range(nn)] + [KT + k * RES + r for k in range(nf)]
                for j, tile in enumerate(tiles):
                    last = pe.matmul(MISC[:, 0:HEAD], probT[:, s % 2, j * P:j * P + P],
                                     vtok[:, tile, hh * HEAD:hh * HEAD + HEAD],
                                     start=j == 0, stop=j == len(tiles) - 1)
                last.then_inc(o_ready, 1)

            def turn_output(pair, b):
                for r in range(RES):
                    last = pe.transpose(MISC[:, r:HALF:RES], otok[:, b * RES + r, :], ident[:, :])
                last.then_inc(ot_ready, 1)

            def out_b_part(k0, k1):
                last = block_gemm(B_OUTB, 0, G[0], O_hi, O_lo, [(k, k) for k in range(k0, k1)],
                                  start=k0 == 0, stop=k1 == KT, ready=(o_lo, k0))
                if k1 == KT:
                    last.then_inc(gemm_done, 1)

            def attend(pair, par, first, project_next):
                done = pair * 16
                for s in range(16):
                    if s == 0:
                        pe.wait_ge(kv_in[par], (pair + (2 - par)) * 16)
                        pe.wait_ge(q_ready, pair * GROUPS + GROUPS)
                    scores(pair, par, s, None if first and s == 0 else 3 * (done + s - 1))

                    if s == 2:
                        if not first:
                            pe.wait_ge(v_tok, pair * 4 + 3)
                            turn_output(pair - 1, 1)
                            pe.wait_ge(o_gated, pair * 2)
                        pe.wait_ge(v_tok, pair * 4 + 4)
                    if s >= 2 or not first:
                        pe.wait_ge(pt_copied, done + (s - 1))
                        if s - 2 > 0 or not first:
                            pe.wait_ge(o_tok, done + (s - 2))
                        if s == 11:
                            pe.wait_ge(o_gated, pair * 2 + 1)
                        if project_next and s in (6, 10, 14):
                            pe.wait_ge(q_kept, pair * GROUPS + (GROUPS + (s - 2) // 4))
                        weigh_values((s - 2) % 16)

                    if s == 1:
                        if not first:
                            pe.wait_ge(pt_copied, done)
                        turn_values(pair, par, 0)
                        turn_values(pair, par, 1)
                        if not first:
                            pe.wait_ge(o_tok, done)
                        turn_values(pair, par, 2)
                        if project_next:
                            project(pair + 1, 0, 0)
                        pe.wait_ge(v_tok, pair * 4 + 1)
                        turn_values(pair, par, 3)
                        pe.wait_ge(v_tok, pair * 4 + 4)
                    if s >= 1 or not first:
                        pe.wait_ge(p_sum, done + s)
                        if s > 1 or not first:
                            pe.wait_ge(pt_copied, done + (s - 1))
                        turn_probs((s - 1) % 16)

                    if s == 10:
                        pe.wait_ge(o_tok, done + 8)
                        pe.wait_ge(o_tok, done + 9)
                        turn_output(pair, 0)
                    if project_next and s % 4 and s != 1:
                        project(pair + 1, s // 4, s % 4 - 1)
                    if project_next and s in (5, 9, 13):
                        pe.wait_ge(o_tok, done + (s - 1))
                        query_stats(pair + 1, (s - 5) // 4)
                    if not project_next and s >= EARLY:
                        out_b_part(s - EARLY, s - EARLY + 1)

            def finish_attention(pair):
                done = pair * 16
                pe.wait_ge(pt_copied, done + 15)
                pe.wait_ge(o_tok, done + 14)
                weigh_values(14)
                pe.wait_ge(p_sum, done + 16)
                turn_probs(15)
                pe.wait_ge(pt_copied, done + 16)
                pe.wait_ge(o_tok, done + 15)
                weigh_values(15)
                out_b_part(16 - EARLY, KT - 1)
                pe.wait_ge(o_tok, done + 16)
                turn_output(pair, 1)

            pe.wait_ge(k_root, KT)
            for g in range(1, 4):
                if g == 3:
                    pe.wait_ge(q_sq, 1)
                block_gemm(B_QG + g, g % 2, first_acc[g], Y_hi, Y_lo, full).then_inc(gemm_done, 1)
                if g > 1:
                    pe.wait_ge(q_kept, g - 1)
                query_stats(0, g - 1)
            pe.wait_ge(mask_in_s, 16)

            attend(0, 0, True, True)
            attend(1, 1, False, True)
            with pe.Fori(1, PAIRS // 2 - 1) as i:
                for u in range(2):
                    attend(i * 2 + u, u, False, True)
            attend(PAIRS - 2, 0, False, True)
            attend(PAIRS - 1, 1, False, False)
            finish_attention(PAIRS - 1)

            out_b_part(KT - 1, KT)
            block_gemm(B_OUTB + 1, 1, G[1], O_hi, O_lo, full).then_inc(gemm_done, 1)
            stream_stat(0, 1, True)
            for m in range(2, KT):
                pe.wait_ge(h_mix, m + (KT - 1))
                block_gemm(m + B_OUTB, m % 2, G[m % 2], O_hi, O_lo, full).then_inc(gemm_done, 1)
                stream_stat(m - 1, 1)
            stream_stat(KT - 1, 1, stop=True)
            ple(1, B_PROJ1, B_GATE1, False)

        @block.scalar
        def _(act):
            act.dma_start(H[:, :, :], xT).then_inc(c_x, 16)
            act.dma_start(vecs[:, :], vecs_in).then_inc(c_vecs, 16)
            act.dma_start(blk[:, :], blk_in).then_inc(c_misc, 16)
            act.dma_start(hind[:, :], hind_in).then_inc(c_misc, 16)
            act.dma_start(ident[:, :], ident_in).then_inc(c_misc, 16)

            act.wait_ge(c_x, 16)
            with act.Fori(0, KT) as k:
                act.activation(Y[:, k, :], H[:, k, :], ACT.Square).then_inc(n_sq, 1)

            def inverse_root(logged, signal, n, src, dst, bias=0.0):
                act.activation(dst, src, ACT.Ln, bias=bias).then_inc(logged, 1)
                act.wait_ge(logged, n)
                act.activation(dst, dst, ACT.Exp, scale=-0.5).then_inc(signal, 1)

            def norm_root(n):
                inverse_root(n_log, n_root, n, STAT, R[:, :], eps_d[:, 0:1])

            def norm_hi(instance, dst):
                with act.Fori(0, KT // 2) as i:
                    for u, scratch in enumerate((TMP, SIG)):
                        act.wait_ge(n_tmp, i * 2 + (8 * instance + u + 1))
                        act.activation(dst[:, i * 2 + u, :], scratch[:, :], ACT.Copy).then_inc(n_hi, 1)

            act.wait_ge(stat0, KT)
            act.wait_ge(c_ones, 4)
            norm_root(1)
            norm_hi(0, U)

            def first_product(c, par, warm):
                act.wait_ge(glu_ready, c + 1)
                if warm:
                    act.wait_ge(conv_step, c * (MAIN - 1) - (2 * MAIN - 3))
                act.activation(part[:, par, :], glu[:, par, 0:S], ACT.Identity, scale=vec(c * TAPS + V_CW),
                               bias=vec(c + V_CB)).then_inc(part_first, 1)

            def side_products(c, par, lo, hi):
                for k in range(lo, hi):
                    if k > 2 or not (isinstance(c, int) and c == 0):
                        act.wait_ge(part_add, c * (SIDE - 1) + (k - 2))
                    act.activation(prod[:, (k + par * (SIDE - 1)) % 2, :], glu[:, par, k:k + S], ACT.Copy,
                                   scale=vec(c * TAPS + (V_CW + k))).then_inc(prod_ready, 1)

            def weights_hi(c, i, u, d):
                off = 3 * u + 2 + d
                act.wait_ge(w_raw_in[off % 2], (i * 3 + (off // 2 + 1)) * 16)
                act.wait_ge(gemm_done, c * 3 + (1 + d))
                act.activation(W_hi[:, off % 2, :], W_raw[:, off % 2, :], ACT.Copy).then_inc(w_hi_side, 1)

            def vec(col):
                return vecs[:, col:col + 1] if isinstance(col, int) else vecs[:, bass.ds(col, 1)]

            def abz(c, i, par, first, warm, last=False):
                act.wait_ge(gemm_done, c * 3 + 1)
                if not first:
                    act.wait_ge(glu_ready, c)
                act.activation(SIG[:, :], G[par], ACT.Sigmoid).then_inc(sig_ready, 1)
                weights_hi(c, i, par, 0)
                if not first:
                    side_products(c - 1, 1 - par, *STAGES[2])
                weights_hi(c, i, par, 1)
                first_product(c, par, warm)
                side_products(c, par, *STAGES[0])
                act.wait_ge(gemm_done, c * 3 + 3)
                if not first:
                    act.wait_ge(z_stored, c * 16)
                act.activation(TMP[:, :], G[par], ACT.Silu).then_inc(z_ready, 1)
                if last:
                    for t in range(LAST):
                        act.activation(diag[:, t, :], ident[:, :], ACT.Copy,
                                       scale=vec(c * TAPS + (V_CW + TAPS - LAST + t))).then_inc(diag_ready, 1)
                weights_hi(c, i, par, 2)
                act.wait_ge(z_ready, c + 1)
                act.dma_start(z_dram[bass.ds(c * P, P), :], TMP[:, :]).then_inc(z_stored, 16)
                if warm:
                    channel_square(c - 2, isinstance(c, int) and c == 2)
                side_products(c, par, *STAGES[1])

            def channel_square(c, first):
                act.wait_ge(y_ready, c + 1)
                if not first:
                    act.wait_ge(sq_add, c)
                act.activation(R[:, :], Y[:, c, :], ACT.Square).then_inc(sq_ready, 1)

            act.wait_ge(glu_pad, 1)
            abz(0, 0, 0, True, False)
            abz(1, 0, 1, False, False)
            abz(2, 1, 0, False, True)
            abz(3, 1, 1, False, True)
            with act.Fori(2, CT // 2 - 1) as i:
                for u in range(2):
                    abz(i * 2 + u, i, u, False, True)
            abz(CT - 2, CT // 2 - 1, 0, False, True)
            act.wait_ge(c_misc, 48)
            abz(CT - 1, CT // 2 - 1, 1, False, True, True)
            side_products(CT - 1, 1, *STAGES[2])
            channel_square(CT - 2, False)
            channel_square(CT - 1, False)

            act.wait_ge(z_stored, CT * 16)
            act.wait_ge(stat_ready, 1)
            act.activation(SIG[:, :], STAT, ACT.Copy).then_inc(mean_copied, 1)
            act.activation(TMP[:, :], STAT, ACT.Square).then_inc(mean_copied, 1)
            act.wait_ge(stat_ready, 2)
            act.dma_start(H[:, :, :], xT).then_inc(x_back, 16)
            act.wait_ge(ln_step, 2)
            inverse_root(ln_log, ln_root, 1, R[:, :], STAT)

            z_buf = (TMP, GLU)

            def z_load(c, par):
                act.dma_start(z_buf[par][:, :], z_dram[bass.ds(c * P, P), :]).then_inc(z_back[par], 16)

            z_load(0, 0)
            z_load(1, 1)

            def ln_silu(c):
                act.wait_ge(y_norm, c + 1)
                act.activation(Y[:, c, :], Y[:, c, :], ACT.Silu, scale=vec(c + V_LNG),
                               bias=vec(c + V_LNB)).then_inc(y_silu, 1)

            def ln_hi(c, par, more):
                act.wait_ge(yz_ready, c + 1)
                act.activation(U[:, c, :], Y[:, c, :], ACT.Copy).then_inc(yz_hi, 1)
                if more:
                    z_load(c + 2, par)

            ln_silu(0)
            with act.Fori(0, CT // 2 - 1) as i:
                for u in range(2):
                    ln_silu(i * 2 + (u + 1))
                    ln_hi(i * 2 + u, u, True)
            ln_silu(CT - 1)
            ln_hi(CT - 2, 0, False)
            ln_hi(CT - 1, 1, False)

            def gate_square(m, first):
                act.wait_ge(h_gate, m + 1)
                if not first:
                    act.wait_ge(g_stat, m)
                act.activation(GLU[:, :], H[:, m, :], ACT.Square).then_inc(g_sq, 1)

            def stream_squares(layer):
                for m in range(KT):
                    act.wait_ge(h_mix, layer * KT + m + 1)
                    if m > 1:
                        act.wait_ge(h_stat, layer * KT + m - 1)
                    act.activation(sq_buf[m % 2][:, :], H[:, m, :], ACT.Square).then_inc(h_sq, 1)

            def ple(layer, instance, with_stat):
                done = layer * KT
                act.wait_ge(gemm_done, (B_PROJ0, B_PROJ1)[layer])
                act.dma_start(Y[:, 0:PK, :], pT[:, layer, :, :]).then_inc(p_in, 16)
                act.wait_ge(p_in, (layer + 1) * 16)
                for k in range(PK):
                    act.activation(YR[:, PK + k, :], Y[:, k, :], ACT.Copy).then_inc(p_hi, 1)
                act.wait_ge(h_stat, done + KT)
                norm_root((2, 4)[layer])
                for m in range(KT):
                    act.wait_ge(n_tmp, 8 * instance + m + 1)
                    act.activation(U[:, m, :], (TMP, SIG)[m % 2][:, :], ACT.Copy).then_inc(n_hi, 1)
                    act.wait_ge(proj_done, done + m + 1)
                    act.activation(Y[:, KT + m, :], G[m % 2], ACT.Copy).then_inc(pp_ready, 1)

                def gate(m, par, first):
                    act.wait_ge(gemm_done, m + ((B_GATE0, B_GATE1)[layer] + 1))
                    if not first:
                        act.wait_ge(gate_mul, m + done)
                    act.activation(SIG[:, :], G[par], ACT.Sigmoid).then_inc(gate_sig, 1)

                def square(m, first):
                    if with_stat:
                        gate_square(m, first)
                    else:
                        act.wait_ge(h_gate, m + (done + 1))
                        act.dma_start(out[:, m, :] if isinstance(m, int) else out[:, bass.ds(m, 1), :],
                                      H[:, m, :] if isinstance(m, int) else H[:, bass.ds(m, 1), :]).then_inc(out_done, 16)

                gate(0, 0, True)
                square(0, True)
                gate(1, 1, False)
                square(1, False)
                with act.Fori(1, KT // 2) as i:
                    for u in range(2):
                        gate(i * 2 + u, u, False)
                        square(i * 2 + u, False)

            stream_squares(0)
            ple(0, 1, True)

            act.wait_ge(g_stat, KT)
            norm_root(3)
            norm_hi(2, U)

            def value(m, first=False):
                act.wait_ge(gemm_done, m + (B_V + 1))
                if not first:
                    act.wait_ge(v_stored, m * 16)
                act.activation(GLU[:, :], G[m % 2], ACT.Copy).then_inc(v_ready, 1)
                act.wait_ge(v_ready, m + 1)
                act.dma_start(v_dram[bass.ds(m * P, P), :], GLU[:, :]).then_inc(v_stored, 16)

            for m in range(KT // 2):
                value(m, m == 0)
                for k in range(2 * m, 2 * m + 2):
                    act.wait_ge(n_tmp, 24 + k + 1)
                    act.activation(YR[:, k, :], (TMP, SIG)[k % 2][:, :], ACT.Copy).then_inc(n_hi, 1)
            act.wait_ge(n_lo, 32)
            act.dma_start(h_dram, H[:, :, :].rearrange("p k s -> p (k s)")).then_inc(h_stored, 16)
            for m in range(KT // 2, KT):
                value(m)

            act.wait_ge(h_stored, 16)
            act.dma_start(cos[:, :], cs_in[0]).then_inc(rope_in, 16)
            act.dma_start(sin[:, :], cs_in[1]).then_inc(rope_in, 16)

            def key(m, par, first):
                act.wait_ge(gemm_done, m + (B_K + 1))
                if not first:
                    act.wait_ge(k_chain, m * 4 - 3)
                act.activation(raw_g[:, :], G[par], ACT.Copy, scale=vecs[:, V_KG:V_KG + 1]).then_inc(k_gain, 1)
                if not first:
                    act.wait_ge(k_stat, m)
                act.activation(sqr[:, :], G[par], ACT.Square).then_inc(k_sq, 1)
                act.wait_ge(k_stat, m + 1)
                if not first:
                    act.wait_ge(k_chain, m * 4 - 3)
                inverse_root(k_log, k_root, m + 1, STAT, r_k[:, :], eps_d[:, 0:1])

            def key_store(m):
                act.wait_ge(k_ready, m + 1)
                act.dma_start(k_dram[bass.ds(m * P, P), :], roped[:, :]).then_inc(k_stored, 16)

            key(0, 0, True)
            key(1, 1, False)
            key_store(0)
            with act.Fori(1, KT // 2) as i:
                for u in range(2):
                    key(i * 2 + u, u, False)
                    key_store(i * 2 + (u - 1))
            key_store(KT - 1)

            act.wait_ge(v_stored, KT * 16)
            act.wait_ge(k_stored, KT * 16)
            act.wait_ge(gemm_done, B_QG)
            act.dma_start(masks[:, :], mask_in).then_inc(mask_in_s, 16)

            def load_pair(pair, par):
                act.dma_start(kpair[:, par, :], k_dram[bass.ds(pair * P, P), :]).then_inc(kv_in[par], 16)
                act.dma_start(vpair[:, par, :], v_dram[bass.ds(pair * P, P), :]).then_inc(kv_in[par], 16)

            load_pair(0, 0)
            load_pair(1, 1)

            def query(pair, g, first, acc=G[0]):
                act.wait_ge(gemm_done, pair * 4 + (B_QG + g + 1))
                if not first:
                    act.wait_ge(q_chain, pair * 9 + (3 * g - 1))
                    act.wait_ge(q_stat, pair * GROUPS + g)
                act.activation(raw_g[:, :], acc, ACT.Copy, scale=vecs[:, V_QG + g:V_QG + g + 1]).then_inc(q_gain, 1)
                act.activation(sqr[:, :], acc, ACT.Square).then_inc(q_sq, 1)

            def query_root(pair, par):
                act.wait_ge(q_kept, pair * GROUPS + GROUPS)
                cols = stat[:, par * 48:par * 48 + 48]
                inverse_root(q_log, q_root, pair + 1, cols, cols, eps_d[:, 1:2])

            def gate_part(pair, par):
                act.wait_ge(gemm_done, pair * 4 + (B_QG + 4))
                act.activation(sg[:, par, :], G[0], ACT.Exp, scale=-1.0).then_inc(gate_exp, 1)
                act.activation(gbuf[:, :], G[0], ACT.Copy).then_inc(gate_raw, 1)

            def exps(pair, par, s):
                b, hh, r = STEPS[s]
                act.wait_ge(sc_max, pair * 16 + (s + 1))
                nn, nf = (NEAR, FAR) if b else (HALF, SPAN)
                tile = b * RES + r
                for g, col, n in ((0, 0, nn), (1, C1, nf), (2, C2, nf)):
                    at_ = par * 48 + tile * 6 + hh * 3 + g
                    dst = col if g < 2 else C1 + FAR
                    act.activation(prob[:, s % 2, dst:dst + n], SC[:, col:col + n], ACT.Exp,
                                   bias=small[:, 4:5], scale=stat[:, at_:at_ + 1],
                                   accum_out=small[:, 8 + g:9 + g]).then_inc(p_part, 1)

            def copy_turned(pair, s):
                b, hh, r = STEPS[s]
                n = (NEAR + FAR) if b else (HALF + SPAN)
                act.wait_ge(pt_ready, pair * 16 + (s + 1))
                act.activation(probT[:, s % 2, 0:n], PT[:, 0:n], ACT.Copy).then_inc(pt_copied, 1)

            for g in range(GROUPS):
                query(0, g, g == 0, first_acc[g])
            query_root(0, 0)
            act.wait_ge(mask_in_s, 16)

            def attend(pair, par, first, project_next, load_next):
                for s in range(16):
                    exps(pair, par, s)
                    if s > 0:
                        copy_turned(pair, s - 1)
                    elif not first:
                        copy_turned(pair - 1, 15)
                    if s == 0:
                        gate_part(pair, par)
                    if project_next and s in (4, 8, 12):
                        query(pair + 1, s // 4 - 1, False)
                    if project_next and s == 14:
                        query_root(pair + 1, 1 - par)
                    if s == 5 and not first:
                        act.wait_ge(o_gated, pair * 2)
                        act.dma_start(o_dram[bass.ds((pair - 1) * P, P), :], obuf[:, :]).then_inc(o_stored, 16)
                    if not project_next and s == 7:
                        act.wait_ge(o_stored, pair * 16)
                        act.wait_ge(gemm_done, B_OUTB)
                        act.wait_ge(q_ready, PAIRS * GROUPS)
                        for k in range(KT - 1):
                            act.dma_start(Y[:, k, :], o_dram[k * P:k * P + P, :]).then_inc(o_back, 16)
                        act.dma_start(H[:, 0:GONE, :].rearrange("p k s -> p (k s)"),
                                      h_dram[:, 0:GONE * S]).then_inc(h_back, 16)
                    if not project_next and s >= SPLIT:
                        if s == SPLIT:
                            act.wait_ge(o_back, (KT - 1) * 16)
                        for k in early_tiles(s):
                            act.activation(YR[:, KT + k, :], Y[:, k, :], ACT.Copy).then_inc(o_hi, 1)
                    if s == 5 and not first:
                        if load_next:
                            load_pair(pair + 1, 1 - par)

            def finish_attention(pair):
                copy_turned(pair, 15)
                act.wait_ge(o_gated, pair * 2 + 2)
                act.activation(YR[:, 2 * KT - 1, :], obuf[:, :], ACT.Copy).then_inc(o_hi, 1)
                act.wait_ge(o_lo, KT)
                act.dma_start(H[:, GONE:KT, :].rearrange("p k s -> p (k s)"),
                              h_dram[:, GONE * S:KT * S]).then_inc(h_rest, 16)

            attend(0, 0, True, True, True)
            attend(1, 1, False, True, True)
            with act.Fori(1, PAIRS // 2 - 1) as i:
                for u in range(2):
                    attend(i * 2 + u, u, False, True, True)
            attend(PAIRS - 2, 0, False, True, True)
            attend(PAIRS - 1, 1, False, False, False)
            finish_attention(PAIRS - 1)

            stream_squares(1)
            ple(1, 4, False)
            act.wait_ge(out_done, KT * 16)

        @block.vector
        def _(dve):
            dve.memset(ones_d[:, :], 1.0 / D).then_inc(c_ones, 1)
            dve.memset(ones_c[:, :], 1.0 / CH).then_inc(c_ones, 1)
            dve.memset(eps_d[:, 0:1], EPS).then_inc(c_ones, 1)
            dve.memset(eps_d[:, 1:2], EPS * HEAD).then_inc(c_ones, 1)
            dve.wait_ge(c_vecs, 16)
            dve.wait_ge(c_ones, 4)

            def vec(col):
                return vecs[:, col:col + 1] if isinstance(col, int) else vecs[:, bass.ds(col, 1)]

            def norm(instance, roots, gain, hi, lo):
                dve.wait_ge(n_root, roots)
                base_n = 8 * instance
                if instance:
                    dve.wait_ge(n_lo, base_n)

                def scaled(k, scratch):
                    dve.scalar_tensor_tensor(out=scratch[:, :], in0=H[:, k, :], scalar=vec(k + gain), in1=R[:, :],
                                             op0=ALU.mult, op1=ALU.mult).then_inc(n_tmp, 1)

                def low(k, scratch):
                    dve.wait_ge(n_hi, k + (base_n + 1))
                    dve.tensor_tensor(lo[:, k, :], scratch[:, :], hi[:, k, :].bitcast(F32),
                                      ALU.subtract).then_inc(n_lo, 1)

                scaled(0, TMP)
                scaled(1, SIG)
                with dve.Fori(0, KT // 2 - 1) as i:
                    for u, scratch in enumerate((TMP, SIG)):
                        low(i * 2 + u, scratch)
                        dve.wait_ge(n_lo, i * 2 + (u + base_n + 1))
                        scaled(i * 2 + (u + 2), scratch)
                low(KT - 2, TMP)
                low(KT - 1, SIG)

            dve.wait_ge(c_x, 16)
            norm(0, 1, V_NORM, U[:, 0:KT, :], U[:, KT:2 * KT, :])

            dve.wait_ge(n_lo, KT)
            dve.memset(glu[:, :, 0:PAD], 0.0).then_inc(glu_pad, 1)
            dve.wait_ge(glu_pad, 1)

            def gate_linear(c, par, warm):
                dve.wait_ge(gemm_done, c * 3 + 2)
                dve.wait_ge(sig_ready, c + 1)
                if warm:
                    dve.wait_ge(y_ready, c - 1)
                    dve.wait_ge(prod_ready, c * (SIDE - 1) - (SIDE - 1))
                dve.tensor_tensor(glu[:, par, PAD:PAD + S], G[1 - par], SIG[:, :], ALU.mult).then_inc(glu_ready, 1)

            def convolve(c, par, first, main=MAIN):
                dve.wait_ge(glu_ready, c + 1)
                dve.wait_ge(part_add, c * (SIDE - 1) + (SIDE - 1))
                if not first:
                    dve.wait_ge(y_ready, c)
                for t in range(main):
                    j = SIDE + t
                    x, w, acc = glu[:, par, j:j + S], vec(c * TAPS + (V_CW + j)), CONV[t % 2]
                    if t >= 2:
                        dve.wait_ge(conv_step, c * (MAIN - 1) + (t - 1))
                    if t == 1:
                        dve.tensor_scalar(acc, x, w, None, ALU.mult).then_inc(conv_step, 1)
                    elif t == main - 1:
                        dve.scalar_tensor_tensor(out=Y[:, c, :], in0=x, scalar=w, in1=acc, op0=ALU.mult,
                                                 op1=ALU.add).then_inc(conv_odd, 1)
                    else:
                        dve.scalar_tensor_tensor(out=acc, in0=x, scalar=w, in1=acc if t else part[:, par, :],
                                                 op0=ALU.mult, op1=ALU.add).then_inc(conv_step, 1)
                dve.wait_ge(conv_odd, c + 1)
                dve.wait_ge(conv_step, c * (MAIN - 1) + (main - 1))
                dve.tensor_tensor(Y[:, c, :], Y[:, c, :], CONV[0], ALU.add).then_inc(
                    y_ready if main == MAIN else conv_even, 1)

            gate_linear(0, 0, False)
            gate_linear(1, 1, False)
            convolve(0, 0, True)
            gate_linear(2, 0, True)
            convolve(1, 1, False)
            with dve.Fori(1, CT // 2 - 1) as i:
                for u in range(2):
                    gate_linear(i * 2 + (u + 1), 1 - u, True)
                    convolve(i * 2 + u, u, False)
            gate_linear(CT - 1, 1, True)
            convolve(CT - 2, 0, False)
            convolve(CT - 1, 1, False, MAIN - LAST)
            dve.wait_ge(conv_even, 1)
            dve.wait_ge(taps_done, 1)
            dve.tensor_tensor(Y[:, CT - 1, :], Y[:, CT - 1, :], G[0], ALU.add).then_inc(y_ready, 1)

            dve.wait_ge(stat_ready, 2)
            dve.wait_ge(mean_copied, 2)
            dve.tensor_tensor(R[:, :], E2, TMP[:, :], ALU.subtract).then_inc(ln_step, 1)
            dve.wait_ge(ln_step, 1)
            dve.tensor_scalar(R[:, :], R[:, :], 0.0, EPS, ALU.max, ALU.add).then_inc(ln_step, 1)
            dve.wait_ge(ln_root, 1)

            z_buf = (TMP, GLU)

            def ln_norm(c):
                dve.wait_ge(y_cent, c + 1)
                dve.tensor_tensor(Y[:, c, :], Y[:, c, :], STAT, ALU.mult).then_inc(y_norm, 1)

            def ln_gate(c, j, par):
                dve.wait_ge(y_silu, c + 1)
                dve.wait_ge(z_back[par], j * 16 + 16)
                dve.tensor_tensor(Y[:, c, :], Y[:, c, :], z_buf[par][:, :], ALU.mult).then_inc(yz_ready, 1)

            def ln_low(c):
                dve.wait_ge(yz_hi, c + 1)
                dve.tensor_tensor(YR[:, c, :], Y[:, c, :], U[:, c, :].bitcast(F32), ALU.subtract).then_inc(yz_lo, 1)

            ln_norm(0)
            ln_norm(1)
            ln_gate(0, 0, 0)
            ln_norm(2)
            ln_gate(1, 0, 1)
            ln_low(0)
            with dve.Fori(1, CT // 2 - 1) as i:
                for u in range(2):
                    ln_norm(i * 2 + (u + 1))
                    ln_gate(i * 2 + u, i, u)
                    ln_low(i * 2 + (u - 1))
            ln_norm(CT - 1)
            ln_gate(CT - 2, CT // 2 - 1, 0)
            ln_low(CT - 3)
            ln_gate(CT - 1, CT // 2 - 1, 1)
            ln_low(CT - 2)
            ln_low(CT - 1)

            def residual(layer):
                if layer == 0:
                    dve.wait_ge(x_back, 16)
                for m in range(KT):
                    if layer == 0:
                        done = B_OUTA + max(2 * m + 2, 2 * LEAD)
                        acc = lead_acc[m] if m < LEAD else G[(m - LEAD) % 2]
                    else:
                        done, acc = B_OUTB + m + 1, G[m % 2]
                    dve.wait_ge(gemm_done, done)
                    dve.tensor_tensor(H[:, m, :], H[:, m, :], acc, ALU.add).then_inc(h_mix, 1)

            def ple(layer, instance):
                done = layer * KT
                for k in range(PK):
                    dve.wait_ge(p_hi, layer * PK + k + 1)
                    dve.tensor_tensor(YR[:, 2 * PK + k, :], Y[:, k, :], YR[:, PK + k, :].bitcast(F32),
                                      ALU.subtract).then_inc(p_lo, 1)
                norm(instance, (2, 4)[layer], V_PLE + layer * KT, U[:, 0:KT, :], U[:, KT:2 * KT, :])
                def gate(m, first):
                    dve.wait_ge(gate_sig, m + (done + 1))
                    if not first:
                        dve.wait_ge(h_gate, m + done)
                    dve.tensor_tensor(TMP[:, :], SIG[:, :], Y[:, m + KT, :], ALU.mult).then_inc(gate_mul, 1)
                    dve.wait_ge(gate_mul, m + (done + 1))
                    dve.tensor_tensor(H[:, m, :], H[:, m, :], TMP[:, :], ALU.add).then_inc(h_gate, 1)

                gate(0, True)
                with dve.Fori(1, KT) as m:
                    gate(m, False)

            lead_acc = (G[0], G[1], E2)
            residual(0)
            ple(0, 1)
            norm(2, 3, V_KV, U[:, 0:KT, :], U[:, KT:2 * KT, :])
            norm(3, 3, V_NORM + KT, YR[:, 0:KT, :], YR[:, KT:2 * KT, :])

            turn = list(range(ROPE // 2, ROPE)) + list(range(ROPE // 2)) + list(range(ROPE, 32))

            def key(m, first):
                dve.wait_ge(k_root, m + 1)
                dve.wait_ge(k_gain, m + 1)
                if not first:
                    dve.wait_ge(k_ready, m)
                dve.tensor_tensor(raw_g2[:, :], raw_g[:, :], r_k[:, :], ALU.mult).then_inc(k_chain, 1)
                if not first:
                    dve.wait_ge(k_stored, m * 16)
                dve.wait_ge(k_chain, m * 4 + 1)
                dve.tensor_tensor(roped[:, :], raw_g2[:, :], cos[:, :], ALU.mult).then_inc(k_chain, 1)
                dve.stream_shuffle(shuf[:, :], raw_g2[:, :], turn).then_inc(k_chain, 1)
                dve.wait_ge(k_chain, m * 4 + 3)
                dve.tensor_tensor(shuf[:, :], shuf[:, :], sin[:, :], ALU.mult).then_inc(k_chain, 1)
                dve.wait_ge(k_chain, m * 4 + 4)
                dve.tensor_tensor(roped[:, :], roped[:, :], shuf[:, :], ALU.add).then_inc(k_ready, 1)

            raw_g2 = obuf
            dve.wait_ge(c_misc, 48)
            dve.tensor_copy(ident_b[:, :], ident[:, :]).then_inc(c_ones, 1)
            dve.wait_ge(rope_in, 32)
            key(0, True)
            with dve.Fori(1, KT) as m:
                key(m, False)

            def query(pair, par, g, part, first):
                q = qbuf[:, par, g, :]
                if part == 0:
                    dve.wait_ge(q_gain, pair * GROUPS + (g + 1))
                    if not first:
                        dve.wait_ge(q_ready, pair * GROUPS + g)
                    dve.tensor_tensor(q, raw_g[:, :], cos[:, :], ALU.mult).then_inc(q_chain, 1)
                elif part == 1:
                    dve.stream_shuffle(shuf[:, :], raw_g[:, :], turn).then_inc(q_chain, 1)
                elif part == 2:
                    dve.wait_ge(q_chain, pair * 9 + (3 * g + 2))
                    dve.tensor_tensor(shuf[:, :], shuf[:, :], sin[:, :], ALU.mult).then_inc(q_chain, 1)
                else:
                    dve.wait_ge(q_chain, pair * 9 + (3 * g + 3))
                    dve.tensor_tensor(q, q, shuf[:, :], ALU.add).then_inc(q_ready, 1)

            def keep_stats(pair, par, g):
                dve.wait_ge(q_stat, pair * GROUPS + (g + 1))
                cols = stat[:, par * 48:par * 48 + 48].rearrange("p (t h g) -> p t h g", h=2, g=GROUPS)
                src = MISC[:, 0:64].rearrange("p (t h g) -> p t h g", h=2, g=4)
                dve.tensor_copy(cols[:, :, :, g], src[:, :, :, g]).then_inc(q_kept, 1)

            def gate_rest(pair, par, part):
                if part == 0:
                    dve.wait_ge(gate_exp, pair + 1)
                    dve.tensor_scalar(sg[:, par, :], sg[:, par, :], 1.0, None, ALU.add).then_inc(gate_chain, 1)
                elif part < 5:
                    quarter = slice((part - 1) * FAR, part * FAR)
                    dve.wait_ge(gate_chain, pair * 5 + 1)
                    dve.reciprocal(sg[:, par, quarter], sg[:, par, quarter]).then_inc(gate_chain, 1)
                else:
                    dve.wait_ge(gate_chain, pair * 5 + 5)
                    dve.wait_ge(gate_raw, pair + 1)
                    dve.tensor_tensor(sg[:, par, :], gbuf[:, :], sg[:, par, :], ALU.mult).then_inc(gate_ready, 1)

            def values(pair, rnd):
                dve.wait_ge(v_turned, pair * 4 + (rnd + 1))
                bank = (PT[:, 0:HALF], PT[:, HALF:2 * HALF], MISC, PT[:, 0:HALF])[rnd]
                dve.tensor_copy(vtok[:, 4 * rnd:4 * rnd + 4, :].rearrange("p t n -> p (t n)"), bank).then_inc(v_tok, 1)

            def maxima(pair, par, s, first):
                b, hh, r = STEPS[s]
                dve.wait_ge(sc_near, pair * 16 + (s + 1))
                if s > 0 or not first:
                    dve.wait_ge(p_part, (pair * 16 + s) * 3)
                nn, nf = (NEAR, FAR) if b else (HALF, SPAN)
                dve.tensor_reduce(small[:, 0:1], SC[:, 0:nn], AX.X, ALU.max).then_inc(m_chain, 1)
                dve.wait_ge(sc_ready, pair * 16 + (s + 1))
                far = SC[:, C1:C1 + 2 * (C2 - C1)].rearrange("p (g n) -> p g n", g=2)[:, :, 0:nf]
                dve.tensor_reduce(small[:, 1:3], far, AX.X, ALU.max).then_inc(m_chain, 1)
                dve.wait_ge(m_chain, pair * 48 + (3 * s + 2))
                at_ = par * 48 + (b * RES + r) * 6 + hh * 3
                dve.tensor_tensor(small[:, 0:3], small[:, 0:3], stat[:, at_:at_ + 3], ALU.mult).then_inc(m_chain, 1)
                dve.wait_ge(m_chain, pair * 48 + (3 * s + 3))
                dve.tensor_reduce(small[:, 4:5], small[:, 0:3], AX.X, ALU.max, negate=True).then_inc(sc_max, 1)

            def add_far(pair, s, first):
                b, hh, r = STEPS[s]
                nf = FAR if b else SPAN
                dve.wait_ge(p_part, (pair * 16 + (s + 1)) * 3)
                if s > 1 or not first:
                    dve.wait_ge(o_tok, pair * 16 + (s - 1))
                dve.tensor_reduce(lsum[:, s % 2:s % 2 + 1], small[:, 8:11], AX.X, ALU.add).then_inc(l_chain, 1)
                dve.tensor_tensor(prob[:, s % 2, C1:C1 + nf], prob[:, s % 2, C1:C1 + nf],
                                  prob[:, s % 2, C1 + FAR:C1 + FAR + nf], ALU.add).then_inc(p_sum, 1)
                dve.wait_ge(l_chain, pair * 32 + (2 * s + 1))
                dve.reciprocal(lsum[:, s % 2:s % 2 + 1], lsum[:, s % 2:s % 2 + 1]).then_inc(l_chain, 1)

            def output(pair, s):
                b, hh, r = STEPS[s]
                dve.wait_ge(o_ready, pair * 16 + (s + 1))
                dve.wait_ge(l_chain, pair * 32 + (2 * s + 2))
                dve.tensor_scalar(otok[:, b * RES + r, hh * HEAD:hh * HEAD + HEAD], MISC[:, 0:HEAD],
                                  lsum[:, s % 2:s % 2 + 1], None, ALU.mult).then_inc(o_tok, 1)

            def gated(pair, par, b, first):
                dve.wait_ge(ot_ready, pair * 2 + (b + 1))
                if b == 0 and not first:
                    dve.wait_ge(o_stored, pair * 16)
                dve.wait_ge(gate_ready, pair + 1)
                half = slice(b * HALF, b * HALF + HALF)
                dve.tensor_tensor(obuf[:, half], MISC, sg[:, par, half], ALU.mult).then_inc(o_gated, 1)

            def output_low(k, src):
                dve.wait_ge(o_hi, k + 1)
                dve.tensor_tensor(YR[:, k, :], src, YR[:, KT + k, :].bitcast(F32), ALU.subtract).then_inc(o_lo, 1)

            dve.wait_ge(k_stored, KT * 16)
            for g in range(GROUPS):
                for q_part in range(4):
                    query(0, 0, g, q_part, g == 0)
                keep_stats(0, 0, g)

            def attend(pair, par, first, project_next):
                dve.wait_ge(q_root, pair + 1)
                for s in range(16):
                    maxima(pair, par, s, first)
                    if s == 2 and not first:
                        gated(pair - 1, 1 - par, 1, False)
                    if s >= 2:
                        output(pair, s - 2)
                    elif not first:
                        output(pair - 1, 14 + s)
                    if s == 1:
                        for rnd in range(3):
                            values(pair, rnd)
                    add_far(pair, s, first)
                    if s == 0:
                        gate_rest(pair, par, 0)
                    if s == 1:
                        values(pair, 3)
                    if 2 <= s < 7:
                        gate_rest(pair, par, s - 1)
                    if not project_next and s >= SPLIT:
                        for k in early_tiles(s):
                            output_low(k, Y[:, k, :])
                    if s == 10:
                        gated(pair, par, 0, first)
                    if project_next and s >= 4:
                        query(pair + 1, 1 - par, s // 4 - 1, s % 4, False)
                    if project_next and s in (5, 9, 13):
                        keep_stats(pair + 1, 1 - par, (s - 5) // 4)

            def finish_attention(pair, par):
                output(pair, 14)
                output(pair, 15)
                gated(pair, par, 1, False)
                output_low(KT - 1, obuf[:, :])

            attend(0, 0, True, True)
            attend(1, 1, False, True)
            with dve.Fori(1, PAIRS // 2 - 1) as i:
                for u in range(2):
                    attend(i * 2 + u, u, False, True)
            attend(PAIRS - 2, 0, False, True)
            attend(PAIRS - 1, 1, False, False)
            finish_attention(PAIRS - 1, 1)

            dve.wait_ge(h_back, 16)
            dve.wait_ge(h_rest, 16)
            residual(1)
            ple(1, 4)


def kernel(x, p, norm_g, w_in_a, conv_w, conv_b, ln_g, ln_b, w_out_a, kv_norm_g, w_kv, k_norm_g,
           w_in_b, q_norm_g, w_out_b, ple_norm_g, w_ple_gate, w_ple_proj):
    import ml_dtypes
    import concourse.bacc as bacc
    from concourse.bass_utils import run_bass_kernel_spmd

    f = np.float32

    def cols(w, n0):
        return w[:, n0:n0 + P].reshape(-1, P, P).transpose(1, 0, 2).reshape(P, -1)

    def proj_blocks(w):
        return [np.concatenate([cols(w, (4 * j + m) * P) for m in range(4)], axis=1) for j in range(2)]

    x, p, norm_g, w_in_a, conv_w, conv_b, ln_g, ln_b, w_out_a, kv_norm_g, w_kv, k_norm_g, w_in_b, \
        q_norm_g, w_out_b, ple_norm_g, w_ple_gate, w_ple_proj = (
            np.asarray(a) for a in (x, p, norm_g, w_in_a, conv_w, conv_b, ln_g, ln_b, w_out_a, kv_norm_g, w_kv,
                                    k_norm_g, w_in_b, q_norm_g, w_out_b, ple_norm_g, w_ple_gate, w_ple_proj))
    wa, woa, wb, wob = w_in_a[0], w_out_a[0], w_in_b[0], w_out_b[0]
    blocks = []
    for c in range(CT):
        blocks += [cols(wa, part * CH + c * P) for part in (1, 0, 2)]
    lead = woa[:, 0:LEAD * P].reshape(CT, P, LEAD, P).transpose(1, 0, 2, 3).reshape(P, 2 * LEAD, KT * P)
    blocks += [lead[:, j] for j in range(2 * LEAD)]
    for m in range(LEAD, KT):
        blocks += [cols(woa[0:D], m * P), cols(woa[D:CH], m * P)]
    blocks += proj_blocks(w_ple_proj[0])
    blocks += [cols(w_ple_gate[0], m * P) for m in range(KT)]
    blocks += [cols(w_kv, D + m * P) for m in range(KT)]
    blocks += [cols(w_kv, m * P) for m in range(KT)]
    for i in range(PAIRS):
        blocks += [cols(wb, g * D + i * P) for g in range(4)]
    blocks += [cols(wob, m * P) for m in range(KT)]
    blocks += proj_blocks(w_ple_proj[1])
    blocks += [cols(w_ple_gate[1], m * P) for m in range(KT)]
    w_all = np.concatenate(blocks, axis=0)

    def tiles(v):
        return v.reshape(-1, P).T

    vecs = np.concatenate([
        tiles(norm_g), tiles(ple_norm_g), tiles(kv_norm_g), tiles(conv_b), tiles(ln_g), tiles(ln_b),
        np.tile(k_norm_g, 2)[:, None], np.tile(q_norm_g[0], (1, 2)).T,
        conv_w[0].T.reshape(CT, P, TAPS).transpose(1, 0, 2).reshape(P, CT * TAPS)], axis=1)

    half = ROPE // 2
    inv = f(500000.0) ** (-np.arange(half, dtype=f) * f(2.0 / ROPE))
    ang = np.arange(S, dtype=f)[:, None] * inv[None, :]
    cs = np.zeros((2, P, S), f)
    cs[0] = 1.0
    for head in range(2):
        for part in range(2):
            rows = slice(head * HEAD + part * half, head * HEAD + (part + 1) * half)
            cs[0, rows] = np.cos(ang).T
            cs[1, rows] = (np.sin(ang) if part else -np.sin(ang)).T
    ident = np.eye(P, dtype=f)
    blk = np.kron(np.eye(2), np.ones((HEAD, HEAD))).astype(f) / f(HEAD)
    hind = np.kron(np.eye(2), np.ones((HEAD, 1))).astype(f)
    masks = np.full((P, MASKS), -1e30, f)
    q = np.arange(P)[:, None]
    for r in range(RES):
        dist = RES * q + r + SPAN - np.arange(NEAR)[None, :]
        masks[:, r * NEAR:(r + 1) * NEAR][(dist >= 0) & (dist <= SPAN)] = 0
    dist = q + SPAN - np.arange(FAR)[None, :]
    masks[:, RES * NEAR:RES * NEAR + FAR][(dist >= 0) & (dist <= SPAN)] = 0
    masks[:, RES * NEAR + FAR:][(dist >= 0) & (dist % 4 == 0)] = 0

    arrays = {
        "in_xT": x[0].T.reshape(KT, P, S).transpose(1, 0, 2),
        "in_pT": p[:, 0].transpose(0, 2, 1).reshape(2, PK, P, S).transpose(2, 0, 1, 3),
        "in_vecs": vecs, "in_w": w_all, "in_cs": cs, "in_ident": ident, "in_blk": blk, "in_hind": hind,
        "in_masks": masks.astype(ml_dtypes.bfloat16),
    }
    arrays = {k: np.ascontiguousarray(v) for k, v in arrays.items()}
    nc = bacc.Bacc("TRN2", target_bir_lowering=False, num_devices=1)
    args = [nc.dram_tensor(k, v.shape, mybir.dt.from_np(v.dtype), kind="ExternalInput").ap()
            for k, v in arrays.items()]
    out = nc.dram_tensor("out_hT", (P, KT, S), F32, kind="ExternalOutput").ap()
    build(nc, *args, out)
    r = run_bass_kernel_spmd(nc, [arrays], core_ids=[0])
    hT = r.results[0]["out_hT"]
    return np.ascontiguousarray(hT.transpose(2, 1, 0).reshape(1, S, D))
```
